# Optimizing a Trainium2 kernel written in Bass

```python
import jax, jax.numpy as jnp
from jax import lax
import numpy as np
import math

D_MODEL = 1024
BATCH = 1
SEQ = 512
DEPTH = 1

GRID_W = 64
Q_BLOCK = 128
ROPE_THETA = 10000.0
EPS = 1e-6
H_A = 8
QK_NOPE = 64
QK_ROPE = 32
V_DIM_A = 64
Q_LORA = 256
KV_LORA = 128
H_B = 8
KV_B = 2
HD_B = 64
D_FF = 4 * D_MODEL
PLE_DIM = 256
IN_SPLITS = [Q_LORA, KV_LORA + QK_ROPE, H_B * HD_B, KV_B * HD_B, KV_B * HD_B, D_MODEL, D_MODEL]
D_IN = sum(IN_SPLITS)


def rmsnorm(x, g):
    xf = x.astype(jnp.float32)
    y = xf * lax.rsqrt(jnp.mean(xf * xf, axis=-1, keepdims=True) + EPS)
    return (y * g.astype(jnp.float32)).astype(x.dtype)

def rope_angles(pos, dim):
    inv = ROPE_THETA ** (-jnp.arange(0, dim, 2, dtype=jnp.float32) / dim)
    return pos.astype(jnp.float32)[:, None] * inv[None, :]

def apply_rope(x, ang):
    cos = jnp.cos(ang)[None, :, None, :].astype(x.dtype)
    sin = jnp.sin(ang)[None, :, None, :].astype(x.dtype)
    x1, x2 = jnp.split(x, 2, axis=-1)
    return jnp.concatenate([x1 * cos - x2 * sin, x1 * sin + x2 * cos], axis=-1)

def blocked_attention(q, k, v):
    B, S, Hk, G, dk = q.shape
    nb = S // Q_BLOCK
    qb = q.reshape(B, nb, Q_BLOCK, Hk, G, dk).transpose(1, 0, 2, 3, 4, 5)

    def one_block(qblk):
        s = jnp.einsum("bqhgd,bkhd->bhgqk", qblk, k).astype(jnp.float32)
        pr = jax.nn.softmax(s, axis=-1).astype(v.dtype)
        return jnp.einsum("bhgqk,bkhd->bqhgd", pr, v)

    o = lax.map(one_block, qb)
    return o.transpose(1, 0, 2, 3, 4, 5).reshape(B, S, Hk * G, v.shape[-1])

def first_inputs(seed: int = 0) -> dict:
    key = jax.random.key(seed)
    ks = jax.random.split(key, 24)
    f32 = jnp.float32

    def w(k, shape, fan_in):
        return jax.random.normal(k, shape, f32) * (fan_in ** -0.5)

    def gain(k, shape):
        return 1.0 + 0.05 * jax.random.normal(k, shape, f32)

    L = DEPTH
    return {
        "x": jax.random.normal(ks[0], (BATCH, SEQ, D_MODEL), f32),
        "p": jax.random.normal(ks[1], (DEPTH, BATCH, SEQ, PLE_DIM), f32),
        "g_mix": gain(ks[2], (L, D_MODEL)),
        "w_in": w(ks[3], (L, D_MODEL, D_IN), D_MODEL),
        "g_qa": gain(ks[4], (L, Q_LORA)),
        "w_qb": w(ks[5], (L, Q_LORA, H_A * (QK_NOPE + QK_ROPE)), Q_LORA),
        "g_kva": gain(ks[6], (L, KV_LORA)),
        "w_kvb": w(ks[7], (L, KV_LORA, H_A * (QK_NOPE + V_DIM_A)), KV_LORA),
        "g_qn": gain(ks[8], (L, HD_B)),
        "g_kn": gain(ks[9], (L, HD_B)),
        "w_oa": w(ks[10], (L, H_A * V_DIM_A, D_MODEL), H_A * V_DIM_A),
        "w_ob": w(ks[11], (L, H_B * HD_B, D_MODEL), H_B * HD_B),
        "w_o": w(ks[12], (L, D_MODEL, D_MODEL), D_MODEL),
        "g_mlp": gain(ks[13], (L, D_MODEL)),
        "w_up": w(ks[14], (L, D_MODEL, D_FF), D_MODEL),
        "w_down": w(ks[15], (L, D_FF, D_MODEL), D_FF),
        "g_ple": gain(ks[16], (L, D_MODEL)),
        "w_ple_gate": w(ks[17], (L, D_MODEL, D_MODEL), D_MODEL),
        "w_ple": w(ks[18], (L, PLE_DIM, D_MODEL), PLE_DIM),
        "g_final": gain(ks[19], (D_MODEL,)),
    }

def first_block(x, p, g_mix, w_in, g_qa, w_qb, g_kva, w_kvb, g_qn, g_kn, w_oa, w_ob, w_o,
              g_mlp, w_up, w_down, g_ple, w_ple_gate, w_ple, g_final):
    B, S, D = x.shape
    ROWS = S // GRID_W
    t = jnp.arange(S)
    row = jnp.broadcast_to(jnp.arange(ROWS)[:, None], (ROWS, GRID_W)).reshape(-1)
    col = jnp.broadcast_to(jnp.arange(GRID_W)[None, :], (ROWS, GRID_W)).reshape(-1)
    ang_1d = rope_angles(t, QK_ROPE)
    ang_row = rope_angles(row, HD_B // 2)
    ang_col = rope_angles(col, HD_B // 2)
    split_idx = list(np.cumsum(IN_SPLITS)[:-1])
    scale_a = (QK_NOPE + QK_ROPE) ** -0.5
    scale_b = HD_B ** -0.5

    for i in range(DEPTH):
        h = rmsnorm(x, g_mix[i])
        z = jnp.einsum("bsd,de->bse", h, w_in[i])
        q_lat, kv_lat, qb, kb, vb, gate_a, gate_b = jnp.split(z, split_idx, axis=-1)

        cq = rmsnorm(q_lat, g_qa[i])
        qa = jnp.einsum("bsr,re->bse", cq, w_qb[i]).reshape(B, S, H_A, QK_NOPE + QK_ROPE)
        qa_nope, qa_rope = jnp.split(qa, [QK_NOPE], axis=-1)
        qa_rope = apply_rope(qa_rope, ang_1d)
        c_kv, k_pe = jnp.split(kv_lat, [KV_LORA], axis=-1)
        c_kv = rmsnorm(c_kv, g_kva[i])
        k_pe = apply_rope(k_pe[:, :, None, :], ang_1d)
        kva = jnp.einsum("bsr,re->bse", c_kv, w_kvb[i]).reshape(B, S, H_A, QK_NOPE + V_DIM_A)
        ka_nope, va = jnp.split(kva, [QK_NOPE], axis=-1)
        qa_full = (jnp.concatenate([qa_nope, qa_rope], axis=-1) * scale_a)[:, :, :, None, :]
        ka_full = jnp.concatenate([ka_nope, jnp.broadcast_to(k_pe, (B, S, H_A, QK_ROPE))], axis=-1)
        oa = blocked_attention(qa_full, ka_full, va).reshape(B, S, H_A * V_DIM_A)
        ya = jnp.einsum("bse,ed->bsd", oa, w_oa[i])

        qb = rmsnorm(qb.reshape(B, S, H_B, HD_B), g_qn[i])
        kb = rmsnorm(kb.reshape(B, S, KV_B, HD_B), g_kn[i])
        vb = vb.reshape(B, S, KV_B, HD_B)
        qr, qc = jnp.split(qb, 2, axis=-1)
        qb = jnp.concatenate([apply_rope(qr, ang_row), apply_rope(qc, ang_col)], axis=-1)
        kr, kc = jnp.split(kb, 2, axis=-1)
        kb = jnp.concatenate([apply_rope(kr, ang_row), apply_rope(kc, ang_col)], axis=-1)
        qb = (qb * scale_b).reshape(B, S, KV_B, H_B // KV_B, HD_B)
        ob = blocked_attention(qb, kb, vb).reshape(B, S, H_B * HD_B)
        yb = jnp.einsum("bse,ed->bsd", ob, w_ob[i])

        merged = jax.nn.sigmoid(gate_a) * ya + jax.nn.sigmoid(gate_b) * yb
        x = x + jnp.einsum("bsd,de->bse", merged, w_o[i])

        h2 = rmsnorm(x, g_mlp[i])
        u = jax.nn.relu(jnp.einsum("bsd,df->bsf", h2, w_up[i]))
        x = x + jnp.einsum("bsf,fd->bsd", u * u, w_down[i])

        h3 = rmsnorm(x, g_ple[i])
        gate = jax.nn.sigmoid(jnp.einsum("bsd,de->bse", h3, w_ple_gate[i]))
        x = x + gate * jnp.einsum("bsk,kd->bsd", p[i], w_ple[i])

    return rmsnorm(x, g_final)


DEPTH_2 = 2

N_A_LAYERS = DEPTH_2 // 2
N_B_LAYERS = DEPTH_2 - N_A_LAYERS

GDN_HEADS = 8
GDN_DK = 128
GDN_DV = 128
GDN_QK_WIDTH = GDN_HEADS * GDN_DK
GDN_V_WIDTH = GDN_HEADS * GDN_DV
GDN_CONV = 4
GDN_CHUNK = 64
GDN_IN_WIDTH = 2 * GDN_QK_WIDTH + 2 * GDN_V_WIDTH + 2 * GDN_HEADS

FOX_HEADS = 16
FOX_HD = 64
FOX_WIDTH = FOX_HEADS * FOX_HD
FOX_QBLOCK = 128
KV_WIDTH = 2 * FOX_WIDTH + FOX_HEADS

D_FF_2 = int(math.ceil(8 * D_MODEL / 3 / 256) * 256)

RMS_EPS = 1e-6


def rms_norm(x, w):
    xf = x.astype(jnp.float32)
    y = xf * lax.rsqrt(jnp.mean(xf * xf, axis=-1, keepdims=True) + RMS_EPS)
    return (y * w.astype(jnp.float32)).astype(x.dtype)

def l2_normalize(x):
    xf = x.astype(jnp.float32)
    return xf * lax.rsqrt(jnp.sum(xf * xf, axis=-1, keepdims=True) + RMS_EPS)

def causal_depthwise_conv_silu(x, w):
    k_width = w.shape[0]
    y = lax.conv_general_dilated(
        x, w[:, None, :].astype(x.dtype), window_strides=(1,), padding=[(k_width - 1, 0)],
        dimension_numbers=("NWC", "WIO", "NWC"), feature_group_count=x.shape[-1])
    return jax.nn.silu(y)

def gated_delta_rule_chunked(q, k, v, g, beta):
    b_sz, t_len, n_h, d_k = q.shape
    d_v = v.shape[-1]
    c = GDN_CHUNK
    n_c = t_len // c

    def to_chunks(a):
        return a.reshape(b_sz, n_c, c, n_h, *a.shape[3:]).swapaxes(2, 3)

    qc, kc, vc, gc, bc = map(to_chunks, (q, k, v, g, beta))
    G = jnp.cumsum(gc, axis=-1)
    causal = jnp.tril(jnp.ones((c, c), dtype=bool))
    strict = jnp.tril(jnp.ones((c, c), dtype=bool), -1)
    diff = G[..., :, None] - G[..., None, :]
    decay_mat = jnp.where(causal, jnp.exp(jnp.where(causal, diff, 0.0)), 0.0)

    kk = jnp.einsum("bnhcd,bnhsd->bnhcs", kc, kc)
    a_strict = jnp.where(strict, bc[..., :, None] * kk * decay_mat, 0.0)
    rhs = jnp.concatenate([bc[..., None] * kc * jnp.exp(G)[..., None], bc[..., None] * vc], axis=-1)
    sol = lax.linalg.triangular_solve(a_strict, rhs, left_side=True, lower=True, unit_diagonal=True)
    w_c, u_c = sol[..., :d_k], sol[..., d_k:]

    a_qk = jnp.einsum("bnhcd,bnhsd->bnhcs", qc, kc) * decay_mat
    g_last = G[..., -1]
    q_dec = qc * jnp.exp(G)[..., None]
    k_dec = kc * jnp.exp(g_last[..., None] - G)[..., None]

    xs = tuple(jnp.moveaxis(a, 1, 0) for a in (q_dec, k_dec, u_c, w_c, a_qk, jnp.exp(g_last)))

    def step(state, inp):
        qg, kd, u_i, w_i, a_i, gl = inp
        v_new = u_i - jnp.einsum("bhcd,bhde->bhce", w_i, state)
        o = jnp.einsum("bhcd,bhde->bhce", qg, state) + jnp.einsum("bhcs,bhse->bhce", a_i, v_new)
        state = state * gl[..., None, None] + jnp.einsum("bhcd,bhce->bhde", kd, v_new)
        return state, o

    s0 = jnp.zeros((b_sz, n_h, d_k, d_v), jnp.float32)
    _, o = lax.scan(step, s0, xs)
    return o.transpose(1, 0, 3, 2, 4).reshape(b_sz, t_len, n_h, d_v)

def gated_deltanet_mixer(h, w_in, conv_w, a_log, dt_bias, out_norm, w_out):
    b_sz, t_len, _ = h.shape
    proj = h @ w_in
    o1 = 2 * GDN_QK_WIDTH + GDN_V_WIDTH
    o2 = o1 + GDN_V_WIDTH
    qkv = causal_depthwise_conv_silu(proj[..., :o1], conv_w)
    z = proj[..., o1:o2].reshape(b_sz, t_len, GDN_HEADS, GDN_DV)
    b_logit = proj[..., o2:o2 + GDN_HEADS]
    a_in = proj[..., o2 + GDN_HEADS:]
    q = qkv[..., :GDN_QK_WIDTH].reshape(b_sz, t_len, GDN_HEADS, GDN_DK)
    k = qkv[..., GDN_QK_WIDTH:2 * GDN_QK_WIDTH].reshape(b_sz, t_len, GDN_HEADS, GDN_DK)
    v = qkv[..., 2 * GDN_QK_WIDTH:].reshape(b_sz, t_len, GDN_HEADS, GDN_DV).astype(jnp.float32)
    q = l2_normalize(q) * (GDN_DK ** -0.5)
    k = l2_normalize(k)
    beta = jax.nn.sigmoid(b_logit.astype(jnp.float32))
    g = -jnp.exp(a_log.astype(jnp.float32)) * jax.nn.softplus(
        a_in.astype(jnp.float32) + dt_bias.astype(jnp.float32))
    o = gated_delta_rule_chunked(q, k, v, g, beta).astype(h.dtype)
    o = rms_norm(o, out_norm) * jax.nn.silu(z)
    return o.reshape(b_sz, t_len, GDN_V_WIDTH) @ w_out

def shared_kv(x, kv_norm, w_kv, b_forget):
    b_sz, t_len, _ = x.shape
    kvf = rms_norm(x, kv_norm) @ w_kv
    k = kvf[..., :FOX_WIDTH].reshape(b_sz, t_len, FOX_HEADS, FOX_HD).transpose(0, 2, 1, 3)
    v = kvf[..., FOX_WIDTH:2 * FOX_WIDTH].reshape(b_sz, t_len, FOX_HEADS, FOX_HD).transpose(0, 2, 1, 3)
    f_logit = (kvf[..., 2 * FOX_WIDTH:] + b_forget).astype(jnp.float32)
    log_f_cum = jnp.cumsum(jax.nn.log_sigmoid(f_logit), axis=1).transpose(0, 2, 1)
    return k, v, log_f_cum

def forgetting_attention_mixer(h, w_q, w_o, k, v, log_f_cum):
    b_sz, t_len, _ = h.shape
    q = (h @ w_q).reshape(b_sz, t_len, FOX_HEADS, FOX_HD).transpose(0, 2, 1, 3)
    scale = FOX_HD ** -0.5
    outs = []
    for blk in range(t_len // FOX_QBLOCK):
        s0 = blk * FOX_QBLOCK
        e = s0 + FOX_QBLOCK
        s = jnp.einsum("bhqd,bhkd->bhqk", q[:, :, s0:e], k[:, :, :e]).astype(jnp.float32) * scale
        s = s + log_f_cum[:, :, s0:e, None] - log_f_cum[:, :, None, :e]
        mask = (s0 + jnp.arange(FOX_QBLOCK))[:, None] >= jnp.arange(e)[None, :]
        p = jax.nn.softmax(jnp.where(mask, s, -jnp.inf), axis=-1)
        outs.append(jnp.einsum("bhqk,bhkd->bhqd", p.astype(v.dtype), v[:, :, :e]))
    o = jnp.concatenate(outs, axis=2)
    return o.transpose(0, 2, 1, 3).reshape(b_sz, t_len, FOX_WIDTH) @ w_o

def swiglu(h, w_in, w_out):
    gu = h @ w_in
    return (jax.nn.silu(gu[..., :D_FF_2]) * gu[..., D_FF_2:]) @ w_out

def second_inputs(seed: int = 0) -> dict:
    key = jax.random.key(seed)
    ks = jax.random.split(key, 20)
    f32 = jnp.float32

    def w(k, shape, fan_in):
        return jax.random.normal(k, shape, f32) * (fan_in ** -0.5)

    def gain(k, shape):
        return 1.0 + 0.1 * jax.random.normal(k, shape, f32)

    x = jax.random.normal(ks[0], (BATCH, SEQ, D_MODEL), f32)
    a_init = jax.random.uniform(ks[9], (N_A_LAYERS, GDN_HEADS), f32, 1.0, 16.0)
    dt = jnp.exp(jax.random.uniform(ks[10], (N_A_LAYERS, GDN_HEADS), f32, math.log(1e-3), math.log(0.1)))
    return {
        "x": x,
        "pre_mix_norm": gain(ks[1], (DEPTH_2, D_MODEL)),
        "post_mix_norm": gain(ks[2], (DEPTH_2, D_MODEL)),
        "pre_ffn_norm": gain(ks[3], (DEPTH_2, D_MODEL)),
        "post_ffn_norm": gain(ks[4], (DEPTH_2, D_MODEL)),
        "w_ffn_in": w(ks[5], (DEPTH_2, D_MODEL, 2 * D_FF_2), D_MODEL),
        "w_ffn_out": w(ks[6], (DEPTH_2, D_FF_2, D_MODEL), D_FF_2),
        "gdn_w_in": w(ks[7], (N_A_LAYERS, D_MODEL, GDN_IN_WIDTH), D_MODEL),
        "gdn_conv": w(ks[8], (N_A_LAYERS, GDN_CONV, 2 * GDN_QK_WIDTH + GDN_V_WIDTH), GDN_CONV),
        "gdn_a_log": jnp.log(a_init),
        "gdn_dt_bias": dt + jnp.log(-jnp.expm1(-dt)),
        "gdn_out_norm": gain(ks[11], (N_A_LAYERS, GDN_DV)),
        "gdn_w_out": w(ks[12], (N_A_LAYERS, GDN_V_WIDTH, D_MODEL), GDN_V_WIDTH),
        "kv_norm": gain(ks[13], (D_MODEL,)),
        "w_kv": w(ks[14], (D_MODEL, KV_WIDTH), D_MODEL),
        "b_forget": 2.0 + 0.5 * jax.random.normal(ks[15], (FOX_HEADS,), f32),
        "fox_w_q": w(ks[16], (N_B_LAYERS, D_MODEL, FOX_WIDTH), D_MODEL),
        "fox_w_o": w(ks[17], (N_B_LAYERS, FOX_WIDTH, D_MODEL), FOX_WIDTH),
    }

def second_block(x, pre_mix_norm, post_mix_norm, pre_ffn_norm, post_ffn_norm, w_ffn_in, w_ffn_out,
              gdn_w_in, gdn_conv, gdn_a_log, gdn_dt_bias, gdn_out_norm, gdn_w_out,
              kv_norm, w_kv, b_forget, fox_w_q, fox_w_o):
    k_sh = v_sh = c_sh = None
    for layer in range(DEPTH_2):
        h = rms_norm(x, pre_mix_norm[layer])
        if layer < N_A_LAYERS:
            i = layer
            mix = gated_deltanet_mixer(h, gdn_w_in[i], gdn_conv[i], gdn_a_log[i], gdn_dt_bias[i],
                                       gdn_out_norm[i], gdn_w_out[i])
        else:
            i = layer - N_A_LAYERS
            if i == 0:
                k_sh, v_sh, c_sh = shared_kv(x, kv_norm, w_kv, b_forget)
            mix = forgetting_attention_mixer(h, fox_w_q[i], fox_w_o[i], k_sh, v_sh, c_sh)
        x = x + rms_norm(mix, post_mix_norm[layer])
        f = swiglu(rms_norm(x, pre_ffn_norm[layer]), w_ffn_in[layer], w_ffn_out[layer])
        x = x + rms_norm(f, post_ffn_norm[layer])
    return x


def setup_inputs(seed=0):
    out = dict(first_inputs(seed))
    for name, value in second_inputs(seed + 1).items():
        if name != "x":
            out[name + "_2"] = value
    return out


def reference(
    x, p, g_mix, w_in, g_qa, w_qb, g_kva, w_kvb, g_qn, g_kn, w_oa, w_ob, w_o, g_mlp, w_up,
    w_down, g_ple, w_ple_gate, w_ple, g_final, pre_mix_norm_2, post_mix_norm_2, pre_ffn_norm_2,
    post_ffn_norm_2, w_ffn_in_2, w_ffn_out_2, gdn_w_in_2, gdn_conv_2, gdn_a_log_2,
    gdn_dt_bias_2, gdn_out_norm_2, gdn_w_out_2, kv_norm_2, w_kv_2, b_forget_2, fox_w_q_2,
    fox_w_o_2,
):
    x = first_block(
        x, p, g_mix, w_in, g_qa, w_qb, g_kva, w_kvb, g_qn, g_kn, w_oa, w_ob, w_o, g_mlp, w_up,
        w_down, g_ple, w_ple_gate, w_ple, g_final,
    )
    return second_block(
        x, pre_mix_norm_2, post_mix_norm_2, pre_ffn_norm_2, post_ffn_norm_2, w_ffn_in_2,
        w_ffn_out_2, gdn_w_in_2, gdn_conv_2, gdn_a_log_2, gdn_dt_bias_2, gdn_out_norm_2,
        gdn_w_out_2, kv_norm_2, w_kv_2, b_forget_2, fox_w_q_2, fox_w_o_2,
    )


_drawn_inputs = setup_inputs


def setup_inputs(seed=0):
    import zlib

    import numpy as np

    out = dict(_drawn_inputs(seed))
    spreads = {}
    factors = {'g_mix': 4.895, 'g_qa': 8.0, 'g_kva': 5.612, 'g_qn': 8.0, 'g_kn': 8.0, 'g_ple': 25.83}
    for name, (base, spread) in spreads.items():
        noise = np.random.default_rng([zlib.crc32(name.encode()), seed]).standard_normal(out[name].shape)
        drawn = base * np.exp(spread * noise) if base else spread * noise
        out[name] = __import__('jax').numpy.asarray(drawn.astype(out[name].dtype))
    for name, factor in factors.items():
        out[name] = (out[name] * factor).astype(out[name].dtype)
    return out
```

```python
import numpy as np

P = 128
T = 512
TT = T // P
D = 1024
DT = D // P
EPS = 1e-6
GRID_W = 64
ROPE_THETA = 10000.0

HEADS = 8
NOPE, ROPE, DV_A = 64, 32, 64
DQ_A = NOPE + ROPE
Q_LORA, KV_LORA = 256, 128
HD_B, KV_B = 64, 2
D_FF = 4 * D
COL_QLAT, COL_KV = 0, Q_LORA
COL_QB = COL_KV + KV_LORA + ROPE
COL_KB = COL_QB + HEADS * HD_B
COL_VB = COL_KB + KV_B * HD_B
COL_GATES = COL_VB + KV_B * HD_B

GH = 8
GDN_QKV = 3 * GH * P
FOX_HEADS, FOX_HD = 16, 64
D_FF2 = 2816
CHUNK = 2048
NEG = -1.0e30

GAIN_ROWS = [("g_mix", 8), ("g_qa", 2), ("g_kva", 1), ("g_mlp", 8), ("g_ple", 8), ("g_final", 8),
             ("pre_mix_norm_2", 16), ("post_mix_norm_2", 16), ("pre_ffn_norm_2", 16),
             ("post_ffn_norm_2", 16), ("kv_norm_2", 8), ("gdn_out_norm_2", 1)]
GAIN_AT = {}
_row = 0
for _name, _tiles in GAIN_ROWS:
    GAIN_AT[_name] = _row
    _row += _tiles
GAIN_AT["g_qn"] = _row
GAIN_AT["g_kn"] = _row + 1
N_GAINS = _row + 2
CONV_TAPS = 4
N_CONV = CONV_TAPS * 3 * GH

CONST_AT = {}
_col = 0
for _name, _n in [("identity", P), ("rotate", P), ("heads_of_pair", 2), ("ones", 1), ("causal_bias", P),
                  ("head_select", GH * GH), ("earlier", P), ("level", 7 * P)]:
    CONST_AT[_name] = (_col, _n)
    _col += _n
N_CONST = _col
N_SMALL_CONST = CONST_AT["earlier"][0]


def shape_constants():
    c = np.zeros((P, N_CONST), np.float32)

    def put(name, value):
        at, n = CONST_AT[name]
        c[:, at:at + n] = value

    row, col = np.arange(P)[:, None], np.arange(P)[None, :]
    put("identity", row == col)
    half = ROPE // 2
    first = (col % ROPE) < half
    put("rotate", np.where(first & (row == col + half), -1.0, 0.0) + np.where(~first & (row == col - half), 1.0, 0.0))
    put("heads_of_pair", (row // HD_B) == np.arange(2)[None, :])
    put("ones", 1.0)
    put("head_select", np.eye(GH).reshape(1, GH * GH))
    put("causal_bias", np.where(col > row, NEG, 0.0))
    put("earlier", row <= col)
    levels = [((row // (2 * b)) == (col // (2 * b))) & ((row // b) % 2 == 0) & ((col // b) % 2 == 1)
              for b in (1, 2, 4, 8, 16, 32, 64)]
    put("level", np.concatenate(levels, axis=1))
    return c


def rope_tables():
    t = np.arange(T)
    out = np.zeros((4, P, T), np.float32)
    inv = (ROPE_THETA ** (-np.arange(0, ROPE, 2, dtype=np.float32) / np.float32(ROPE))).astype(np.float32)
    ang = (t.astype(np.float32)[None, :] * inv[:, None]).astype(np.float32)
    out[0, :, :] = 1.0
    for half in range(2):
        at = NOPE + half * (ROPE // 2)
        out[0, at:at + ROPE // 2] = np.cos(ang)
        out[1, at:at + ROPE // 2] = np.sin(ang)
    row_ang = ((t // GRID_W).astype(np.float32)[None, :] * inv[:, None]).astype(np.float32)
    col_ang = ((t % GRID_W).astype(np.float32)[None, :] * inv[:, None]).astype(np.float32)
    for group in range(P // 16):
        a = row_ang if (group // 2) % 2 == 0 else col_ang
        out[2, group * 16:(group + 1) * 16] = np.cos(a)
        out[3, group * 16:(group + 1) * 16] = np.sin(a)
    return out


class Chunk:

    def __init__(self, first, i=0, per_turn=0):
        assert per_turn % 2 == 0
        self.slot = first % 2
        self.number = first + i * per_turn if per_turn else first
        self.uses = first // 2 + 1 + i * (per_turn // 2) if per_turn else first // 2 + 1
        self.first, self.i, self.per_turn = first, i, per_turn


class Stage:

    def __init__(self, nc, label):
        from contextlib import ExitStack
        self.nc, self.label, self.stack, self.sems = nc, label, ExitStack(), []

    def sem(self, name):
        s = self.stack.enter_context(self.nc.semaphore(f"{self.label}_{name}"))
        self.sems.append(s)
        return s

    def sbuf(self, name, shape, dtype):
        return self.stack.enter_context(self.nc.sbuf_tensor(f"{self.label}_{name}", shape, dtype))

    def __enter__(self):
        self.stack.__enter__()
        return self

    def __exit__(self, *exc):
        if exc[0] is None:
            numbers = sorted(s.num for s in self.sems)
            at = 0
            while at < len(numbers):
                end = at
                while end + 1 < len(numbers) and numbers[end + 1] == numbers[end] + 1:
                    end += 1
                self.nc.all_engine_barrier(sems_to_clear=range(numbers[at], numbers[end] + 1))
                at = end + 1
        return self.stack.__exit__(*exc)


class Weights:

    def __init__(self, nc, enter, plan):
        from concourse import mybir
        self.nc, self.plan = nc, plan
        f32, f32r = mybir.dt.float32, mybir.dt.float32r
        self.f32, self.sub = f32, mybir.AluOpType.subtract
        self.raw = enter(nc.sbuf_tensor("weights_raw", [P, 2, CHUNK], f32))
        self.high = enter(nc.sbuf_tensor("weights_high", [P, 2, CHUNK], f32r))
        self.low = enter(nc.sbuf_tensor("weights_low", [P, 2, CHUNK], f32r))
        self.loaded = [enter(nc.semaphore(f"weights_loaded_{s}")) for s in range(2)]
        self.high_ready = enter(nc.semaphore("weights_high_ready"))
        self.low_ready = enter(nc.semaphore("weights_low_ready"))
        self.products = enter(nc.semaphore("products_done"))
        self.start = {}
        n = 0
        for name, segments in plan:
            self.start[name] = n
            n += sum(turns * len(items) for turns, items in segments)
        self.total = n
        self.width, self.tiles_before, tiles, self.turn = [], [0], 0, []
        for _, segments in plan:
            for turns, items in segments:
                for i in range(turns):
                    for kt, cols, _, count in items:
                        self.width.append(kt * cols)
                        tiles += count
                        self.tiles_before.append(tiles)

    def load(self, sp, chunk, item, i):
        kt, cols, source, _ = item
        if chunk.first >= 2:
            sp.wait_ge(self.low_ready, chunk.number - 1)
        sp.dma_start(self.raw[:, chunk.slot, 0:kt * cols].rearrange("p (k c) -> p k c", k=kt),
                     source(i)).then_inc(self.loaded[chunk.slot], 16)

    def load_segments(self, sp, first, segments):
        for turns, items in segments:
            if turns == 1:
                for item in items:
                    self.load(sp, Chunk(first), item, 0)
                    first += 1
            else:
                with sp.Fori(0, turns) as i:
                    for pos, item in enumerate(items):
                        self.load(sp, Chunk(first + pos, i, len(items)), item, i)
                first += turns * len(items)

    @staticmethod
    def shifted(items, by):
        def later(source):
            return lambda i: source(i + by)
        return [(kt, cols, later(source), count) for kt, cols, source, count in items]

    def after_two(self, segments):
        rest, head, need = [], [], 2
        for turns, items in segments:
            if need == 0:
                rest.append((turns, items))
                continue
            skipped = 0
            while need and skipped < turns:
                turn = self.shifted(items, skipped)
                take = min(need, len(items))
                head += turn[:take]
                need -= take
                skipped += 1
                if take < len(items):
                    rest.append((1, turn[take:]))
            if skipped < turns:
                rest.append((turns - skipped, self.shifted(items, skipped)))
        return head, rest

    def load_for(self, sp, name):
        names = [n for n, _ in self.plan]
        at = names.index(name)
        _, rest = self.after_two(self.plan[at][1])
        self.load_segments(sp, self.start[name] + 2, rest)
        if at + 1 < len(names):
            head, _ = self.after_two(self.plan[at + 1][1])
            self.load_segments(sp, self.start[names[at + 1]], [(1, head)])

    def plan_item(self, name, n):
        for turns, items in dict(self.plan)[name]:
            if n < turns * len(items):
                return self.shifted(items, n // len(items))[n % len(items)]
            n -= turns * len(items)

    def split_high(self, act, chunk):
        if chunk.first >= self.total:
            return
        width = self.width[chunk.first]
        act.wait_ge(self.loaded[chunk.slot], 16 * chunk.uses)
        if chunk.first >= 2:
            act.wait_ge(self.products, self.tiles_at(chunk, -1))
        self.nc.scalar.copy(self.high[:, chunk.slot, 0:width],
                            self.raw[:, chunk.slot, 0:width]).then_inc(self.high_ready, 1)

    def tiles_at(self, chunk, by=0):
        at = self.tiles_before[chunk.first + by]
        if chunk.per_turn:
            step = chunk.per_turn
            slope = self.tiles_before[chunk.first + by + step] - at
            return chunk.i * slope + at
        return at

    def split_low(self, pool, chunk):
        if chunk.first >= self.total:
            return
        width = self.width[chunk.first]
        pool.wait_ge(self.high_ready, chunk.number + 1)
        self.nc.gpsimd.tensor_tensor(out=self.low[:, chunk.slot, 0:width],
                                     in0=self.raw[:, chunk.slot, 0:width],
                                     in1=self.high[:, chunk.slot, 0:width].bitcast(self.f32),
                                     op=self.sub).then_inc(self.low_ready, 1)

    def split_low_all(self, pool, name):
        first = self.start[name] + 1
        for turns, items in dict(self.plan)[name]:
            if turns == 1:
                for pos in range(len(items)):
                    self.split_low(pool, Chunk(first + pos))
            else:
                with pool.Fori(0, turns) as i:
                    for pos in range(len(items)):
                        self.split_low(pool, Chunk(first + pos, i, len(items)))
            first += turns * len(items)

    def parts(self, chunk, kt):
        width = self.width[chunk.first]
        return [x[:, chunk.slot, 0:width].rearrange("p (k c) -> p k c", k=kt) for x in (self.high, self.low)]


def weight_plan(w):
    import concourse.bass as bass

    def cols(matrix, kt, n, at, tiles=2):
        view = matrix.rearrange("(k p) c -> p k c", p=P)
        return (kt, n, lambda i: view[:, :, bass.ds(at(i), n)], tiles)

    def rows(matrix, at):
        view = matrix.rearrange("(k p) c -> p k c", p=P)
        return (2, D, lambda i: view[:, bass.ds(at(i), 2), :], DT)

    def halves(matrix, n, at, half):
        view = matrix.rearrange("(k p) c -> p k c", p=P)
        return (4, n, lambda i: view[:, 4 * half:4 * half + 4, bass.ds(at(i), n)], TT)

    def pairs(matrix, turns, start=0):
        return (turns, [cols(matrix, DT, 256, lambda i: i * 512 + start),
                        cols(matrix, DT, 256, lambda i: i * 512 + (start + 256))])

    def once(*items):
        return (1, list(items))

    w_in, qb, kvb = w["w_in"][0], w["w_qb"][0], w["w_kvb"][0]
    up, down = w["w_up"][0], w["w_down"][0]

    def u1(t0, step):
        return cols(up, DT, 256, lambda i: i * (256 * step) + 256 * t0)

    def d1(t0, step):
        return rows(down, lambda i: i * (2 * step) + 2 * t0)

    def swiglu(layer):
        inner, outer = w["w_ffn_in_2"][layer], w["w_ffn_out_2"][layer]

        def g(t0, step):
            return cols(inner, DT, 256, lambda i: i * (256 * step) + 256 * t0)

        def u(t0, step):
            return cols(inner, DT, 256, lambda i: i * (256 * step) + (256 * t0 + D_FF2))

        def d(t0, step):
            return rows(outer, lambda i: i * (2 * step) + 2 * t0)

        return [once(g(0, 0), u(0, 0)), (5, [g(1, 2), u(1, 2), d(0, 2), g(2, 2), u(2, 2), d(1, 2)]), once(d(10, 0))]

    gdn, kv = w["gdn_w_in_2"][0], w["w_kv_2"]
    return [
        ("mixer_in", [pairs(w_in, 4, COL_GATES),
                      once(cols(w_in, DT, 256, lambda i: COL_QLAT),
                           cols(w_in, DT, 256, lambda i: COL_QB), cols(w_in, DT, 256, lambda i: COL_QB + 256),
                           cols(w_in, DT, 256, lambda i: COL_KB),
                           cols(w_in, DT, 256, lambda i: COL_KV))]),
        ("latent_up", [once(cols(qb, 2, HEADS * DQ_A, lambda i: 0, HEADS), cols(kvb, 1, D, lambda i: 0, HEADS + TT))]),
        ("merge", [(2, [cols(w["w_oa"][0], 4, 512, lambda i: i * 512, 4),
                        cols(w["w_ob"][0], 4, 512, lambda i: i * 512, 4)])]),
        ("mixer_out", [pairs(w["w_o"][0], 2)]),
        ("mlp", [once(u1(0, 0), u1(1, 0), d1(0, 0)), (7, [u1(2, 2), d1(1, 2), u1(3, 2), d1(2, 2)]), once(d1(15, 0))]),
        ("ple", [once(cols(w["w_ple"][0], 2, D, lambda i: 0, DT)), pairs(w["w_ple_gate"][0], 2)]),
        ("gdn_in", [pairs(gdn, 6), pairs(gdn, 2, GDN_QKV), once(cols(gdn, DT, 256, lambda i: GDN_QKV + D + 2 * GH - 256))]),
        ("gdn_out", [pairs(w["gdn_w_out_2"][0], 2)]),
        ("ffn0", swiglu(0)),
        ("fox_kv", [pairs(kv, 2),
                    (2, [halves(kv, 512, lambda i: i * 512 + D, 0), halves(kv, 512, lambda i: i * 512 + D, 1)]),
                    once(cols(kv, DT, 256, lambda i: 2 * D + FOX_HEADS - 256, 1))]),
        ("fox_q", [pairs(w["fox_w_q_2"][0], 2)]),
        ("fox_out", [pairs(w["fox_w_o_2"][0], 2)]),
        ("ffn1", swiglu(1)),
    ]


def build_program(nc, w, constants, tables, out):
    import concourse.bass as bass
    from concourse import mybir
    from contextlib import ExitStack

    f32, f32r = mybir.dt.float32, mybir.dt.float32r
    ALU, ACT, AX = mybir.AluOpType, mybir.ActivationFunctionType, mybir.AxisListType
    ds = bass.ds
    ctx = ExitStack()
    enter = ctx.enter_context


    def stage(label):
        return Stage(nc, label)


    with ctx:
        weights = Weights(nc, enter, weight_plan(w))
        const = enter(nc.sbuf_tensor("const", [P, N_SMALL_CONST], f32))
        gains = enter(nc.sbuf_tensor("gains", [P, N_GAINS], f32))
        x = enter(nc.sbuf_tensor("x_stream", [P, DT, T], f32))
        psum = enter(nc.psum_tensor("psum", [P, 8, T], f32))

        def constant(name):
            at, n = CONST_AT[name]
            return const[:, at:at + n]

        identity, rotate, ones = constant("identity"), constant("rotate"), constant("ones")

        def gain(name, tile=0):
            at = GAIN_AT[name] + tile
            return gains[:, at:at + 1]

        def product(bank, w_parts, a_parts, first, last):
            (wh, wl), (ah, al) = w_parts, a_parts
            nc.tensor.matmul(bank, wh, ah, start=first, stop=False)
            nc.tensor.matmul(bank, wh, al, start=False, stop=False)
            return nc.tensor.matmul(bank, wl, ah, start=False, stop=last)

        with stage("init") as s:
            rows_in = s.sbuf("gain_rows", [P, P], f32)
            x_rows = s.sbuf("x_rows", [P, TT, D], f32)
            loaded, gains_in, x_in = s.sem("const_loaded"), s.sem("gains_loaded"), s.sem("x_loaded")
            zeroed, turned, copied = s.sem("gain_rows_zeroed"), s.sem("turned"), s.sem("copied")
            with nc.Block() as block:
                @block.sync
                def _(sp):
                    sp.dma_start(const[:], constants[:, 0:N_SMALL_CONST]).then_inc(loaded, 16)
                    for j in range(TT):
                        sp.dma_start(x_rows[:, j, :], w["x"][0, j * P:(j + 1) * P, :]).then_inc(x_in, 16)
                    head, _ = weights.after_two(weights.plan[0][1])
                    weights.load_segments(sp, 0, [(1, head)])

                @block.scalar
                def _(act):
                    act.wait_ge(zeroed, 1)
                    for name, tiles in GAIN_ROWS:
                        at = GAIN_AT[name]
                        g = w[name]
                        if len(g.shape) == 2:
                            g = g.rearrange("l (t p) -> (l t) p", p=P)
                        else:
                            g = g.rearrange("(t p) -> t p", p=P)
                        act.dma_start(rows_in[at:at + tiles, :], g).then_inc(gains_in, 16)
                    for name in ("g_qn", "g_kn"):
                        at = GAIN_AT[name]
                        for half in range(2):
                            act.dma_start(rows_in[at:at + 1, half * HD_B:(half + 1) * HD_B],
                                          w[name]).then_inc(gains_in, 16)
                    weights.split_high(act, Chunk(0))

                @block.gpsimd
                def _(pool):
                    nc.gpsimd.memset(rows_in[:], 0.0).then_inc(zeroed, 1)
                    weights.split_low(pool, Chunk(0))

                @block.tensor
                def _(pe):
                    pe.wait_ge(loaded, 16)
                    pe.wait_ge(x_in, 16 * TT)
                    for t in range(DT):
                        if t >= 4:
                            pe.wait_ge(copied, t - 3)
                        for j in range(TT):
                            last = nc.tensor.transpose(psum[:, t % 4, j * P:(j + 1) * P],
                                                       x_rows[:, j, t * P:(t + 1) * P], identity)
                        last.then_inc(turned, 1)
                    pe.wait_ge(gains_in, 16 * (len(GAIN_ROWS) + 4))
                    nc.tensor.transpose(psum[:, 4, 0:P], rows_in[:], identity).then_inc(turned, 1)

                @block.vector
                def _(dve):
                    for t in range(DT):
                        dve.wait_ge(turned, t + 1)
                        nc.vector.tensor_copy(x[:, t, :], psum[:, t % 4, :]).then_inc(copied, 1)
                    dve.wait_ge(turned, DT + 1)
                    nc.vector.tensor_copy(gains[:], psum[:, 4, 0:N_GAINS])

        def rms_normalize(label, source, tiles, gain_at, split=None, plain=None, add_to=None):
            with stage(label) as s:
                work = s.sbuf("work", [P, tiles, T], f32)
                stat = s.sbuf("stat", [P, 3, TT], f32)
                squared, summed, mean, root = s.sem("squared"), s.sem("summed"), s.sem("mean"), s.sem("root")
                rstd, spread, scaled, high_done = s.sem("rstd"), s.sem("spread"), s.sem("scaled"), s.sem("high_done")
                with nc.Block() as block:
                    @block.scalar
                    def _(act):
                        for t in range(tiles):
                            nc.scalar.activation(work[:, t, :], source[:, t, :], ACT.Square).then_inc(squared, 1)
                        act.wait_ge(mean, 1)
                        nc.scalar.activation(stat[:, 1, :], stat[:, 0, :], ACT.Sqrt).then_inc(root, 1)
                        if split is not None:
                            for t in range(tiles):
                                act.wait_ge(scaled, t + 1)
                                nc.scalar.copy(split[:, 0, t, :], work[:, t, :]).then_inc(high_done, 1)

                    @block.tensor
                    def _(pe):
                        for j in range(TT):
                            for t in range(tiles):
                                if j == 0:
                                    pe.wait_ge(squared, t + 1)
                                last = nc.tensor.matmul(psum[:, 0, j:j + 1], work[:, t, j * P:(j + 1) * P], ones,
                                                        start=(t == 0), stop=(t == tiles - 1))
                        last.then_inc(summed, 1)
                        pe.wait_ge(rstd, 1)
                        for j in range(TT):
                            last = nc.tensor.matmul(psum[:, 1, j * P:(j + 1) * P],
                                                    stat[:, 2, j:j + 1].broadcast_to([P, P]), identity,
                                                    start=True, stop=True)
                        last.then_inc(spread, 1)

                    @block.vector
                    def _(dve):
                        dve.wait_ge(summed, 1)
                        nc.vector.tensor_scalar(stat[:, 0, :], psum[:, 0, 0:TT], 1.0 / (tiles * P), EPS,
                                                ALU.mult, ALU.add).then_inc(mean, 1)
                        dve.wait_ge(root, 1)
                        nc.vector.reciprocal(stat[:, 2, :], stat[:, 1, :]).then_inc(rstd, 1)
                        dve.wait_ge(spread, 1)
                        for t in range(tiles):
                            target = plain[:, t, :] if plain is not None else work[:, t, :]
                            nc.vector.scalar_tensor_tensor(out=target, in0=source[:, t, :], scalar=gain_at(t),
                                                           in1=psum[:, 1, :], op0=ALU.mult,
                                                           op1=ALU.mult).then_inc(scaled, 1)
                            if add_to is not None and t >= 1:
                                dve.wait_ge(scaled, t)
                                nc.vector.tensor_tensor(out=add_to[:, t - 1, :], in0=add_to[:, t - 1, :],
                                                        in1=work[:, t - 1, :], op=ALU.add)
                        if add_to is not None:
                            dve.wait_ge(scaled, tiles)
                            nc.vector.tensor_tensor(out=add_to[:, tiles - 1, :], in0=add_to[:, tiles - 1, :],
                                                    in1=work[:, tiles - 1, :], op=ALU.add)

                    if split is not None:
                        @block.gpsimd
                        def _(pool):
                            for t in range(tiles):
                                pool.wait_ge(high_done, t + 1)
                                nc.gpsimd.tensor_tensor(out=split[:, 1, t, :], in0=work[:, t, :],
                                                        in1=split[:, 0, t, :].bitcast(f32), op=ALU.subtract)

        def linear(label, turns, act_in, finish_scalar=None, finish_vector=None):
            start = weights.start[label]
            tiles0 = weights.tiles_before[start]
            with stage(label) as s:
                scalar_done, bank_free = s.sem("scalar_done"), s.sem("bank_free")
                both = finish_scalar is not None and finish_vector is not None
                handed = s.sbuf("handed", [P, 2, T], f32) if both else None
                with nc.Block() as block:
                    @block.sync
                    def _(sp):
                        weights.load_for(sp, label)

                    @block.gpsimd
                    def _(pool):
                        weights.split_low_all(pool, label)

                    @block.tensor
                    def _(pe):
                        with pe.Fori(0, turns) as i:
                            for c in range(2):
                                chunk = Chunk(start + c, i, 2)
                                pe.wait_ge(weights.low_ready, chunk.number + 1)
                                high, low = weights.parts(chunk, DT)
                                for j in (2 * c, 2 * c + 1):
                                    pe.wait_ge(bank_free, i * 4 + (j + 1))
                                    sl = slice((j % 2) * P, (j % 2 + 1) * P)
                                    for k in range(DT):
                                        last = product(psum[:, j, :], (high[:, k, sl], low[:, k, sl]),
                                                       (act_in[:, 0, k, :], act_in[:, 1, k, :]), k == 0, k == DT - 1)
                                    last.then_inc(weights.products, 1)

                    @block.scalar
                    def _(act):
                        with act.Fori(0, turns) as i:
                            for c in range(2):
                                weights.split_high(act, Chunk(start + c + 1, i, 2))
                                for j in (2 * c, 2 * c + 1) if finish_scalar else ():
                                    act.wait_ge(weights.products, i * 4 + (tiles0 + j + 1))
                                    if both:
                                        act.wait_ge(bank_free, i * 4 + (j + 3))
                                        finish_scalar(j, handed[:, j % 2, :], i * 4 + j).then_inc(scalar_done, 1)
                                    else:
                                        finish_scalar(j, None, i * 4 + j).then_inc(bank_free, 1)

                    @block.vector
                    def _(dve):
                        dve.sem_inc(bank_free, 4)
                        if finish_vector is not None:
                            with dve.Fori(0, turns) as i:
                                for j in range(4):
                                    if both:
                                        dve.wait_ge(scalar_done, i * 4 + (j + 1))
                                    else:
                                        dve.wait_ge(weights.products, i * 4 + (tiles0 + j + 1))
                                    finish_vector(j, handed[:, j % 2, :] if both else None,
                                                  i * 4 + j).then_inc(bank_free, 1)

        def block_one():
            gates = ctx1.enter_context(nc.sbuf_tensor("gates", [P, 2 * DT, T], f32))
            split = ctx1.enter_context(nc.sbuf_tensor("block1_split", [P, 2, DT, T], f32r))
            rms_normalize("norm_mix", x, DT, lambda t: gain("g_mix", t), split=split)
            attn = ExitStack()
            with attn:
                def keep(name, shape, dtype=f32):
                    return attn.enter_context(nc.sbuf_tensor(name, shape, dtype))

                q_a = keep("q_a", [P, HEADS, T])
                k_a = keep("k_a", [P, HEADS, T])
                v_a = keep("v_a", [P, TT, HEADS * DV_A])
                qk_b = keep("qk_b", [P, 6, T])
                v_b = keep("v_b", [P, TT, KV_B * HD_B])
                k_pe = keep("k_pe", [P, T])

                with ExitStack() as latents:
                    q_lat = latents.enter_context(nc.sbuf_tensor("q_lat", [P, 2, T], f32))
                    kv_lat = latents.enter_context(nc.sbuf_tensor("kv_lat", [P, 1, T], f32))
                    mixer_in(split, gates, q_lat, kv_lat, qk_b, v_b, k_pe)
                    q_split, kv_split = split[:, :, 0:2, :], split[:, :, 2:3, :]
                    rms_normalize("norm_qa", q_lat, 2, lambda t: gain("g_qa", t), split=q_split)
                    rms_normalize("norm_kva", kv_lat, 1, lambda t: gain("g_kva"), split=kv_split)
                    latent_up(q_split, kv_split, q_a, k_a, v_a)
                rope_and_norms(q_a, k_a, k_pe, qk_b)
                attention("attn_a", HEADS // 2, split, 0, q_a, k_a, v_a, DQ_A, DV_A, "latent")
                attention("attn_b", HEADS // 2, split, HEADS // 2, qk_b, qk_b, v_b, HD_B, HD_B, "grouped")
            with nc.sbuf_tensor("merged", [P, 2, DT, T], f32r) as merged:
                merge(split, gates, merged)

                def add_to_x(bank, _, tile):
                    return nc.vector.tensor_tensor(out=x[:, ds(tile, 1), :], in0=psum[:, bank:bank + 1, :],
                                                   in1=x[:, ds(tile, 1), :], op=ALU.add)

                linear("mixer_out", 2, merged, finish_vector=add_to_x)
            rms_normalize("norm_mlp", x, DT, lambda t: gain("g_mlp", t), split=split)
            mlp(split)
            rms_normalize("norm_ple", x, DT, lambda t: gain("g_ple", t), split=split)
            ple(split, gates)
            rms_normalize("norm_final", x, DT, lambda t: gain("g_final", t), plain=x)

        def mixer_in(split, gates, q_lat, kv_lat, qk_b, v_b, k_pe):
            start = weights.start["mixer_in"]
            last_gate = 2 * DT
            with stage("mixer_in") as s:
                gate_bank_free, bank_free = s.sem("gate_bank_free"), s.sem("bank_free")
                lower, upper = slice(0, HD_B), slice(HD_B, P)
                whole = slice(0, P)
                targets = [[(q_lat[:, n, :], whole)] for n in range(2)] + [[(qk_b[:, n, :], whole)] for n in range(4)]
                targets += [[(qk_b[half, 4 + g, :], (lower, upper)[g]) for g in range(KV_B) for half in (lower, upper)],
                            [(v_b[:], whole)], [(kv_lat[:, 0, :], whole)], [(k_pe[:], whole)]]
                with nc.Block() as block:
                    @block.sync
                    def _(sp):
                        weights.load_for(sp, "mixer_in")

                    @block.gpsimd
                    def _(pool):
                        weights.split_low_all(pool, "mixer_in")

                    @block.tensor
                    def _(pe):
                        with pe.Fori(0, 4) as i:
                            for c in range(2):
                                chunk = Chunk(start + c, i, 2)
                                pe.wait_ge(weights.low_ready, chunk.number + 1)
                                high, low = weights.parts(chunk, DT)
                                for j in (2 * c, 2 * c + 1):
                                    pe.wait_ge(gate_bank_free, i * 4 + (j + 1))
                                    sl = slice((j % 2) * P, (j % 2 + 1) * P)
                                    for k in range(DT):
                                        last = product(psum[:, j, :], (high[:, k, sl], low[:, k, sl]),
                                                       (split[:, 0, k, :], split[:, 1, k, :]), k == 0, k == DT - 1)
                                    last.then_inc(weights.products, 1)
                        tile = 0

                        def feature_tile(parts, stationary):
                            nonlocal tile
                            if tile >= 4:
                                pe.wait_ge(bank_free, tile - 3)
                            for k in range(DT):
                                last = product(psum[:, 4 + tile % 4, :], [stationary(x, k) for x in parts],
                                               (split[:, 0, k, :], split[:, 1, k, :]), k == 0, k == DT - 1)
                            last.then_inc(weights.products, 1)
                            tile += 1

                        for c in range(3):
                            pe.wait_ge(weights.low_ready, start + 8 + c + 1)
                            parts = weights.parts(Chunk(start + 8 + c), DT)
                            for m in range(2):
                                feature_tile(parts, lambda x, k: x[:, k, m * P:(m + 1) * P])
                        pe.wait_ge(weights.low_ready, start + 12)
                        parts = weights.parts(Chunk(start + 11), DT)
                        feature_tile(parts, lambda x, k: x[:, k, 0:P])
                        pe.wait_ge(bank_free, tile - 3)
                        for j in range(TT):
                            for k in range(DT):
                                token = [split[:, n, k, j * P:(j + 1) * P] for n in range(2)]
                                last = product(psum[:, 4 + tile % 4, j * P:(j + 1) * P], token,
                                               [x[:, k, P:2 * P] for x in parts], k == 0, k == DT - 1)
                        last.then_inc(weights.products, 1)
                        tile += 1
                        pe.wait_ge(weights.low_ready, start + 13)
                        parts = weights.parts(Chunk(start + 12), DT)
                        feature_tile(parts, lambda x, k: x[:, k, 0:KV_LORA])
                        feature_tile(parts, lambda x, k: x[:, k, KV_LORA - NOPE:KV_LORA - NOPE + P])

                    @block.scalar
                    def _(act):
                        act.sem_inc(gate_bank_free, 4)
                        with act.Fori(0, 4) as i:
                            for c in range(2):
                                weights.split_high(act, Chunk(start + c + 1, i, 2))
                                for j in (2 * c, 2 * c + 1):
                                    act.wait_ge(weights.products, i * 4 + (j + 1))
                                    nc.scalar.activation(gates[:, ds(i * 4 + j, 1), :], psum[:, j:j + 1, :], ACT.Tanh,
                                                         scale=0.5).then_inc(gate_bank_free, 1)
                        for c in range(5):
                            weights.split_high(act, Chunk(start + 9 + c))

                    @block.vector
                    def _(dve):
                        for n, target in enumerate(targets):
                            dve.wait_ge(weights.products, last_gate + n + 1)
                            for to, rows in target:
                                source = psum[rows, 4 + n % 4, :]
                                if n == 7:
                                    source = source.rearrange("p (j c) -> p j c", j=TT)
                                last = nc.vector.tensor_copy(to, source)
                            last.then_inc(bank_free, 1)

        def latent_up(q_split, kv_split, q_a, k_a, v_a):
            start = weights.start["latent_up"]
            tiles0 = weights.tiles_before[start]
            with stage("latent_up") as s:
                bank_free = s.sem("bank_free")
                with nc.Block() as block:
                    @block.sync
                    def _(sp):
                        weights.load_for(sp, "latent_up")

                    @block.gpsimd
                    def _(pool):
                        weights.split_low_all(pool, "latent_up")

                    @block.scalar
                    def _(act):
                        for c in range(2):
                            weights.split_high(act, Chunk(start + c + 1))

                    @block.tensor
                    def _(pe):
                        tile = 0
                        pe.wait_ge(weights.low_ready, start + 1)
                        parts = weights.parts(Chunk(start), 2)
                        for h in range(HEADS):
                            if tile >= 4:
                                pe.wait_ge(bank_free, tile - 3)
                            for k in range(2):
                                last = product(psum[0:DQ_A, tile % 4, :],
                                               [y[:, k, h * DQ_A:(h + 1) * DQ_A] for y in parts],
                                               (q_split[:, 0, k, :], q_split[:, 1, k, :]), k == 0, k == 1)
                            last.then_inc(weights.products, 1)
                            tile += 1
                        pe.wait_ge(weights.low_ready, start + 2)
                        parts = weights.parts(Chunk(start + 1), 1)
                        latent = (kv_split[:, 0, 0, :], kv_split[:, 1, 0, :])
                        for h in range(HEADS):
                            pe.wait_ge(bank_free, tile - 3)
                            at = h * (NOPE + DV_A)
                            last = product(psum[:, tile % 4, :], [y[:, 0, at:at + P] for y in parts],
                                           latent, True, True)
                            last.then_inc(weights.products, 1)
                            tile += 1
                        for j in range(TT):
                            pe.wait_ge(bank_free, tile - 3)
                            last = product(psum[:, tile % 4, :].rearrange("p (h c) -> p h c", h=HEADS),
                                           [y[:, j * P:(j + 1) * P] for y in latent],
                                           [y[:, 0, :].rearrange("p (h c) -> p h c", h=HEADS)[:, :, NOPE:NOPE + DV_A]
                                            for y in parts], True, True)
                            last.then_inc(weights.products, 1)
                            tile += 1

                    @block.vector
                    def _(dve):
                        tile = 0
                        for target, rows in ((q_a, DQ_A), (k_a, NOPE)):
                            for h in range(HEADS):
                                dve.wait_ge(weights.products, tiles0 + tile + 1)
                                nc.vector.tensor_copy(target[0:rows, h, :], psum[0:rows, tile % 4, :]).then_inc(bank_free, 1)
                                tile += 1
                        for j in range(TT):
                            dve.wait_ge(weights.products, tiles0 + tile + 1)
                            nc.vector.tensor_copy(v_a[:, j, :], psum[:, tile % 4, :]).then_inc(bank_free, 1)
                            tile += 1

        def rope_and_norms(q_a, k_a, k_pe, qk_b):
            with stage("rope") as s:
                table = s.sbuf("table", [P, 4, T], f32)
                squares = s.sbuf("squares", [P, 2, T], f32)
                stat = s.sbuf("stat", [P, 3, 6 * TT * 2], f32)
                turned = s.sbuf("turned", [P, 2, T], f32)
                table_in, squared, summed, mean, root, rstd = [s.sem(n) for n in (
                    "table_in", "squared", "summed", "mean", "root", "rstd")]
                spread, normed, rotated, rotation_read = [s.sem(n) for n in (
                    "spread", "normed", "rotated", "rotation_read")]
                scaled, key_roped, turned_ready = s.sem("scaled"), s.sem("key_roped"), s.sem("turned_ready")
                in_place = s.sem("in_place")
                n_a = HEADS + 1
                jobs = [(q_a[0:DQ_A, h, :], DQ_A, 0, DQ_A ** -0.5) for h in range(HEADS)]
                jobs += [(k_pe[:], P, 0, 1.0)]
                jobs += [(qk_b[:, n, :], P, 2, HD_B ** -0.5 if n < 4 else 1.0) for n in range(6)]
                with nc.Block() as block:
                    @block.sync
                    def _(sp):
                        sp.dma_start(table[:], tables.rearrange("n p t -> p n t")).then_inc(table_in, 16)

                    @block.scalar
                    def _(act):
                        for n in range(6):
                            if n >= 2:
                                act.wait_ge(summed, n - 1)
                            nc.scalar.activation(squares[:, n % 2, :], qk_b[:, n, :], ACT.Square).then_inc(squared, 1)
                        act.wait_ge(mean, 1)
                        nc.scalar.activation(stat[:, 1, :], stat[:, 0, :], ACT.Sqrt).then_inc(root, 1)

                    @block.tensor
                    def _(pe):
                        for n in range(6):
                            pe.wait_ge(squared, n + 1)
                            for j in range(TT):
                                at = (n * TT + j) * 2
                                last = nc.tensor.matmul(psum[:, 0, at:at + 2], squares[:, n % 2, j * P:(j + 1) * P],
                                                        constant("heads_of_pair"), start=True, stop=True)
                            last.then_inc(summed, 1)

                        def rotate_tile(n):
                            tile, rows, _, _ = jobs[n]
                            if n >= 2:
                                pe.wait_ge(rotation_read, n - 1)
                            nc.tensor.matmul(psum[0:rows, 1 + n % 2, :], rotate[0:rows, 0:rows], tile,
                                             start=True, stop=True).then_inc(rotated, 1)

                        for n in range(n_a):
                            rotate_tile(n)
                        pe.wait_ge(rstd, 1)
                        for n in range(6):
                            if n >= 2:
                                pe.wait_ge(normed, n - 1)
                            for j in range(TT):
                                at = (n * TT + j) * 2
                                for half in range(2):
                                    last = nc.tensor.matmul(psum[half * HD_B:(half + 1) * HD_B, 3 + n % 2, j * P:(j + 1) * P],
                                                            stat[:, 2, at + half:at + half + 1].broadcast_to([P, HD_B]),
                                                            identity, start=True, stop=True)
                            last.then_inc(spread, 1)
                        for n in range(6):
                            pe.wait_ge(normed, n + 1)
                            rotate_tile(n_a + n)

                    @block.vector
                    def _(dve):
                        dve.wait_ge(summed, 6)
                        nc.vector.tensor_scalar(stat[:, 0, :], psum[:, 0, 0:6 * TT * 2], 1.0 / HD_B, EPS,
                                                ALU.mult, ALU.add).then_inc(mean, 1)
                        dve.wait_ge(root, 1)
                        nc.vector.reciprocal(stat[:, 2, :], stat[:, 1, :]).then_inc(rstd, 1)
                        dve.wait_ge(table_in, 16)

                        def rope_tile(n):
                            tile, rows, at, scale = jobs[n]
                            buffer = turned[0:rows, n % 2, :]
                            if n >= 2:
                                dve.wait_ge(in_place, n - 1)
                            dve.wait_ge(rotated, n + 1)
                            nc.vector.scalar_tensor_tensor(out=buffer, in0=psum[0:rows, 1 + n % 2, :], scalar=scale,
                                                           in1=table[0:rows, at + 1, :], op0=ALU.mult,
                                                           op1=ALU.mult).then_inc(rotation_read, 1)
                            nc.vector.scalar_tensor_tensor(out=tile, in0=tile, scalar=scale, in1=table[0:rows, at, :],
                                                           op0=ALU.mult, op1=ALU.mult).then_inc(scaled, 1)
                            dve.wait_ge(rotation_read, n + 1)
                            dve.wait_ge(scaled, n + 1)
                            nc.vector.tensor_tensor(out=tile, in0=tile, in1=buffer, op=ALU.add).then_inc(in_place, 1)

                        for n in range(HEADS + 1):
                            rope_tile(n)
                        for n in range(6):
                            dve.wait_ge(spread, n + 1)
                            tile = qk_b[:, n, :]
                            nc.vector.scalar_tensor_tensor(out=tile, in0=tile, scalar=gain("g_qn" if n < 4 else "g_kn"),
                                                           in1=psum[:, 3 + n % 2, :], op0=ALU.mult,
                                                           op1=ALU.mult).then_inc(normed, 1)
                        for n in range(n_a, n_a + 6):
                            rope_tile(n)

                    @block.gpsimd
                    def _(pool):
                        pool.wait_ge(in_place, n_a)
                        for h in range(HEADS):
                            nc.gpsimd.tensor_copy(k_a[NOPE:DQ_A, h, :], k_pe[NOPE:DQ_A, :])

        def attention(label, pairs, out_split, out_base, q, k, v, rows, width_v, kind, decay=None):
            latent, forget = kind == "latent", kind == "forget"
            heads_on = 2 if latent else 1
            units = 2 * TT
            with stage(label) as s:
                q_st = s.sbuf("q_st", [P, heads_on, T], f32)
                k_st = s.sbuf("k_st", [P, heads_on, T], f32)
                v_st = s.sbuf("v_st", [P, TT, P], f32)
                prob = s.sbuf("prob", [P, 3, T], f32)
                prob_t = s.sbuf("prob_t", [P, 2, TT, T], f32)
                small = s.sbuf("small", [P, 3, units], f32)
                names = ["qk_staged", "v_staged", "scored", "score_read", "max_ready", "exp_ready", "sum_inverted",
                         "prob_ready", "turned", "turned_read", "attended", "high_ready", "stored"]
                (qk_staged, v_staged, scored, score_read, max_ready, exp_ready, sum_inverted,
                 prob_ready, turned, turned_read, attended, high_ready, stored) = [s.sem(n) for n in names]
                if forget:
                    rows_, cols_ = decay
                    picked = s.sbuf("picked", [FOX_HEADS, 2, T], f32)
                    c_col = s.sbuf("c_col", [P, TT, 2], f32)
                    minus_c = s.sbuf("minus_c", [P, 2, T], f32)
                    decayed = s.sbuf("decayed", [P, 3, T], f32)
                    picked_ready, decay_spread, decay_ready = [s.sem(n) for n in (
                        "picked_ready", "decay_spread", "decay_ready")]

                def keys(qt):
                    return (qt + 1) * P if forget else T

                def operand(buffer, head, at, n):
                    if latent:
                        return buffer[0:rows, head, at:at + n]
                    return buffer[head * rows:(head + 1) * rows, 0, at:at + n]

                with nc.Block() as block:
                    @block.gpsimd
                    def _(pool):
                        with pool.Fori(0, pairs) as i:
                            pool.wait_ge(score_read if forget else scored, i * units + 1)
                            if latent:
                                nc.gpsimd.tensor_copy(q_st[0:rows], q[0:rows, ds(i * 2, 2), :])
                                nc.gpsimd.tensor_copy(k_st[0:rows], k[0:rows, ds(i * 2, 2), :]).then_inc(qk_staged, 1)
                            elif forget:
                                nc.gpsimd.tensor_copy(q_st[:], q[:, ds(i, 1), :])
                                nc.gpsimd.tensor_copy(k_st[:], k[:, ds(i, 1), :]).then_inc(qk_staged, 1)
                            else:
                                nc.gpsimd.tensor_copy(q_st[:], q[:, ds(i, 1), :])
                                nc.gpsimd.tensor_copy(k_st[:], k[:, ds(i // 2 + HEADS // 2, 1), :]).then_inc(qk_staged, 1)
                            if forget:
                                for head in range(2):
                                    own = identity[0:FOX_HEADS, ds(i * 2 + head, 1)].broadcast_to([FOX_HEADS, T])
                                    nc.gpsimd.tensor_tensor(out=picked[:, head, :], in0=rows_[:], in1=own,
                                                            op=ALU.mult).then_inc(picked_ready, 1)
                                nc.gpsimd.tensor_copy(c_col[:], cols_[:, :, ds(i * 2, 2)]).then_inc(picked_ready, 1)
                            pool.wait_ge(attended, i * 2 + 1)
                            if kind == "grouped":
                                nc.gpsimd.tensor_copy(v_st[:, :, 0:width_v],
                                                      v[:, :, ds(i // 2 * width_v, width_v)]).then_inc(v_staged, 1)
                            else:
                                nc.gpsimd.tensor_copy(v_st[:], v[:, :, ds(i * P, P)]).then_inc(v_staged, 1)

                    @block.tensor
                    def _(pe):
                        pe.sem_inc(scored, 1)
                        pe.sem_inc(attended, 1)
                        with pe.Fori(0, pairs) as i:
                            def score(u):
                                head, qt = divmod(u, TT)
                                pe.wait_ge(score_read if forget else exp_ready, i * units + (1 + max(0, u - 2)))
                                out_ = psum[:, u % 3, 0:keys(qt)]
                                mm = nc.tensor.matmul(out_, operand(q_st, head, qt * P, P), operand(k_st, head, 0, keys(qt)),
                                                      start=True, stop=not forget)
                                if forget:
                                    mm = nc.tensor.matmul(psum[:, u % 3, qt * P:(qt + 1) * P], identity,
                                                          constant("causal_bias"), start=False, stop=True)
                                mm.then_inc(scored, 1)

                            def turn(u):
                                head, qt = divmod(u, TT)
                                pe.wait_ge(prob_ready, i * units + (u + 1))
                                if u >= 2:
                                    pe.wait_ge(turned_read, i * units + (u - 1))
                                for kt in range(keys(qt) // P):
                                    mm = nc.tensor.transpose(psum[:, 3 + u % 2, kt * P:(kt + 1) * P],
                                                             prob[:, u % 3, kt * P:(kt + 1) * P], identity)
                                mm.then_inc(turned, 1)

                            def attend(head):
                                pe.wait_ge(turned_read, i * units + (head + 1) * TT)
                                if head == 0:
                                    pe.wait_ge(v_staged, i + 1)
                                    pe.wait_ge(stored, i + 1)
                                for kt in range(TT):
                                    at = kt * P if forget else 0
                                    v_at = 0 if kind == "grouped" else head * width_v
                                    mm = nc.tensor.matmul(psum[head * width_v:(head + 1) * width_v, 5, at:T],
                                                          v_st[:, kt, v_at:v_at + width_v], prob_t[:, head, kt, at:T],
                                                          start=(kt == 0), stop=(kt == TT - 1))
                                mm.then_inc(attended, 1)

                            pe.wait_ge(qk_staged, i + 1)
                            if forget:
                                pe.wait_ge(picked_ready, i * 3 + 2)
                                pe.wait_ge(decay_ready, i * 2 + 1)
                                for head in range(2):
                                    nc.tensor.matmul(psum[:, 6 + head, :], ones[0:FOX_HEADS].broadcast_to([FOX_HEADS, P]),
                                                     picked[:, head, :], start=True, stop=True).then_inc(decay_spread, 1)
                            score(0)
                            score(1)
                            for u in range(units):
                                if u + 2 < units:
                                    score(u + 2)
                                turn(u)
                                if u == TT:
                                    attend(0)
                            attend(1)

                    @block.vector
                    def _(dve):
                        dve.sem_inc(score_read, 1)
                        dve.sem_inc(stored, 1)
                        with dve.Fori(0, pairs) as i:
                            def normalize(u):
                                qt = u % TT
                                dve.wait_ge(exp_ready, i * units + (u + 2))
                                nc.vector.reciprocal(small[:, 2, u:u + 1], small[:, 1, u:u + 1]).then_inc(sum_inverted, 1)
                                dve.wait_ge(sum_inverted, i * units + (u + 1))
                                nc.vector.tensor_scalar(prob[:, u % 3, 0:keys(qt)], prob[:, u % 3, 0:keys(qt)],
                                                        small[:, 2, u:u + 1], None, ALU.mult).then_inc(prob_ready, 1)

                            for u in range(units):
                                head, qt = divmod(u, TT)
                                dve.wait_ge(scored, i * units + (u + 2))
                                source = psum[:, u % 3, 0:keys(qt)]
                                if forget:
                                    if u == 0:
                                        dve.wait_ge(picked_ready, i * 3 + 3)
                                    if qt == 0:
                                        dve.wait_ge(decay_ready, i * 2 + (head + 2))
                                    nc.vector.scalar_tensor_tensor(out=decayed[:, u % 3, 0:keys(qt)], in0=source,
                                                                   scalar=c_col[:, qt, head:head + 1],
                                                                   in1=minus_c[:, head, 0:keys(qt)], op0=ALU.add,
                                                                   op1=ALU.add).then_inc(score_read, 1)
                                    dve.wait_ge(score_read, i * units + (u + 2))
                                    source = decayed[:, u % 3, 0:keys(qt)]
                                nc.vector.tensor_reduce(small[:, 0, u:u + 1], source, AX.X, ALU.max,
                                                        negate=True).then_inc(max_ready, 1)
                                if u >= 1:
                                    normalize(u - 1)
                            normalize(units - 1)
                            dve.wait_ge(high_ready, i + 1)
                            nc.vector.tensor_tensor(out=out_split[:, 1, ds(i + out_base, 1), :], in0=psum[:, 5:6, :],
                                                    in1=out_split[:, 0, ds(i + out_base, 1), :].bitcast(f32),
                                                    op=ALU.subtract).then_inc(stored, 1)

                    @block.scalar
                    def _(act):
                        act.sem_inc(exp_ready, 1)
                        if forget:
                            act.sem_inc(decay_ready, 1)
                        with act.Fori(0, pairs) as i:
                            def read_turned(u):
                                head, qt = divmod(u, TT)
                                n = keys(qt) // P
                                act.wait_ge(turned, i * units + (u + 1))
                                nc.scalar.copy(prob_t[:, head, 0:n, qt * P:(qt + 1) * P],
                                               psum[:, 3 + u % 2, 0:n * P].rearrange("p (k c) -> p k c", k=n)
                                               ).then_inc(turned_read, 1)

                            if forget:
                                for head in range(2):
                                    act.wait_ge(decay_spread, i * 2 + (head + 1))
                                    nc.scalar.activation(minus_c[:, head, :], psum[:, 6 + head, :], ACT.Copy,
                                                         scale=-1.0).then_inc(decay_ready, 1)
                            for u in range(units):
                                head, qt = divmod(u, TT)
                                act.wait_ge(max_ready, i * units + (u + 1))
                                if u >= 3:
                                    act.wait_ge(turned, i * units + (u - 2))
                                source = decayed[:, u % 3, 0:keys(qt)] if forget else psum[:, u % 3, :]
                                e = nc.scalar.activation(prob[:, u % 3, 0:keys(qt)], source, ACT.Exp,
                                                         bias=small[:, 0, u:u + 1], accum_out=small[:, 1, u:u + 1])
                                e.then_inc(exp_ready, 1)
                                if u >= 1:
                                    read_turned(u - 1)
                            read_turned(units - 1)
                            act.wait_ge(attended, i * 2 + 3)
                            nc.scalar.copy(out_split[:, 0, ds(i + out_base, 1), :], psum[:, 5:6, :]).then_inc(high_ready, 1)

        def merge(attended, gates, merged):
            start = weights.start["merge"]
            tiles0 = weights.tiles_before[start]
            with stage("merge") as s:
                part = s.sbuf("part", [P, 2, 4, T], f32)
                product_read, summed, high_ready = s.sem("product_read"), s.sem("summed"), s.sem("high_ready")
                parts_ready, low_done = s.sem("parts_ready"), s.sem("low_done")
                with nc.Block() as block:
                    @block.sync
                    def _(sp):
                        weights.load_for(sp, "merge")

                    @block.gpsimd
                    def _(pool):
                        weights.split_low_all(pool, "merge")

                    @block.tensor
                    def _(pe):
                        with pe.Fori(0, 2) as i:
                            for c in range(2):
                                chunk = Chunk(start + c, i, 2)
                                pe.wait_ge(weights.low_ready, chunk.number + 1)
                                high, low = weights.parts(chunk, 4)
                                for m in range(4):
                                    pe.wait_ge(product_read, i * 8 + 1)
                                    sl = slice(m * P, (m + 1) * P)
                                    for k in range(4):
                                        a = 4 * c + k
                                        last = product(psum[:, 4 * c + m, :], (high[:, k, sl], low[:, k, sl]),
                                                       (attended[:, 0, a, :], attended[:, 1, a, :]), k == 0, k == 3)
                                    last.then_inc(weights.products, 1)

                    @block.scalar
                    def _(act):
                        act.sem_inc(high_ready, 1)
                        with act.Fori(0, 2) as i:
                            for c in range(2):
                                weights.split_high(act, Chunk(start + c + 1, i, 2))
                            for m in range(4):
                                act.wait_ge(summed, i * 4 + (m + 1))
                                nc.scalar.activation(merged[:, 0, ds(i * 4 + m, 1), :], part[:, 0, m:m + 1, :], ACT.Copy,
                                                     scale=0.5).then_inc(high_ready, 1)

                    @block.vector
                    def _(dve):
                        dve.sem_inc(product_read, 1)
                        dve.sem_inc(low_done, 1)
                        with dve.Fori(0, 2) as i:
                            for c in range(2):
                                for m in range(4):
                                    dve.wait_ge(weights.products, i * 8 + (tiles0 + 4 * c + m + 1))
                                    if c == 0 and m == 0:
                                        dve.wait_ge(high_ready, i * 4 + 1)
                                        dve.wait_ge(low_done, i * 4 + 1)
                                    nc.vector.scalar_tensor_tensor(out=part[:, c, m:m + 1, :],
                                                                   in0=gates[:, ds(i * 4 + (DT * c + m), 1), :], scalar=1.0,
                                                                   in1=psum[:, 4 * c + m:4 * c + m + 1, :], op0=ALU.add,
                                                                   op1=ALU.mult).then_inc(product_read, 1)
                            for m in range(4):
                                dve.wait_ge(product_read, i * 8 + (6 + m))
                                nc.vector.tensor_tensor(out=part[:, 0, m, :], in0=part[:, 0, m, :], in1=part[:, 1, m, :],
                                                        op=ALU.add).then_inc(summed, 1)
                            for m in range(4):
                                dve.wait_ge(high_ready, i * 4 + (m + 2))
                                nc.vector.scalar_tensor_tensor(out=merged[:, 1, ds(i * 4 + m, 1), :], in0=part[:, 0, m:m + 1, :],
                                                               scalar=0.5, in1=merged[:, 0, ds(i * 4 + m, 1), :].bitcast(f32),
                                                               op0=ALU.mult, op1=ALU.subtract).then_inc(low_done, 1)

        def mlp(split):
            start = weights.start["mlp"]
            tiles0 = weights.tiles_before[start]
            blocks = D_FF // 256
            with stage("mlp") as s:
                hidden = s.sbuf("hidden", [P, 2, 2, 2, T], f32r)
                relu = s.sbuf("relu", [P, 2, T], f32)
                square = s.sbuf("square", [P, 2, T], f32)
                rectified, squared, high_ready, hidden_ready, added = [s.sem(n) for n in (
                    "rectified", "squared", "high_ready", "hidden_ready", "added")]

                with nc.Block() as block:
                    @block.sync
                    def _(sp):
                        weights.load_for(sp, "mlp")

                    @block.gpsimd
                    def _(pool):
                        weights.split_low_all(pool, "mlp")

                    @block.tensor
                    def _(pe):
                        def up(chunk, t, parity):
                            pe.wait_ge(weights.low_ready, chunk.number + 1)
                            high, low = weights.parts(chunk, DT)
                            for m in range(2):
                                if not isinstance(t, int) or t >= 1:
                                    pe.wait_ge(rectified, t * 2 + (m - 1))
                                sl = slice(m * P, (m + 1) * P)
                                for k in range(DT):
                                    last = product(psum[:, m, :], (high[:, k, sl], low[:, k, sl]),
                                                   (split[:, 0, k, :], split[:, 1, k, :]), k == 0, k == DT - 1)
                                last.then_inc(weights.products, 1)

                        def down(chunk, t, parity):
                            pe.wait_ge(weights.low_ready, chunk.number + 1)
                            high, low = weights.parts(chunk, 2)
                            pe.wait_ge(hidden_ready, t * 2 + 2)
                            for m in range(DT):
                                if not isinstance(t, int) or t * DT + m >= 4:
                                    pe.wait_ge(added, t * DT + (m - 3))
                                sl = slice(m * P, (m + 1) * P)
                                for k in range(2):
                                    last = product(psum[:, 4 + m % 4, :], (high[:, k, sl], low[:, k, sl]),
                                                   (hidden[:, parity, 0, k, :], hidden[:, parity, 1, k, :]),
                                                   k == 0, k == 1)
                                last.then_inc(weights.products, 1)

                        up(Chunk(start), 0, 0)
                        up(Chunk(start + 1), 1, 1)
                        down(Chunk(start + 2), 0, 0)
                        with pe.Fori(0, (blocks - 2) // 2) as i:
                            for b in range(2):
                                up(Chunk(start + 3 + 2 * b, i, 4), i * 2 + (2 + b), b)
                                down(Chunk(start + 4 + 2 * b, i, 4), i * 2 + (1 + b), (1 + b) % 2)
                        down(Chunk(start + 2 * blocks - 1), blocks - 1, 1)

                    @block.scalar
                    def _(act):
                        def high(t, parity):
                            base = t * 10 + (tiles0 - 8) if not isinstance(t, int) or t else tiles0
                            for m in range(2):
                                act.wait_ge(weights.products, base + (m + 1))
                                if not isinstance(t, int) or t >= 1:
                                    act.wait_ge(squared, t * 2 + (m - 1))
                                nc.scalar.activation(relu[:, m, :], psum[:, m, :], ACT.Relu).then_inc(rectified, 1)
                            for m in range(2):
                                act.wait_ge(squared, t * 2 + (m + 1))
                                nc.scalar.copy(hidden[:, parity, 0, m, :], square[:, m, :]).then_inc(high_ready, 1)

                        weights.split_high(act, Chunk(start + 1))
                        weights.split_high(act, Chunk(start + 2))
                        high(0, 0)
                        weights.split_high(act, Chunk(start + 3))
                        high(1, 1)
                        with act.Fori(0, (blocks - 2) // 2) as i:
                            for b in range(2):
                                weights.split_high(act, Chunk(start + 4 + 2 * b, i, 4))
                                weights.split_high(act, Chunk(start + 5 + 2 * b, i, 4))
                                high(i * 2 + (2 + b), b)
                        weights.split_high(act, Chunk(start + 2 * blocks))

                    @block.vector
                    def _(dve):
                        def hide(t, parity):
                            for m in range(2):
                                dve.wait_ge(rectified, t * 2 + (m + 1))
                                if not isinstance(t, int) or t >= 1:
                                    dve.wait_ge(hidden_ready, t * 2 + (m - 1))
                                nc.vector.tensor_tensor(out=square[:, m, :], in0=relu[:, m, :], in1=relu[:, m, :],
                                                        op=ALU.mult).then_inc(squared, 1)
                            for m in range(2):
                                dve.wait_ge(high_ready, t * 2 + (m + 1))
                                nc.vector.tensor_tensor(out=hidden[:, parity, 1, m, :], in0=square[:, m, :],
                                                        in1=hidden[:, parity, 0, m, :].bitcast(f32),
                                                        op=ALU.subtract).then_inc(hidden_ready, 1)

                        def accumulate(t):
                            last = isinstance(t, int) and t == blocks - 1
                            base = tiles0 + 10 * t + (2 if last else 4) if isinstance(t, int) else t * 10 + (tiles0 + 4)
                            for m in range(DT):
                                dve.wait_ge(weights.products, base + (m + 1))
                                nc.vector.tensor_tensor(out=x[:, m, :], in0=psum[:, 4 + m % 4, :], in1=x[:, m, :],
                                                        op=ALU.add).then_inc(added, 1)

                        hide(0, 0)
                        hide(1, 1)
                        accumulate(0)
                        with dve.Fori(0, (blocks - 2) // 2) as i:
                            for b in range(2):
                                hide(i * 2 + (2 + b), b)
                                accumulate(i * 2 + (1 + b))
                        accumulate(blocks - 1)

        def ple(split, scratch):
            start = weights.start["ple"]
            tiles0 = weights.tiles_before[start]
            with stage("ple_in") as s:
                p_rows = s.sbuf("p_rows", [P, TT, 2 * P], f32)
                p_split = s.sbuf("p_split", [P, 2, 2, T], f32r)
                p_in, turned, high_ready = s.sem("p_in"), s.sem("turned"), s.sem("high_ready")
                bank_free = s.sem("bank_free")
                low_ready = s.sem("low_ready")
                with nc.Block() as block:
                    @block.sync
                    def _(sp):
                        sp.dma_start(p_rows[:], w["p"][0, 0].rearrange("(j q) c -> q j c", q=P)).then_inc(p_in, 16)
                        weights.load(sp, Chunk(start + 2), weights.plan_item("ple", 2), 0)

                    @block.gpsimd
                    def _(pool):
                        weights.split_low(pool, Chunk(start + 1))

                    @block.scalar
                    def _(act):
                        for t in range(2):
                            act.wait_ge(turned, t + 1)
                            nc.scalar.copy(p_split[:, 0, t, :], psum[:, t, :]).then_inc(high_ready, 1)
                        weights.split_high(act, Chunk(start + 1))

                    @block.tensor
                    def _(pe):
                        pe.wait_ge(p_in, 16)
                        for t in range(2):
                            for j in range(TT):
                                last = nc.tensor.transpose(psum[:, t, j * P:(j + 1) * P], p_rows[:, j, t * P:(t + 1) * P],
                                                           identity)
                            last.then_inc(turned, 1)
                        pe.wait_ge(low_ready, 2)
                        pe.wait_ge(weights.low_ready, start + 1)
                        parts = weights.parts(Chunk(start), 2)
                        for m in range(DT):
                            if m >= 4:
                                pe.wait_ge(bank_free, m - 3)
                            for k in range(2):
                                last = product(psum[:, 4 + m % 4, :], [y[:, k, m * P:(m + 1) * P] for y in parts],
                                               (p_split[:, 0, k, :], p_split[:, 1, k, :]), k == 0, k == 1)
                            last.then_inc(weights.products, 1)

                    @block.vector
                    def _(dve):
                        for t in range(2):
                            dve.wait_ge(high_ready, t + 1)
                            nc.vector.tensor_tensor(out=p_split[:, 1, t, :], in0=psum[:, t, :],
                                                    in1=p_split[:, 0, t, :].bitcast(f32), op=ALU.subtract).then_inc(low_ready, 1)
                        for m in range(DT):
                            dve.wait_ge(weights.products, tiles0 + m + 1)
                            nc.vector.tensor_scalar(scratch[:, m, :], psum[:, 4 + m % 4, :], 0.5, None,
                                                    ALU.mult).then_inc(bank_free, 1)

            start1 = start + 1
            with stage("ple") as s:
                gated = s.sbuf("gated", [P, 2, T], f32)
                handed = s.sbuf("handed", [P, 4, T], f32)
                tanh_ready, bank_free, product_ready = s.sem("tanh_ready"), s.sem("bank_free"), s.sem("product_ready")
                with nc.Block() as block:
                    @block.sync
                    def _(sp):
                        for n in (3, 4):
                            weights.load(sp, Chunk(start + n), weights.plan_item("ple", n), 0)
                        weights.load_segments(sp, start + 5, [(1, weights.after_two(dict(weights.plan)["gdn_in"])[0])])

                    @block.gpsimd
                    def _(pool):
                        for n in range(4):
                            weights.split_low(pool, Chunk(start1 + n + 1))

                    @block.tensor
                    def _(pe):
                        for n in range(4):
                            pe.wait_ge(weights.low_ready, start1 + n + 1)
                            high, low = weights.parts(Chunk(start1 + n), DT)
                            for m in range(2):
                                tile = 2 * n + m
                                if tile >= 4:
                                    pe.wait_ge(bank_free, tile - 3)
                                sl = slice(m * P, (m + 1) * P)
                                for k in range(DT):
                                    last = product(psum[:, tile % 4, :], (high[:, k, sl], low[:, k, sl]),
                                                   (split[:, 0, k, :], split[:, 1, k, :]), k == 0, k == DT - 1)
                                last.then_inc(weights.products, 1)

                    @block.scalar
                    def _(act):
                        for n in range(4):
                            weights.split_high(act, Chunk(start1 + n + 1))
                            for m in range(2):
                                tile = 2 * n + m
                                act.wait_ge(weights.products, tiles0 + DT + tile + 1)
                                if tile >= 4:
                                    act.wait_ge(product_ready, tile - 3)
                                nc.scalar.activation(handed[:, tile % 4, :], psum[:, tile % 4, :], ACT.Tanh,
                                                     scale=0.5).then_inc(bank_free, 1)

                    @block.vector
                    def _(dve):
                        for tile in range(DT):
                            dve.wait_ge(bank_free, tile + 1)
                            nc.vector.scalar_tensor_tensor(out=gated[:, tile % 2, :], in0=handed[:, tile % 4, :], scalar=1.0,
                                                           in1=scratch[:, tile, :], op0=ALU.add,
                                                           op1=ALU.mult).then_inc(product_ready, 1)
                            dve.wait_ge(product_ready, tile + 1)
                            nc.vector.tensor_tensor(out=x[:, tile, :], in0=x[:, tile, :], in1=gated[:, tile % 2, :],
                                                    op=ALU.add).then_inc(tanh_ready, 1)

        def swiglu(label, split, total):
            start = weights.start[label]
            tiles0 = weights.tiles_before[start]
            blocks = D_FF2 // 256
            with stage(label) as s:
                hidden = s.sbuf("hidden", [P, 2, 2, 2, T], f32r)
                tanh = s.sbuf("tanh", [P, 2, T], f32)
                gated = s.sbuf("gated", [P, 2, T], f32)
                inner = s.sbuf("inner", [P, 2, T], f32)
                tanh_ready, gated_ready, inner_ready, high_ready, hidden_ready, added = [s.sem(n) for n in (
                    "tanh_ready", "gated_ready", "inner_ready", "high_ready", "hidden_ready", "added")]

                def first(t):
                    return isinstance(t, int) and t == 0

                def gate_tiles(t):
                    return tiles0 if first(t) else t * 12 + (tiles0 - 8)

                def up_tiles(t):
                    return tiles0 + 2 if first(t) else t * 12 + (tiles0 - 6)

                with nc.Block() as block:
                    @block.sync
                    def _(sp):
                        weights.load_for(sp, label)

                    @block.gpsimd
                    def _(pool):
                        weights.split_low_all(pool, label)

                    @block.tensor
                    def _(pe):
                        def into_hidden(chunk, t, bank, read):
                            pe.wait_ge(weights.low_ready, chunk.number + 1)
                            high, low = weights.parts(chunk, DT)
                            for m in range(2):
                                if not first(t):
                                    pe.wait_ge(read, t * 2 + (m - 1))
                                sl = slice(m * P, (m + 1) * P)
                                for k in range(DT):
                                    last = product(psum[:, bank + m, :], (high[:, k, sl], low[:, k, sl]),
                                                   (split[:, 0, k, :], split[:, 1, k, :]), k == 0, k == DT - 1)
                                last.then_inc(weights.products, 1)

                        def down(chunk, t, parity):
                            pe.wait_ge(weights.low_ready, chunk.number + 1)
                            high, low = weights.parts(chunk, 2)
                            pe.wait_ge(hidden_ready, t * 2 + 2)
                            for m in range(DT):
                                pe.wait_ge(added, t * DT + (m + 5))
                                sl = slice(m * P, (m + 1) * P)
                                for k in range(2):
                                    last = product(psum[:, 4 + m % 4, :], (high[:, k, sl], low[:, k, sl]),
                                                   (hidden[:, parity, 0, k, :], hidden[:, parity, 1, k, :]),
                                                   k == 0, k == 1)
                                last.then_inc(weights.products, 1)

                        into_hidden(Chunk(start), 0, 0, gated_ready)
                        into_hidden(Chunk(start + 1), 0, 2, inner_ready)
                        with pe.Fori(0, blocks // 2) as i:
                            for b in range(2):
                                t = i * 2 + (b + 1)
                                into_hidden(Chunk(start + 2 + 3 * b, i, 6), t, 0, gated_ready)
                                into_hidden(Chunk(start + 3 + 3 * b, i, 6), t, 2, inner_ready)
                                down(Chunk(start + 4 + 3 * b, i, 6), i * 2 + b if b else i * 2, b)
                        down(Chunk(start + 3 * blocks - 1), blocks - 1, 0)

                    @block.scalar
                    def _(act):
                        def gate(t):
                            for m in range(2):
                                act.wait_ge(weights.products, gate_tiles(t) + (m + 1))
                                if not first(t):
                                    act.wait_ge(gated_ready, t * 2 + (m - 1))
                                nc.scalar.activation(tanh[:, m, :], psum[:, m, :], ACT.Tanh, scale=0.5).then_inc(tanh_ready, 1)

                        def high(t, parity):
                            for m in range(2):
                                act.wait_ge(inner_ready, t * 2 + (m + 1))
                                nc.scalar.copy(hidden[:, parity, 0, m, :], inner[:, m, :]).then_inc(high_ready, 1)

                        weights.split_high(act, Chunk(start + 1))
                        weights.split_high(act, Chunk(start + 2))
                        gate(0)
                        high(0, 0)
                        with act.Fori(0, blocks // 2) as i:
                            for b in range(2):
                                t = i * 2 + (b + 1)
                                weights.split_high(act, Chunk(start + 3 + 3 * b, i, 6))
                                weights.split_high(act, Chunk(start + 4 + 3 * b, i, 6))
                                gate(t)
                                weights.split_high(act, Chunk(start + 5 + 3 * b, i, 6))
                                high(t, (b + 1) % 2)
                        weights.split_high(act, Chunk(start + 3 * blocks))

                    @block.vector
                    def _(dve):
                        def hide(t, parity):
                            for m in range(2):
                                dve.wait_ge(tanh_ready, t * 2 + (m + 1))
                                if not first(t):
                                    dve.wait_ge(inner_ready, t * 2 + (m - 1))
                                nc.vector.scalar_tensor_tensor(out=gated[:, m, :], in0=tanh[:, m, :], scalar=1.0,
                                                               in1=psum[:, m, :], op0=ALU.add,
                                                               op1=ALU.mult).then_inc(gated_ready, 1)
                            for m in range(2):
                                dve.wait_ge(weights.products, up_tiles(t) + (m + 1))
                                dve.wait_ge(gated_ready, t * 2 + (m + 1))
                                if not first(t):
                                    dve.wait_ge(hidden_ready, t * 2 + (m - 1))
                                nc.vector.scalar_tensor_tensor(out=inner[:, m, :], in0=gated[:, m, :], scalar=0.5,
                                                               in1=psum[:, 2 + m, :], op0=ALU.mult,
                                                               op1=ALU.mult).then_inc(inner_ready, 1)
                            for m in range(2):
                                dve.wait_ge(high_ready, t * 2 + (m + 1))
                                nc.vector.tensor_tensor(out=hidden[:, parity, 1, m, :], in0=inner[:, m, :],
                                                        in1=hidden[:, parity, 0, m, :].bitcast(f32),
                                                        op=ALU.subtract).then_inc(hidden_ready, 1)

                        def accumulate(t):
                            last = isinstance(t, int) and t == blocks - 1
                            base = tiles0 + 12 * t + 4 if last else t * 12 + (tiles0 + 8)
                            for m in range(DT):
                                dve.wait_ge(weights.products, base + (m + 1))
                                dve.wait_ge(added, t * DT + (m + 1))
                                nc.vector.tensor_tensor(out=total[:, m, :], in0=psum[:, 4 + m % 4, :], in1=total[:, m, :],
                                                        op=ALU.add).then_inc(added, 1)

                        nc.vector.memset(total[:], 0.0).then_inc(added, DT)
                        hide(0, 0)
                        with dve.Fori(0, blocks // 2) as i:
                            for b in range(2):
                                hide(i * 2 + (b + 1), (b + 1) % 2)
                                accumulate(i * 2 + b if b else i * 2)
                        accumulate(blocks - 1)

        def copy_to(target, scale=None):
            def finish(bank, _, tile):
                if scale is None:
                    return nc.vector.tensor_copy(target[:, ds(tile, 1), :], psum[:, bank:bank + 1, :])
                return nc.vector.tensor_scalar(target[:, ds(tile, 1), :], psum[:, bank:bank + 1, :], scale, None, ALU.mult)
            return finish

        def gdn_in(split, qkv, z2, conv, ba):
            start = weights.start["gdn_in"]
            tiles0 = weights.tiles_before[start]
            tiles_z = tiles0 + 3 * GH
            tiles_ba = tiles_z + GH
            with stage("gdn_in") as s:
                mixed = s.sbuf("mixed", [P, 2, T], f32)
                tanh = s.sbuf("tanh", [P, 2, T], f32)
                bank_free, tap_done, convolved, tanh_ready, activated = [s.sem(n) for n in (
                    "bank_free", "tap_done", "convolved", "tanh_ready", "activated")]
                z_tanh, z_ready = s.sem("z_tanh"), s.sem("z_ready")
                with nc.Block() as block:
                    @block.sync
                    def _(sp):
                        weights.load_for(sp, "gdn_in")

                    @block.gpsimd
                    def _(pool):
                        weights.split_low_all(pool, "gdn_in")

                    @block.tensor
                    def _(pe):
                        def turn(i, first_chunk, free, base):
                            for c in range(2):
                                chunk = Chunk(first_chunk + c, i, 2)
                                pe.wait_ge(weights.low_ready, chunk.number + 1)
                                high, low = weights.parts(chunk, DT)
                                for j in (2 * c, 2 * c + 1):
                                    pe.wait_ge(free, i * 4 + (j + 1))
                                    sl = slice((j % 2) * P, (j % 2 + 1) * P)
                                    for k in range(DT):
                                        last = product(psum[:, base + j, :], (high[:, k, sl], low[:, k, sl]),
                                                       (split[:, 0, k, :], split[:, 1, k, :]), k == 0, k == DT - 1)
                                    last.then_inc(weights.products, 1)

                        with pe.Fori(0, 6) as i:
                            turn(i, start, bank_free, 0)
                        with pe.Fori(0, 2) as i:
                            turn(i, start + 12, z_ready, 4)
                        pe.wait_ge(weights.low_ready, start + 17)
                        parts = weights.parts(Chunk(start + 16), DT)
                        for n, at in enumerate((256 - 2 * GH - 64, 256 - GH - 64)):
                            for k in range(DT):
                                last = product(psum[0:64 + GH, n, :], [y[:, k, at:at + 64 + GH] for y in parts],
                                               (split[:, 0, k, :], split[:, 1, k, :]), k == 0, k == DT - 1)
                            last.then_inc(weights.products, 1)

                    @block.scalar
                    def _(act):
                        act.sem_inc(z_ready, 4)
                        with act.Fori(0, 6) as i:
                            for c in range(2):
                                weights.split_high(act, Chunk(start + c + 1, i, 2))
                                for j in (2 * c, 2 * c + 1):
                                    act.wait_ge(weights.products, i * 4 + (tiles0 + j + 1))
                                    act.wait_ge(activated, i * 4 + (j + 1))
                                    nc.scalar.activation(mixed[:, j % 2, :], psum[:, j, :], ACT.Copy,
                                                         scale=conv[:, ds(i * 4 + (j + 3 * 3 * GH), 1)]).then_inc(tap_done, 1)
                                    act.wait_ge(bank_free, i * 4 + (j + 5))
                                    nc.scalar.activation(tanh[:, j % 2, :], mixed[:, j % 2, :], ACT.Tanh,
                                                         scale=0.5).then_inc(tanh_ready, 1)
                        act.wait_ge(activated, 3 * GH + 2)
                        with act.Fori(0, 2) as i:
                            for c in range(2):
                                weights.split_high(act, Chunk(start + 12 + c + 1, i, 2))
                                for j in (2 * c, 2 * c + 1):
                                    act.wait_ge(weights.products, i * 4 + (tiles_z + j + 1))
                                    act.wait_ge(z_ready, i * 4 + (j + 3))
                                    nc.scalar.activation(tanh[:, j % 2, :], psum[:, 4 + j, :], ACT.Tanh,
                                                         scale=0.5).then_inc(z_tanh, 1)
                        weights.split_high(act, Chunk(start + 17))

                    @block.vector
                    def _(dve):
                        dve.sem_inc(bank_free, 4)
                        dve.sem_inc(activated, 2)
                        with dve.Fori(0, 6) as i:
                            for j in range(4):
                                dve.wait_ge(tap_done, i * 4 + (j + 1))
                                for tap in (2, 1, 0):
                                    back = 3 - tap
                                    if tap < 2:
                                        dve.wait_ge(convolved, i * 8 + (2 * j + back - 1))
                                    nc.vector.scalar_tensor_tensor(
                                        out=mixed[:, j % 2, back:T], in0=psum[:, j, 0:T - back],
                                        scalar=conv[:, ds(i * 4 + (j + tap * 3 * GH), 1)],
                                        in1=mixed[:, j % 2, back:T], op0=ALU.mult, op1=ALU.add).then_inc(bank_free if tap == 0 else convolved, 1)
                                dve.wait_ge(tanh_ready, i * 4 + (j + 1))
                                nc.vector.scalar_tensor_tensor(out=qkv[:, ds(i * 4 + j, 1), :], in0=tanh[:, j % 2:j % 2 + 1, :],
                                                               scalar=1.0, in1=mixed[:, j % 2:j % 2 + 1, :], op0=ALU.add,
                                                               op1=ALU.mult).then_inc(activated, 1)
                        with dve.Fori(0, 2) as i:
                            for j in range(4):
                                dve.wait_ge(z_tanh, i * 4 + (j + 1))
                                nc.vector.scalar_tensor_tensor(out=z2[:, ds(i * 4 + j, 1), :], in0=tanh[:, j % 2:j % 2 + 1, :],
                                                               scalar=1.0, in1=psum[:, 4 + j:5 + j, :], op0=ALU.add,
                                                               op1=ALU.mult).then_inc(z_ready, 1)
                        for n in range(2):
                            dve.wait_ge(weights.products, tiles_ba + n + 1)
                            nc.vector.tensor_copy(ba[:, n, :], psum[64:64 + GH, n, :])

        def gdn_rows(qkv, ba, rows, columns):
            with stage("gdn_rows") as s:
                squares = s.sbuf("squares", [P, 2, T], f32)
                work = s.sbuf("work", [GH, 8, T], f32)
                head_col = s.sbuf("head_col", [GH, 3], f32)
                loaded, squared, summed, act_done, dve_done = [s.sem(n) for n in (
                    "loaded", "squared", "summed", "act_done", "dve_done")]
                turned = s.sem("turned")
                b_raw, a_raw = ba[:, 0, :], ba[:, 1, :]
                y, size, e, sp, q_mean, k_mean, decay, one = [work[:, n, :] for n in range(8)]
                big_g = rows[:, 3, :]

                def by_chunk(row, n):
                    return row[:, n * P:(n + 1) * P]

                with nc.Block() as block:
                    @block.sync
                    def _(sp):
                        sp.dma_start(head_col[:, 0:1], w["gdn_a_log_2"].rearrange("l h -> h l")).then_inc(loaded, 16)
                        sp.dma_start(head_col[:, 1:2], w["gdn_dt_bias_2"].rearrange("l h -> h l")).then_inc(loaded, 16)

                    @block.tensor
                    def _(pe):
                        for n in range(2 * GH):
                            pe.wait_ge(squared, n + 1)
                            nc.tensor.matmul(psum[0:GH, n // GH, :], constant("head_select")[:, n % GH * GH:(n % GH + 1) * GH],
                                             squares[:, n % 2, :], start=(n % GH == 0), stop=(n % GH == GH - 1)
                                             ).then_inc(summed, 1)
                        pe.wait_ge(dve_done, 12)
                        pe.wait_ge(act_done, 7)
                        for m, row in enumerate((big_g, y, decay)):
                            for n in range(TT):
                                at = (n * 3 + m) * GH
                                last = nc.tensor.transpose(psum[:, 2, at:at + GH], by_chunk(row, n), identity[0:GH, 0:GH])
                        last.then_inc(turned, 1)

                    @block.scalar
                    def _(act):
                        for n in range(2 * GH):
                            if n >= 2:
                                act.wait_ge(summed, n - 1)
                            nc.scalar.activation(squares[:, n % 2, :], qkv[:, n, :], ACT.Square).then_inc(squared, 1)
                        act.wait_ge(loaded, 32)
                        nc.scalar.activation(head_col[:, 2:3], head_col[:, 0:1], ACT.Exp).then_inc(act_done, 1)
                        nc.scalar.activation(sp, b_raw, ACT.Exp, scale=-1.0).then_inc(act_done, 1)
                        act.wait_ge(dve_done, 2)
                        nc.scalar.activation(e, size, ACT.Exp, scale=-1.0).then_inc(act_done, 1)
                        act.wait_ge(dve_done, 3)
                        nc.scalar.activation(e, e, ACT.Ln).then_inc(act_done, 1)
                        act.wait_ge(dve_done, 9)
                        for n, mean in enumerate((q_mean, k_mean)):
                            nc.scalar.activation(mean, mean, ACT.Sqrt).then_inc(act_done, 1)
                        act.wait_ge(dve_done, 10)
                        nc.scalar.activation(decay, decay, ACT.Exp).then_inc(act_done, 1)

                    @block.vector
                    def _(dve):
                        dve.wait_ge(loaded, 32)
                        nc.vector.memset(one, 1.0)
                        nc.vector.tensor_scalar(y, a_raw, head_col[:, 1:2], None, ALU.add).then_inc(dve_done, 1)
                        dve.wait_ge(dve_done, 1)
                        nc.vector.scalar_tensor_tensor(out=size, in0=y, scalar=-1.0, in1=y, op0=ALU.mult,
                                                       op1=ALU.max).then_inc(dve_done, 1)
                        dve.wait_ge(act_done, 3)
                        nc.vector.tensor_scalar(e, e, 1.0, None, ALU.add).then_inc(dve_done, 1)
                        dve.wait_ge(act_done, 4)
                        nc.vector.scalar_tensor_tensor(out=size, in0=y, scalar=0.0, in1=e, op0=ALU.max,
                                                       op1=ALU.add).then_inc(dve_done, 1)
                        dve.wait_ge(dve_done, 4)
                        nc.vector.tensor_scalar(size, size, head_col[:, 2:3], -1.0, ALU.mult, ALU.mult).then_inc(dve_done, 1)
                        dve.wait_ge(dve_done, 5)
                        for n in range(TT):
                            last = nc.vector.tensor_tensor_scan(by_chunk(big_g, n), by_chunk(one, n), by_chunk(size, n), 0.0,
                                                                ALU.mult, ALU.add)
                        last.then_inc(dve_done, 1)
                        nc.vector.tensor_scalar(sp, sp, 1.0, None, ALU.add).then_inc(dve_done, 1)
                        dve.wait_ge(summed, 2 * GH)
                        for n, mean in enumerate((q_mean, k_mean)):
                            nc.vector.tensor_scalar(mean, psum[0:GH, n, :], 0.25, EPS, ALU.mult, ALU.add).then_inc(dve_done, 1)
                        dve.wait_ge(dve_done, 6)
                        for n in range(TT):
                            last = nc.vector.tensor_scalar(by_chunk(decay, n), by_chunk(big_g, n), -1.0,
                                                           big_g[:, (n + 1) * P - 1:(n + 1) * P], ALU.mult, ALU.add)
                        last.then_inc(dve_done, 1)
                        dve.wait_ge(dve_done, 7)
                        nc.vector.reciprocal(rows[:, 2, :], sp).then_inc(dve_done, 1)
                        dve.wait_ge(dve_done, 11)
                        nc.vector.tensor_scalar(y, rows[:, 2, :], 0.5, None, ALU.mult).then_inc(dve_done, 1)
                        dve.wait_ge(act_done, 6)
                        nc.vector.reciprocal(rows[:, 0, :], q_mean).then_inc(dve_done, 1)
                        nc.vector.reciprocal(rows[:, 1, :], k_mean).then_inc(dve_done, 1)
                        dve.wait_ge(dve_done, 14)
                        nc.vector.tensor_scalar(rows[:, 0, :], rows[:, 0, :], 0.5 * P ** -0.5, None, ALU.mult)
                        nc.vector.tensor_scalar(rows[:, 1, :], rows[:, 1, :], 0.5, None, ALU.mult)
                        dve.wait_ge(turned, 1)
                        nc.vector.tensor_copy(columns[:], psum[:, 2, 0:TT * 3 * GH].rearrange("p (n m h) -> p n m h", n=TT, m=3))

        def gdn_chunks(qkv, rows, columns):
            H = GH
            with stage("gdn_chunks") as s:
                def matrix(name):
                    return s.sbuf(name, [P, H, P], f32)

                (qn, kn, kb, kbg, qg, grow, decay, part0, part1, kd, bv, lt, aq, u_, t_, y_, state) = [matrix(n) for n in (
                    "query", "key", "key_beta", "key_beta_grown", "query_grown", "grown", "decay", "part0", "part1",
                    "key_decayed", "value_beta", "lower_t", "query_key", "inverse_t", "inverse", "product", "state")]
                parts = (part0, part1)
                last_growth = s.sbuf("last_growth", [P, H], f32)
                cols = s.sbuf("cols", [P, 3, H], f32)
                mask = s.sbuf("mask", [P, 8, P], f32)
                names = ["masks_in", "cols_in", "q_spread", "k_spread", "b_spread", "g_spread", "q_ready", "k_ready",
                         "kb_ready", "grown_ready", "diff_ready", "diff_exp", "decay_ready", "v_staged", "qg_ready",
                         "kbg_ready", "k_turned", "kd_ready", "v_turned", "bv_ready", "kk_done", "lt_ready", "qk_done",
                         "aq_ready", "u_ready", "t_ready", "part_ready", "part_turned", "y_done", "y_ready", "zt_done",
                         "z_done", "ks_done", "r_ready", "vn_done", "vn_ready", "o_done", "o_read", "ds_done",
                         "state_ready", "last_ready", "part_first"]
                S = {n: s.sem(n) for n in names}

                def pair(n):
                    return psum[:, 2 * n:2 * n + 2, :].rearrange("p b (h c) -> p (b h) c", h=4)

                A, B, C, E = [pair(n) for n in range(4)]

                def chunk_of(first_tile, i):
                    return qkv[:, first_tile:first_tile + H, ds(i * P, P)]

                def over_heads(m):
                    return m.unsqueeze(1).broadcast_to([P, H, P])

                def over_columns(c):
                    return c.unsqueeze(2).broadcast_to([P, H, P])

                with nc.Block() as block:
                    @block.sync
                    def _(sp):
                        at = CONST_AT["earlier"][0]
                        sp.dma_start(mask[:].rearrange("p n c -> p (n c)"), constants[:, at:at + 8 * P]).then_inc(S["masks_in"], 16)

                    @block.tensor
                    def _(pe):
                        for name in ("ds_done", "zt_done", "o_done"):
                            pe.sem_inc(S[name], 1)
                        with pe.Fori(0, TT) as i:
                            def spread(target, row, done):
                                for h in range(H):
                                    last = nc.tensor.matmul(target[:, h, :], identity[0:H, h:h + 1].broadcast_to([H, P]),
                                                            rows[:, row, ds(i * P, P)], start=True, stop=True)
                                last.then_inc(S[done], 1)

                            def heads(target, left, right, done):
                                for h in range(H):
                                    last = nc.tensor.matmul(target[:, h, :], left[:, h, :], right[:, h, :], start=True, stop=True)
                                last.then_inc(S[done], 1)

                            def turn(target, source, done):
                                for h in range(H):
                                    last = nc.tensor.transpose(target[:, h, :], source[:, h, :], identity)
                                last.then_inc(S[done], 1)

                            pe.wait_ge(S["vn_ready"], i + 1)
                            spread(A, 0, "q_spread")
                            pe.wait_ge(S["o_read"], i + 1)
                            spread(B, 1, "k_spread")
                            pe.wait_ge(S["state_ready"], i + 1)
                            spread(C, 2, "b_spread")
                            spread(E, 3, "g_spread")
                            pe.wait_ge(S["k_ready"], i + 1)
                            turn(A, kn, "k_turned")
                            pe.wait_ge(S["v_staged"], i + 1)
                            turn(B, y_, "v_turned")
                            pe.wait_ge(S["kb_ready"], i + 1)
                            heads(C, kn, kb, "kk_done")
                            pe.wait_ge(S["diff_ready"], i + 1)
                            pe.wait_ge(S["grown_ready"], i + 1)
                            heads(E, kn, qn, "qk_done")
                            pe.wait_ge(S["part_first"], i + 1)
                            pe.wait_ge(S["kd_ready"], i + 1)
                            turn(A, part0, "part_turned")
                            for level in range(1, 7):
                                n = i * 6 + level
                                pe.wait_ge(S["part_ready"], n)
                                pe.wait_ge(S["t_ready"], n)
                                heads(A, parts[level % 2], t_, "y_done")
                                pe.wait_ge(S["y_ready"], n)
                                pe.wait_ge(S["u_ready"], i * 7 + level)
                                heads(B, y_, u_, "zt_done")
                                if level < 6:
                                    heads(C, u_, y_, "z_done")
                            pe.wait_ge(S["aq_ready"], i + 1)
                            pe.wait_ge(S["kbg_ready"], i + 1)
                            heads(E, kbg, state, "ks_done")
                            pe.wait_ge(S["u_ready"], i * 7 + 7)
                            pe.wait_ge(S["r_ready"], i + 1)
                            heads(A, u_, kb, "vn_done")
                            pe.wait_ge(S["qg_ready"], i + 1)
                            pe.wait_ge(S["vn_ready"], i + 2)
                            for h in range(H):
                                nc.tensor.matmul(B[:, h, :], state[:, h, :], qg[:, h, :], start=True, stop=False)
                                last = nc.tensor.matmul(B[:, h, :], grow[:, h, :], aq[:, h, :], start=False, stop=True)
                            last.then_inc(S["o_done"], 1)
                            heads(C, kd, grow, "ds_done")

                    @block.vector
                    def _(dve):
                        def tt(out_, in0, in1, op, done):
                            nc.vector.tensor_tensor(out=out_, in0=in0, in1=in1, op=op).then_inc(S[done], 1)

                        nc.vector.memset(state[:], 0.0).then_inc(S["last_ready"], 1)
                        dve.wait_ge(S["masks_in"], 16)
                        dve.sem_inc(S["state_ready"], 1)
                        with dve.Fori(0, TT) as i:
                            nc.vector.tensor_copy(cols[:].unsqueeze(1), columns[:, ds(i, 1), :, :]).then_inc(S["cols_in"], 1)
                            dve.wait_ge(S["q_spread"], i + 1)
                            tt(qn[:], chunk_of(0, i), A, ALU.mult, "q_ready")
                            dve.wait_ge(S["k_spread"], i + 1)
                            tt(kn[:], chunk_of(H, i), B, ALU.mult, "k_ready")
                            dve.wait_ge(S["b_spread"], i + 1)
                            dve.wait_ge(S["k_ready"], i + 1)
                            tt(kb[:], kn[:], C, ALU.mult, "kb_ready")
                            dve.wait_ge(S["g_spread"], i + 1)
                            dve.wait_ge(S["cols_in"], i + 1)
                            for h in range(H):
                                last = nc.vector.tensor_scalar(decay[:, h, :], E[:, h, :], cols[:, 0, h:h + 1], 0.0,
                                                               ALU.subtract, ALU.min)
                            last.then_inc(S["diff_ready"], 1)
                            dve.wait_ge(S["diff_exp"], i + 1)
                            tt(decay[:], decay[:], over_heads(mask[:, 0, :]), ALU.mult, "decay_ready")
                            dve.wait_ge(S["kk_done"], i + 1)
                            dve.wait_ge(S["decay_ready"], i + 1)
                            tt(lt[:], decay[:], C, ALU.mult, "lt_ready")
                            dve.wait_ge(S["lt_ready"], i + 1)
                            tt(part0[:], lt[:], over_heads(mask[:, 1, :]), ALU.mult, "part_first")
                            dve.wait_ge(S["part_first"], i + 1)
                            tt(u_[:], over_heads(identity), part0[:], ALU.subtract, "u_ready")
                            dve.wait_ge(S["k_turned"], i + 1)
                            tt(kd[:], A, over_columns(cols[:, 2, :]), ALU.mult, "kd_ready")
                            dve.wait_ge(S["v_turned"], i + 1)
                            tt(bv[:], B, over_columns(cols[:, 1, :]), ALU.mult, "bv_ready")
                            dve.wait_ge(S["part_turned"], i + 1)
                            tt(t_[:], over_heads(identity), A, ALU.subtract, "t_ready")
                            dve.wait_ge(S["qk_done"], i + 1)
                            tt(aq[:], decay[:], E, ALU.mult, "aq_ready")
                            dve.wait_ge(S["grown_ready"], i + 1)
                            nc.vector.tensor_copy(last_growth[:].unsqueeze(2), grow[:, :, P - 1:P]).then_inc(S["last_ready"], 1)
                            for level in range(1, 7):
                                if level < 6:
                                    dve.wait_ge(S["z_done"], i * 5 + level)
                                    dve.wait_ge(S["t_ready"], i * 6 + level)
                                    dve.wait_ge(S["zt_done"], i * 6 + (level + 1))
                                    dve.wait_ge(S["u_ready"], i * 7 + level)
                                    tt(t_[:], t_[:], C, ALU.subtract, "t_ready")
                                    tt(u_[:], u_[:], B, ALU.subtract, "u_ready")
                                else:
                                    dve.wait_ge(S["zt_done"], i * 6 + (level + 1))
                                    dve.wait_ge(S["u_ready"], i * 7 + level)
                                    tt(u_[:], u_[:], B, ALU.subtract, "u_ready")
                            dve.wait_ge(S["ks_done"], i + 1)
                            dve.wait_ge(S["bv_ready"], i + 1)
                            dve.wait_ge(S["kbg_ready"], i + 1)
                            tt(kb[:], bv[:], E, ALU.subtract, "r_ready")
                            dve.wait_ge(S["ds_done"], i + 2)
                            dve.wait_ge(S["last_ready"], i + 2)
                            for h in range(H):
                                last = nc.vector.scalar_tensor_tensor(out=state[:, h, :], in0=state[:, h, :],
                                                                      scalar=last_growth[:, h:h + 1], in1=C[:, h, :],
                                                                      op0=ALU.mult, op1=ALU.add)
                            last.then_inc(S["state_ready"], 1)

                    @block.scalar
                    def _(act):
                        for name in ("vn_ready", "o_read"):
                            act.sem_inc(S[name], 1)
                        with act.Fori(0, TT) as i:
                            act.wait_ge(S["g_spread"], i + 1)
                            act.wait_ge(S["ds_done"], i + 1)
                            act.wait_ge(S["diff_ready"], i + 1)
                            nc.scalar.activation(grow[:], E, ACT.Exp).then_inc(S["grown_ready"], 1)
                            nc.scalar.activation(decay[:], decay[:], ACT.Exp).then_inc(S["diff_exp"], 1)
                            for level in range(1, 7):
                                act.wait_ge(S["y_done"], i * 6 + level)
                                nc.scalar.copy(y_[:], A).then_inc(S["y_ready"], 1)
                            act.wait_ge(S["vn_done"], i + 1)
                            act.wait_ge(S["kbg_ready"], i + 1)
                            act.wait_ge(S["last_ready"], i + 2)
                            nc.scalar.copy(grow[:], A).then_inc(S["vn_ready"], 1)
                            act.wait_ge(S["o_done"], i + 2)
                            nc.scalar.copy(chunk_of(0, i), B).then_inc(S["o_read"], 1)

                    @block.gpsimd
                    def _(pool):
                        pool.wait_ge(S["masks_in"], 16)
                        with pool.Fori(0, TT) as i:
                            pool.wait_ge(S["zt_done"], i * 6 + 1)
                            nc.gpsimd.tensor_copy(y_[:], chunk_of(2 * H, i)).then_inc(S["v_staged"], 1)
                            pool.wait_ge(S["lt_ready"], i + 1)
                            for level in range(1, 7):
                                if level == 2:
                                    pool.wait_ge(S["part_turned"], i + 1)
                                    pool.wait_ge(S["u_ready"], i * 7 + 1)
                                if level >= 3:
                                    pool.wait_ge(S["y_done"], i * 6 + (level - 2))
                                nc.gpsimd.tensor_tensor(out=parts[level % 2][:], in0=lt[:], in1=over_heads(mask[:, 1 + level, :]),
                                                        op=ALU.mult).then_inc(S["part_ready"], 1)
                                if level == 1:
                                    pool.wait_ge(S["grown_ready"], i + 1)
                                    pool.wait_ge(S["q_ready"], i + 1)
                                    pool.wait_ge(S["o_done"], i + 1)
                                    nc.gpsimd.tensor_tensor(out=qg[:], in0=qn[:], in1=grow[:], op=ALU.mult).then_inc(S["qg_ready"], 1)
                                    pool.wait_ge(S["kb_ready"], i + 1)
                                    nc.gpsimd.tensor_tensor(out=kbg[:], in0=kb[:], in1=grow[:], op=ALU.mult).then_inc(S["kbg_ready"], 1)

        def gdn_post(qkv, z2, split):
            with stage("gdn_post") as s:
                squares = s.sbuf("squares", [P, 2, T], f32)
                row = s.sbuf("row", [GH, T], f32)
                factor = s.sbuf("factor", [GH, T], f32)
                normed = s.sbuf("normed", [P, 2, T], f32)
                gated = s.sbuf("gated", [P, 2, T], f32)
                squared, summed, mean, root, ready, spread, normed_ready, gated_ready, high_ready, low_done = [s.sem(n) for n in (
                    "squared", "summed", "mean", "root", "ready", "spread", "normed_ready", "gated_ready", "high_ready", "low_done")]
                with nc.Block() as block:
                    @block.scalar
                    def _(act):
                        for h in range(GH):
                            if h >= 2:
                                act.wait_ge(summed, h - 1)
                            nc.scalar.activation(squares[:, h % 2, :], qkv[:, h, :], ACT.Square).then_inc(squared, 1)
                        act.wait_ge(mean, 1)
                        nc.scalar.activation(row[:], row[:], ACT.Sqrt).then_inc(root, 1)
                        for h in range(GH):
                            act.wait_ge(gated_ready, h + 1)
                            nc.scalar.copy(split[:, 0, h, :], gated[:, h % 2, :]).then_inc(high_ready, 1)

                    @block.tensor
                    def _(pe):
                        for h in range(GH):
                            pe.wait_ge(squared, h + 1)
                            nc.tensor.matmul(psum[0:GH, 0, :], constant("head_select")[:, h * GH:(h + 1) * GH],
                                             squares[:, h % 2, :], start=(h == 0), stop=(h == GH - 1)).then_inc(summed, 1)
                        pe.wait_ge(ready, 1)
                        for h in range(GH):
                            if h >= 2:
                                pe.wait_ge(normed_ready, h - 1)
                            nc.tensor.matmul(psum[:, 1 + h % 2, :], identity[0:GH, h:h + 1].broadcast_to([GH, P]), factor[:],
                                             start=True, stop=True).then_inc(spread, 1)

                    @block.vector
                    def _(dve):
                        dve.wait_ge(summed, GH)
                        nc.vector.tensor_scalar(row[:], psum[0:GH, 0, :], 1.0 / P, EPS, ALU.mult, ALU.add).then_inc(mean, 1)
                        dve.wait_ge(root, 1)
                        nc.vector.reciprocal(factor[:], row[:]).then_inc(ready, 1)
                        for h in range(GH):
                            dve.wait_ge(spread, h + 1)
                            if h >= 2:
                                dve.wait_ge(gated_ready, h - 1)
                            nc.vector.scalar_tensor_tensor(out=normed[:, h % 2, :], in0=qkv[:, h, :], scalar=gain("gdn_out_norm_2"),
                                                           in1=psum[:, 1 + h % 2, :], op0=ALU.mult, op1=ALU.mult
                                                           ).then_inc(normed_ready, 1)
                            dve.wait_ge(normed_ready, h + 1)
                            if h >= 2:
                                dve.wait_ge(low_done, h - 1)
                            nc.vector.scalar_tensor_tensor(out=gated[:, h % 2, :], in0=normed[:, h % 2, :], scalar=0.5,
                                                           in1=z2[:, h, :], op0=ALU.mult, op1=ALU.mult).then_inc(gated_ready, 1)

                    @block.gpsimd
                    def _(pool):
                        for h in range(GH):
                            pool.wait_ge(high_ready, h + 1)
                            nc.gpsimd.tensor_tensor(out=split[:, 1, h, :], in0=gated[:, h % 2, :],
                                                    in1=split[:, 0, h, :].bitcast(f32), op=ALU.subtract).then_inc(low_done, 1)

        def fox_kv(split, keys, values, f_raw):
            start = weights.start["fox_kv"]
            tiles0 = weights.tiles_before[start]
            with stage("fox_kv") as s:
                key_bank_free, value_bank_free = s.sem("key_bank_free"), s.sem("value_bank_free")
                with nc.Block() as block:
                    @block.sync
                    def _(sp):
                        weights.load_for(sp, "fox_kv")

                    @block.gpsimd
                    def _(pool):
                        weights.split_low_all(pool, "fox_kv")

                    @block.scalar
                    def _(act):
                        for first in (0, 4):
                            with act.Fori(0, 2) as i:
                                for c in range(2):
                                    weights.split_high(act, Chunk(start + first + c + 1, i, 2))
                        weights.split_high(act, Chunk(start + 9))

                    @block.tensor
                    def _(pe):
                        with pe.Fori(0, 2) as i:
                            for c in range(2):
                                chunk = Chunk(start + c, i, 2)
                                pe.wait_ge(weights.low_ready, chunk.number + 1)
                                high, low = weights.parts(chunk, DT)
                                for j in (2 * c, 2 * c + 1):
                                    pe.wait_ge(key_bank_free, i * 4 + (j + 1))
                                    sl = slice((j % 2) * P, (j % 2 + 1) * P)
                                    for k in range(DT):
                                        last = product(psum[:, j, :], (high[:, k, sl], low[:, k, sl]),
                                                       (split[:, 0, k, :], split[:, 1, k, :]), k == 0, k == DT - 1)
                                    last.then_inc(weights.products, 1)
                        with pe.Fori(0, 2) as i:
                            for half in range(2):
                                chunk = Chunk(start + 4 + half, i, 2)
                                pe.wait_ge(weights.low_ready, chunk.number + 1)
                                parts = weights.parts(chunk, 4)
                                for j in range(TT):
                                    if half == 0:
                                        pe.wait_ge(value_bank_free, i * 4 + (j + 1))
                                    for k in range(4):
                                        a = 4 * half + k
                                        token = [split[:, n, a, j * P:(j + 1) * P] for n in range(2)]
                                        last = product(psum[:, 4 + j, :], token, [y[:, k, :] for y in parts], a == 0, a == DT - 1)
                                    last.then_inc(weights.products, 1)
                        pe.wait_ge(weights.low_ready, start + 9)
                        parts = weights.parts(Chunk(start + 8), DT)
                        at = 256 - FOX_HEADS - 64
                        for k in range(DT):
                            last = product(psum[0:64 + FOX_HEADS, 0, :], [y[:, k, at:at + 64 + FOX_HEADS] for y in parts],
                                           (split[:, 0, k, :], split[:, 1, k, :]), k == 0, k == DT - 1)
                        last.then_inc(weights.products, 1)

                    @block.vector
                    def _(dve):
                        dve.sem_inc(key_bank_free, 4)
                        dve.sem_inc(value_bank_free, 4)
                        with dve.Fori(0, 2) as i:
                            for j in range(4):
                                dve.wait_ge(weights.products, i * 4 + (tiles0 + j + 1))
                                nc.vector.tensor_copy(keys[:, ds(i * 4 + j, 1), :], psum[:, j:j + 1, :]).then_inc(key_bank_free, 1)
                        with dve.Fori(0, 2) as i:
                            for j in range(TT):
                                dve.wait_ge(weights.products, i * 8 + (tiles0 + 8 + 4 + j + 1))
                                nc.vector.tensor_copy(values[:, j, ds(i * T, T)], psum[:, 4 + j, :]).then_inc(value_bank_free, 1)
                        dve.wait_ge(weights.products, tiles0 + 8 + 16 + 1)
                        nc.vector.tensor_copy(f_raw[:], psum[64:64 + FOX_HEADS, 0, :])

        def fox_rows(f_raw, c_rows, c_cols):
            with stage("fox_rows") as s:
                bias = s.sbuf("bias", [FOX_HEADS, 1], f32)
                work = s.sbuf("work", [FOX_HEADS, 4, T], f32)
                y, size, e, one = [work[:, n, :] for n in range(4)]
                loaded, step, exp_ready, ln_ready, turned = [s.sem(n) for n in ("loaded", "step", "exp_ready", "ln_ready", "turned")]
                with nc.Block() as block:
                    @block.sync
                    def _(sp):
                        sp.dma_start(bias[:], w["b_forget_2"].rearrange("(h a) -> h a", a=1)).then_inc(loaded, 16)

                    @block.scalar
                    def _(act):
                        act.wait_ge(step, 2)
                        nc.scalar.activation(e, size, ACT.Exp, scale=-1.0).then_inc(exp_ready, 1)
                        act.wait_ge(step, 3)
                        nc.scalar.activation(e, e, ACT.Ln).then_inc(ln_ready, 1)

                    @block.tensor
                    def _(pe):
                        pe.wait_ge(step, 5)
                        for n in range(TT):
                            last = nc.tensor.transpose(psum[:, 0, n * FOX_HEADS:(n + 1) * FOX_HEADS], c_rows[:, n * P:(n + 1) * P],
                                                       identity[0:FOX_HEADS, 0:FOX_HEADS])
                        last.then_inc(turned, 1)

                    @block.vector
                    def _(dve):
                        nc.vector.memset(one, 1.0)
                        dve.wait_ge(loaded, 16)
                        nc.vector.tensor_scalar(y, f_raw[:], bias[:], None, ALU.add).then_inc(step, 1)
                        dve.wait_ge(step, 1)
                        nc.vector.scalar_tensor_tensor(out=size, in0=y, scalar=-1.0, in1=y, op0=ALU.mult, op1=ALU.max).then_inc(step, 1)
                        dve.wait_ge(exp_ready, 1)
                        nc.vector.tensor_scalar(e, e, 1.0, None, ALU.add).then_inc(step, 1)
                        dve.wait_ge(ln_ready, 1)
                        nc.vector.scalar_tensor_tensor(out=y, in0=y, scalar=0.0, in1=e, op0=ALU.min, op1=ALU.subtract).then_inc(step, 1)
                        dve.wait_ge(step, 4)
                        nc.vector.tensor_tensor_scan(c_rows[:], one, y, 0.0, ALU.mult, ALU.add).then_inc(step, 1)
                        dve.wait_ge(turned, 1)
                        nc.vector.tensor_copy(c_cols[:], psum[:, 0, 0:TT * FOX_HEADS].rearrange("p (n h) -> p n h", n=TT))


        def block_two():
            with ExitStack() as gdn:
                def keep(name, shape, dtype=f32):
                    return gdn.enter_context(nc.sbuf_tensor(name, shape, dtype))

                qkv = keep("gdn_qkv", [P, 3 * GH, T])
                z2 = keep("gdn_z2", [P, GH, T])
                rows = keep("gdn_rows_kept", [GH, 4, T])
                columns = keep("gdn_columns", [P, TT, 3, GH])
                with ExitStack() as early:
                    conv = early.enter_context(nc.sbuf_tensor("conv", [P, N_CONV], f32))
                    ba = early.enter_context(nc.sbuf_tensor("gdn_ba", [GH, 2, T], f32))
                    with stage("conv") as s:
                        conv_rows = s.sbuf("conv_rows", [N_CONV, P], f32)
                        loaded, turned = s.sem("loaded"), s.sem("turned")
                        with nc.Block() as block:
                            @block.sync
                            def _(sp):
                                sp.dma_start(conv_rows[:], w["gdn_conv_2"][0].rearrange("k (t p) -> (k t) p", p=P)).then_inc(loaded, 16)

                            @block.tensor
                            def _(pe):
                                pe.wait_ge(loaded, 16)
                                nc.tensor.transpose(psum[:, 0, 0:N_CONV], conv_rows[:], identity[0:N_CONV, 0:N_CONV]).then_inc(turned, 1)

                            @block.vector
                            def _(dve):
                                dve.wait_ge(turned, 1)
                                nc.vector.tensor_copy(conv[:], psum[:, 0, 0:N_CONV])
                    with nc.sbuf_tensor("gdn_split", [P, 2, DT, T], f32r) as split:
                        rms_normalize("norm_gdn", x, DT, lambda t: gain("pre_mix_norm_2", t), split=split)
                        gdn_in(split, qkv, z2, conv, ba)
                    gdn_rows(qkv, ba, rows, columns)
                gdn_chunks(qkv, rows, columns)
                with nc.sbuf_tensor("gdn_out_split", [P, 2, DT, T], f32r) as split, \
                        nc.sbuf_tensor("gdn_mix", [P, DT, T], f32) as mix:
                    gdn_post(qkv, z2, split)
                    linear("gdn_out", 2, split, finish_vector=copy_to(mix))
                    rms_normalize("norm_gdn_out", mix, DT, lambda t: gain("post_mix_norm_2", t), add_to=x)

            def feed_forward(layer):
                with nc.sbuf_tensor(f"ffn_split{layer}", [P, 2, DT, T], f32r) as split, \
                        nc.sbuf_tensor(f"ffn_total{layer}", [P, DT, T], f32) as total:
                    rms_normalize(f"norm_ffn{layer}", x, DT, lambda t: gain("pre_ffn_norm_2", layer * DT + t), split=split)
                    swiglu(f"ffn{layer}", split, total)
                    rms_normalize(f"norm_ffn_out{layer}", total, DT, lambda t: gain("post_ffn_norm_2", layer * DT + t), add_to=x)

            feed_forward(0)
            with ExitStack() as fox:
                def keep_fox(name, shape, dtype=f32):
                    return fox.enter_context(nc.sbuf_tensor(name, shape, dtype))

                split = keep_fox("fox_split", [P, 2, DT, T], f32r)
                keys = keep_fox("fox_keys", [P, DT, T])
                queries = keep_fox("fox_queries", [P, DT, T])
                values = keep_fox("fox_values", [P, TT, D])
                c_rows = keep_fox("fox_c_rows", [FOX_HEADS, T])
                c_cols = keep_fox("fox_c_cols", [P, TT, FOX_HEADS])
                with nc.sbuf_tensor("fox_f_raw", [FOX_HEADS, T], f32) as f_raw:
                    rms_normalize("norm_kv", x, DT, lambda t: gain("kv_norm_2", t), split=split)
                    fox_kv(split, keys, values, f_raw)
                    fox_rows(f_raw, c_rows, c_cols)
                rms_normalize("norm_fox", x, DT, lambda t: gain("pre_mix_norm_2", DT + t), split=split)
                linear("fox_q", 2, split, finish_vector=copy_to(queries, FOX_HD ** -0.5))
                attention("fox", FOX_HEADS // 2, split, 0, queries, keys, values, FOX_HD, FOX_HD, "forget",
                          decay=(c_rows, c_cols))
                linear("fox_out", 2, split, finish_vector=copy_to(queries))
                rms_normalize("norm_fox_out", queries, DT, lambda t: gain("post_mix_norm_2", DT + t), add_to=x)
            feed_forward(1)

        def write_out():
            with stage("write") as s:
                rows_out = s.sbuf("rows", [P, TT, D], f32)
                turned, copied, stored = s.sem("turned"), s.sem("copied"), s.sem("stored")
                with nc.Block() as block:
                    @block.tensor
                    def _(pe):
                        for n in range(2 * TT):
                            j, half = divmod(n, 2)
                            if n >= 4:
                                pe.wait_ge(copied, n - 3)
                            for t in range(4):
                                last = nc.tensor.transpose(psum[:, n % 4, t * P:(t + 1) * P],
                                                           x[:, half * 4 + t, j * P:(j + 1) * P], identity)
                            last.then_inc(turned, 1)

                    @block.vector
                    def _(dve):
                        for n in range(2 * TT):
                            j, half = divmod(n, 2)
                            dve.wait_ge(turned, n + 1)
                            nc.vector.tensor_copy(rows_out[:, j, half * T:(half + 1) * T], psum[:, n % 4, :]).then_inc(copied, 1)

                    @block.sync
                    def _(sp):
                        for j in range(TT):
                            sp.wait_ge(copied, 2 * j + 2)
                            sp.dma_start(out[0, j * P:(j + 1) * P, :], rows_out[:, j, :]).then_inc(stored, 16)
                        sp.wait_ge(stored, 16 * TT)

        ctx1 = ExitStack()
        with ctx1:
            block_one()
        block_two()
        write_out()


_OUT_SHAPE = (1, T, D)


def kernel(**inputs):
    import concourse.bacc as bacc
    from concourse import mybir
    from concourse.bass_utils import run_bass_kernel_spmd

    nc = bacc.Bacc("TRN2", target_bir_lowering=False, num_devices=1, dynamic_dma_scratch_size=1024)
    arrays, handles = {}, {}
    for name, value in inputs.items():
        a = np.ascontiguousarray(value)
        arrays[f"in_{name}"] = a
        handles[name] = nc.dram_tensor(f"in_{name}", a.shape, mybir.dt.from_np(a.dtype), kind="ExternalInput").ap()
    arrays["shape_constants"] = shape_constants()
    arrays["rope_tables"] = rope_tables()
    constants = nc.dram_tensor("shape_constants", (P, N_CONST), mybir.dt.float32, kind="ExternalInput").ap()
    tables = nc.dram_tensor("rope_tables", (4, P, T), mybir.dt.float32, kind="ExternalInput").ap()
    out = nc.dram_tensor("out", _OUT_SHAPE, mybir.dt.float32, kind="ExternalOutput").ap()
    build_program(nc, handles, constants, tables, out)
    result = run_bass_kernel_spmd(nc, [arrays], core_ids=[0])
    return result.results[0]["out"]
```

```python
import numpy as np

P = 128
T = 512
TT = T // P
D = 1024
DT = D // P
EPS = 1e-6
GRID_W = 64
ROPE_THETA = 10000.0

HEADS = 8
NOPE, ROPE, DV_A = 64, 32, 64
DQ_A = NOPE + ROPE
Q_LORA, KV_LORA = 256, 128
HD_B, KV_B = 64, 2
D_FF = 4 * D
COL_QLAT, COL_KV = 0, Q_LORA
COL_QB = COL_KV + KV_LORA + ROPE
COL_KB = COL_QB + HEADS * HD_B
COL_VB = COL_KB + KV_B * HD_B
COL_GATES = COL_VB + KV_B * HD_B

GH = 8
GDN_QKV = 3 * GH * P
FOX_HEADS, FOX_HD = 16, 64
D_FF2 = 2816
CHUNK = 2048
NEG = -1.0e30

GAIN_ROWS = [("g_mix", 8), ("g_qa", 2), ("g_kva", 1), ("g_mlp", 8), ("g_ple", 8), ("g_final", 8),
             ("pre_mix_norm_2", 16), ("post_mix_norm_2", 16), ("pre_ffn_norm_2", 16),
             ("post_ffn_norm_2", 16), ("kv_norm_2", 8), ("gdn_out_norm_2", 1)]
GAIN_AT = {}
_row = 0
for _name, _tiles in GAIN_ROWS:
    GAIN_AT[_name] = _row
    _row += _tiles
GAIN_AT["g_qn"] = _row
GAIN_AT["g_kn"] = _row + 1
N_GAINS = _row + 2
CONV_TAPS = 4
N_CONV = CONV_TAPS * 3 * GH

CONST_AT = {}
_col = 0
for _name, _n in [("identity", P), ("rotate", P), ("heads_of_pair", 2), ("ones", 1), ("causal_bias", P),
                  ("head_select", GH * GH), ("earlier", P), ("level", 7 * P)]:
    CONST_AT[_name] = (_col, _n)
    _col += _n
N_CONST = _col
N_SMALL_CONST = CONST_AT["earlier"][0]


def shape_constants():
    c = np.zeros((P, N_CONST), np.float32)

    def put(name, value):
        at, n = CONST_AT[name]
        c[:, at:at + n] = value

    row, col = np.arange(P)[:, None], np.arange(P)[None, :]
    put("identity", row == col)
    half = ROPE // 2
    first = (col % ROPE) < half
    put("rotate", np.where(first & (row == col + half), -1.0, 0.0) + np.where(~first & (row == col - half), 1.0, 0.0))
    put("heads_of_pair", (row // HD_B) == np.arange(2)[None, :])
    put("ones", 1.0)
    put("head_select", np.eye(GH).reshape(1, GH * GH))
    put("causal_bias", np.where(col > row, NEG, 0.0))
    put("earlier", row <= col)
    levels = [((row // (2 * b)) == (col // (2 * b))) & ((row // b) % 2 == 0) & ((col // b) % 2 == 1)
              for b in (1, 2, 4, 8, 16, 32, 64)]
    put("level", np.concatenate(levels, axis=1))
    return c


def rope_tables():
    t = np.arange(T)
    out = np.zeros((4, P, T), np.float32)
    inv = (ROPE_THETA ** (-np.arange(0, ROPE, 2, dtype=np.float32) / np.float32(ROPE))).astype(np.float32)
    ang = (t.astype(np.float32)[None, :] * inv[:, None]).astype(np.float32)
    out[0, :, :] = 1.0
    for half in range(2):
        at = NOPE + half * (ROPE // 2)
        out[0, at:at + ROPE // 2] = np.cos(ang)
        out[1, at:at + ROPE // 2] = np.sin(ang)
    row_ang = ((t // GRID_W).astype(np.float32)[None, :] * inv[:, None]).astype(np.float32)
    col_ang = ((t % GRID_W).astype(np.float32)[None, :] * inv[:, None]).astype(np.float32)
    for group in range(P // 16):
        a = row_ang if (group // 2) % 2 == 0 else col_ang
        out[2, group * 16:(group + 1) * 16] = np.cos(a)
        out[3, group * 16:(group + 1) * 16] = np.sin(a)
    return out


class Chunk:

    def __init__(self, first, i=0, per_turn=0):
        assert per_turn % 2 == 0
        self.slot = first % 2
        self.number = first + i * per_turn if per_turn else first
        self.uses = first // 2 + 1 + i * (per_turn // 2) if per_turn else first // 2 + 1
        self.first, self.i, self.per_turn = first, i, per_turn


class Stage:

    def __init__(self, nc, label):
        from contextlib import ExitStack
        self.nc, self.label, self.stack, self.sems = nc, label, ExitStack(), []

    def sem(self, name):
        s = self.stack.enter_context(self.nc.semaphore(f"{self.label}_{name}"))
        self.sems.append(s)
        return s

    def sbuf(self, name, shape, dtype):
        return self.stack.enter_context(self.nc.sbuf_tensor(f"{self.label}_{name}", shape, dtype))

    def __enter__(self):
        self.stack.__enter__()
        return self

    def __exit__(self, *exc):
        if exc[0] is None:
            numbers = sorted(s.num for s in self.sems)
            at = 0
            while at < len(numbers):
                end = at
                while end + 1 < len(numbers) and numbers[end + 1] == numbers[end] + 1:
                    end += 1
                self.nc.all_engine_barrier(sems_to_clear=range(numbers[at], numbers[end] + 1))
                at = end + 1
        return self.stack.__exit__(*exc)


class Weights:

    def __init__(self, nc, enter, plan):
        from concourse import mybir
        self.nc, self.plan = nc, plan
        f32, f32r = mybir.dt.float32, mybir.dt.float32r
        self.f32, self.sub = f32, mybir.AluOpType.subtract
        self.raw = enter(nc.sbuf_tensor("weights_raw", [P, 2, CHUNK], f32))
        self.high = enter(nc.sbuf_tensor("weights_high", [P, 2, CHUNK], f32r))
        self.low = enter(nc.sbuf_tensor("weights_low", [P, 2, CHUNK], f32r))
        self.loaded = [enter(nc.semaphore(f"weights_loaded_{s}")) for s in range(2)]
        self.high_ready = enter(nc.semaphore("weights_high_ready"))
        self.low_ready = enter(nc.semaphore("weights_low_ready"))
        self.products = enter(nc.semaphore("products_done"))
        self.start = {}
        n = 0
        for name, segments in plan:
            self.start[name] = n
            n += sum(turns * len(items) for turns, items in segments)
        self.total = n
        self.width, self.tiles_before, tiles, self.turn = [], [0], 0, []
        for _, segments in plan:
            for turns, items in segments:
                for i in range(turns):
                    for kt, cols, _, count in items:
                        self.width.append(kt * cols)
                        tiles += count
                        self.tiles_before.append(tiles)

    def load(self, sp, chunk, item, i):
        kt, cols, source, _ = item
        if chunk.first >= 2:
            sp.wait_ge(self.low_ready, chunk.number - 1)
        sp.dma_start(self.raw[:, chunk.slot, 0:kt * cols].rearrange("p (k c) -> p k c", k=kt),
                     source(i)).then_inc(self.loaded[chunk.slot], 16)

    def load_segments(self, sp, first, segments):
        for turns, items in segments:
            if turns == 1:
                for item in items:
                    self.load(sp, Chunk(first), item, 0)
                    first += 1
            else:
                with sp.Fori(0, turns) as i:
                    for pos, item in enumerate(items):
                        self.load(sp, Chunk(first + pos, i, len(items)), item, i)
                first += turns * len(items)

    @staticmethod
    def shifted(items, by):
        def later(source):
            return lambda i: source(i + by)
        return [(kt, cols, later(source), count) for kt, cols, source, count in items]

    def after_two(self, segments):
        rest, head, need = [], [], 2
        for turns, items in segments:
            if need == 0:
                rest.append((turns, items))
                continue
            skipped = 0
            while need and skipped < turns:
                turn = self.shifted(items, skipped)
                take = min(need, len(items))
                head += turn[:take]
                need -= take
                skipped += 1
                if take < len(items):
                    rest.append((1, turn[take:]))
            if skipped < turns:
                rest.append((turns - skipped, self.shifted(items, skipped)))
        return head, rest

    def load_for(self, sp, name):
        names = [n for n, _ in self.plan]
        at = names.index(name)
        _, rest = self.after_two(self.plan[at][1])
        self.load_segments(sp, self.start[name] + 2, rest)
        if at + 1 < len(names):
            head, _ = self.after_two(self.plan[at + 1][1])
            self.load_segments(sp, self.start[names[at + 1]], [(1, head)])

    def plan_item(self, name, n):
        for turns, items in dict(self.plan)[name]:
            if n < turns * len(items):
                return self.shifted(items, n // len(items))[n % len(items)]
            n -= turns * len(items)

    def split_high(self, act, chunk):
        if chunk.first >= self.total:
            return
        width = self.width[chunk.first]
        act.wait_ge(self.loaded[chunk.slot], 16 * chunk.uses)
        if chunk.first >= 2:
            act.wait_ge(self.products, self.tiles_at(chunk, -1))
        self.nc.scalar.copy(self.high[:, chunk.slot, 0:width],
                            self.raw[:, chunk.slot, 0:width]).then_inc(self.high_ready, 1)

    def tiles_at(self, chunk, by=0):
        at = self.tiles_before[chunk.first + by]
        if chunk.per_turn:
            step = chunk.per_turn
            slope = self.tiles_before[chunk.first + by + step] - at
            return chunk.i * slope + at
        return at

    def split_low(self, pool, chunk):
        if chunk.first >= self.total:
            return
        width = self.width[chunk.first]
        pool.wait_ge(self.high_ready, chunk.number + 1)
        self.nc.gpsimd.tensor_tensor(out=self.low[:, chunk.slot, 0:width],
                                     in0=self.raw[:, chunk.slot, 0:width],
                                     in1=self.high[:, chunk.slot, 0:width].bitcast(self.f32),
                                     op=self.sub).then_inc(self.low_ready, 1)

    def split_low_all(self, pool, name):
        first = self.start[name] + 1
        for turns, items in dict(self.plan)[name]:
            if turns == 1:
                for pos in range(len(items)):
                    self.split_low(pool, Chunk(first + pos))
            else:
                with pool.Fori(0, turns) as i:
                    for pos in range(len(items)):
                        self.split_low(pool, Chunk(first + pos, i, len(items)))
            first += turns * len(items)

    def parts(self, chunk, kt):
        width = self.width[chunk.first]
        return [x[:, chunk.slot, 0:width].rearrange("p (k c) -> p k c", k=kt) for x in (self.high, self.low)]


def weight_plan(w):
    import concourse.bass as bass

    def cols(matrix, kt, n, at, tiles=2):
        view = matrix.rearrange("(k p) c -> p k c", p=P)
        return (kt, n, lambda i: view[:, :, bass.ds(at(i), n)], tiles)

    def rows(matrix, at):
        view = matrix.rearrange("(k p) c -> p k c", p=P)
        return (2, D, lambda i: view[:, bass.ds(at(i), 2), :], DT)

    def halves(matrix, n, at, half):
        view = matrix.rearrange("(k p) c -> p k c", p=P)
        return (4, n, lambda i: view[:, 4 * half:4 * half + 4, bass.ds(at(i), n)], TT)

    def pairs(matrix, turns, start=0):
        return (turns, [cols(matrix, DT, 256, lambda i: i * 512 + start),
                        cols(matrix, DT, 256, lambda i: i * 512 + (start + 256))])

    def once(*items):
        return (1, list(items))

    w_in, qb, kvb = w["w_in"][0], w["w_qb"][0], w["w_kvb"][0]
    up, down = w["w_up"][0], w["w_down"][0]

    def u1(t0, step):
        return cols(up, DT, 256, lambda i: i * (256 * step) + 256 * t0)

    def d1(t0, step):
        return rows(down, lambda i: i * (2 * step) + 2 * t0)

    def swiglu(layer):
        inner, outer = w["w_ffn_in_2"][layer], w["w_ffn_out_2"][layer]

        def g(t0, step):
            return cols(inner, DT, 256, lambda i: i * (256 * step) + 256 * t0)

        def u(t0, step):
            return cols(inner, DT, 256, lambda i: i * (256 * step) + (256 * t0 + D_FF2))

        def d(t0, step):
            return rows(outer, lambda i: i * (2 * step) + 2 * t0)

        return [once(g(0, 0), u(0, 0)), (5, [g(1, 2), u(1, 2), d(0, 2), g(2, 2), u(2, 2), d(1, 2)]), once(d(10, 0))]

    gdn, kv = w["gdn_w_in_2"][0], w["w_kv_2"]
    return [
        ("mixer_in", [pairs(w_in, 4, COL_GATES),
                      once(cols(w_in, DT, 256, lambda i: COL_QLAT),
                           cols(w_in, DT, 256, lambda i: COL_QB), cols(w_in, DT, 256, lambda i: COL_QB + 256),
                           cols(w_in, DT, 256, lambda i: COL_KB),
                           cols(w_in, DT, 256, lambda i: COL_KV))]),
        ("latent_up", [once(cols(qb, 2, HEADS * DQ_A, lambda i: 0, HEADS), cols(kvb, 1, D, lambda i: 0, HEADS + TT))]),
        ("merge", [(2, [cols(w["w_oa"][0], 4, 512, lambda i: i * 512, 4),
                        cols(w["w_ob"][0], 4, 512, lambda i: i * 512, 4)])]),
        ("mixer_out", [pairs(w["w_o"][0], 2)]),
        ("mlp", [once(u1(0, 0), u1(1, 0), d1(0, 0)), (7, [u1(2, 2), d1(1, 2), u1(3, 2), d1(2, 2)]), once(d1(15, 0))]),
        ("ple", [once(cols(w["w_ple"][0], 2, D, lambda i: 0, DT)), pairs(w["w_ple_gate"][0], 2)]),
        ("gdn_in", [pairs(gdn, 6), pairs(gdn, 2, GDN_QKV), once(cols(gdn, DT, 256, lambda i: GDN_QKV + D + 2 * GH - 256))]),
        ("gdn_out", [pairs(w["gdn_w_out_2"][0], 2)]),
        ("ffn0", swiglu(0)),
        ("fox_kv", [pairs(kv, 2),
                    (2, [halves(kv, 512, lambda i: i * 512 + D, 0), halves(kv, 512, lambda i: i * 512 + D, 1)]),
                    once(cols(kv, DT, 256, lambda i: 2 * D + FOX_HEADS - 256, 1))]),
        ("fox_q", [pairs(w["fox_w_q_2"][0], 2)]),
        ("fox_out", [pairs(w["fox_w_o_2"][0], 2)]),
        ("ffn1", swiglu(1)),
    ]


def build_program(nc, w, constants, tables, out):
    import concourse.bass as bass
    from concourse import mybir
    from contextlib import ExitStack

    f32, f32r = mybir.dt.float32, mybir.dt.float32r
    ALU, ACT, AX = mybir.AluOpType, mybir.ActivationFunctionType, mybir.AxisListType
    ds = bass.ds
    ctx = ExitStack()
    enter = ctx.enter_context


    def stage(label):
        return Stage(nc, label)


    with ctx:
        weights = Weights(nc, enter, weight_plan(w))
        const = enter(nc.sbuf_tensor("const", [P, N_SMALL_CONST], f32))
        gains = enter(nc.sbuf_tensor("gains", [P, N_GAINS], f32))
        x = enter(nc.sbuf_tensor("x_stream", [P, DT, T], f32))
        square_sum = enter(nc.sbuf_tensor("square_sum", [P, T], f32))
        psum = enter(nc.psum_tensor("psum", [P, 8, T], f32))

        def constant(name):
            at, n = CONST_AT[name]
            return const[:, at:at + n]

        identity, rotate, ones = constant("identity"), constant("rotate"), constant("ones")

        def gain(name, tile=0):
            at = GAIN_AT[name] + tile
            return gains[:, at:at + 1]

        def product(bank, w_parts, a_parts, first, last):
            (wh, wl), (ah, al) = w_parts, a_parts
            nc.tensor.matmul(bank, wh, ah, start=first, stop=False)
            nc.tensor.matmul(bank, wh, al, start=False, stop=False)
            return nc.tensor.matmul(bank, wl, ah, start=False, stop=last)

        with stage("init") as s:
            rows_in = s.sbuf("gain_rows", [P, P], f32)
            x_rows = s.sbuf("x_rows", [P, TT, D], f32)
            loaded, gains_in, x_in = s.sem("const_loaded"), s.sem("gains_loaded"), s.sem("x_loaded")
            zeroed, turned, copied = s.sem("gain_rows_zeroed"), s.sem("turned"), s.sem("copied")
            with nc.Block() as block:
                @block.sync
                def _(sp):
                    sp.dma_start(const[:], constants[:, 0:N_SMALL_CONST]).then_inc(loaded, 16)
                    for j in range(TT):
                        sp.dma_start(x_rows[:, j, :], w["x"][0, j * P:(j + 1) * P, :]).then_inc(x_in, 16)
                    head, _ = weights.after_two(weights.plan[0][1])
                    weights.load_segments(sp, 0, [(1, head)])

                @block.scalar
                def _(act):
                    act.wait_ge(zeroed, 1)
                    for name, tiles in GAIN_ROWS:
                        at = GAIN_AT[name]
                        g = w[name]
                        if len(g.shape) == 2:
                            g = g.rearrange("l (t p) -> (l t) p", p=P)
                        else:
                            g = g.rearrange("(t p) -> t p", p=P)
                        act.dma_start(rows_in[at:at + tiles, :], g).then_inc(gains_in, 16)
                    for name in ("g_qn", "g_kn"):
                        at = GAIN_AT[name]
                        for half in range(2):
                            act.dma_start(rows_in[at:at + 1, half * HD_B:(half + 1) * HD_B],
                                          w[name]).then_inc(gains_in, 16)
                    weights.split_high(act, Chunk(0))

                @block.gpsimd
                def _(pool):
                    nc.gpsimd.memset(rows_in[:], 0.0).then_inc(zeroed, 1)
                    weights.split_low(pool, Chunk(0))

                @block.tensor
                def _(pe):
                    pe.wait_ge(loaded, 16)
                    pe.wait_ge(x_in, 16 * TT)
                    for t in range(DT):
                        if t >= 4:
                            pe.wait_ge(copied, t - 3)
                        for j in range(TT):
                            last = nc.tensor.transpose(psum[:, t % 4, j * P:(j + 1) * P],
                                                       x_rows[:, j, t * P:(t + 1) * P], identity)
                        last.then_inc(turned, 1)
                    pe.wait_ge(gains_in, 16 * (len(GAIN_ROWS) + 4))
                    nc.tensor.transpose(psum[:, 4, 0:P], rows_in[:], identity).then_inc(turned, 1)

                @block.vector
                def _(dve):
                    for t in range(DT):
                        dve.wait_ge(turned, t + 1)
                        nc.vector.tensor_copy(x[:, t, :], psum[:, t % 4, :]).then_inc(copied, 1)
                    dve.wait_ge(turned, DT + 1)
                    nc.vector.tensor_copy(gains[:], psum[:, 4, 0:N_GAINS])

        class Norm:

            def __init__(self, s, source, tiles, gain_at, split=None, plain=None, add_to=None, given=False,
                         sum_next=False):
                self.source, self.tiles, self.gain_at, self.split = source, tiles, gain_at, split
                self.plain, self.add_to, self.given, self.sum_next = plain, add_to, given, sum_next
                self.squares = s.sbuf("norm_squares", [P, 2, T], f32)
                if plain is None:
                    self.ring = s.sbuf("norm_ring", [P, 4, T], f32)
                self.stat = s.sbuf("norm_stat", [P, 3, TT], f32)
                (self.squared, self.accumulated, self.summed, self.mean, self.root, self.rstd, self.spread,
                 self.scaled, self.high_done, self.low_even, self.low_odd, self.added) = [s.sem("norm_" + n) for n in (
                    "squared", "accumulated", "summed", "mean", "root", "rstd", "spread", "scaled", "high_done",
                    "low_even", "low_odd", "added")]
                self.before = 0 if given else tiles

            def wait_tile(self, pe, t):
                pe.wait_ge((self.low_even, self.low_odd)[t % 2], t // 2 + 1)

            def square(self, act, n, source, t):
                if t == 0 or n < 2:
                    target = square_sum[:] if t == 0 else self.squares[:, t % 2, :]
                else:
                    target = self.squares[:, t % 2, :]
                    act.wait_ge(self.accumulated, n - 1)
                nc.scalar.activation(target, source[:, t, :], ACT.Square).then_inc(self.squared, 1)

            def accumulate(self, dve, n, t):
                dve.wait_ge(self.squared, n + 1)
                if n >= 1:
                    dve.wait_ge(self.accumulated, n)
                if t == 0:
                    dve.sem_inc(self.accumulated, 1)
                else:
                    nc.vector.tensor_tensor(out=square_sum[:], in0=square_sum[:], in1=self.squares[:, t % 2, :],
                                            op=ALU.add).then_inc(self.accumulated, 1)

            def scalar(self, act):
                if not self.given:
                    for t in range(self.tiles):
                        self.square(act, t, self.source, t)
                act.wait_ge(self.mean, 1)
                nc.scalar.activation(self.stat[:, 1, :], self.stat[:, 0, :], ACT.Sqrt).then_inc(self.root, 1)
                if self.split is not None:
                    for t in range(self.tiles):
                        act.wait_ge(self.scaled, t + 1)
                        nc.scalar.copy(self.split[:, 0, t, :], self.ring[:, t % 4, :]).then_inc(self.high_done, 1)
                if self.sum_next:
                    for t in range(self.tiles):
                        result, ready = (self.plain, self.scaled) if self.add_to is None else (self.add_to, self.added)
                        act.wait_ge(ready, t + 1)
                        self.square(act, self.before + t, result, t)

            def tensor(self, pe):
                if not self.given:
                    pe.wait_ge(self.accumulated, self.tiles)
                for j in range(TT):
                    last = nc.tensor.matmul(psum[:, 6, j:j + 1], square_sum[:, j * P:(j + 1) * P], ones,
                                            start=True, stop=True)
                last.then_inc(self.summed, 1)
                pe.wait_ge(self.rstd, 1)
                for j in range(TT):
                    last = nc.tensor.matmul(psum[:, 7, j * P:(j + 1) * P],
                                            self.stat[:, 2, j:j + 1].broadcast_to([P, P]), identity,
                                            start=True, stop=True)
                last.then_inc(self.spread, 1)

            def vector(self, dve):
                tiles = self.tiles
                if not self.given:
                    for t in range(tiles):
                        self.accumulate(dve, t, t)
                dve.wait_ge(self.summed, 1)
                nc.vector.tensor_scalar(self.stat[:, 0, :], psum[:, 6, 0:TT], 1.0 / (tiles * P), EPS,
                                        ALU.mult, ALU.add).then_inc(self.mean, 1)
                dve.wait_ge(self.root, 1)
                nc.vector.reciprocal(self.stat[:, 2, :], self.stat[:, 1, :]).then_inc(self.rstd, 1)
                dve.wait_ge(self.spread, 1)
                for t in range(tiles + 2):
                    if t < tiles:
                        if self.plain is None and t >= 4:
                            if self.split is None:
                                dve.wait_ge(self.added, t - 3)
                            else:
                                self.wait_tile(dve, t - 4)
                        target = self.plain[:, t, :] if self.plain is not None else self.ring[:, t % 4, :]
                        nc.vector.scalar_tensor_tensor(out=target, in0=self.source[:, t, :], scalar=self.gain_at(t),
                                                       in1=psum[:, 7, :], op0=ALU.mult,
                                                       op1=ALU.mult).then_inc(self.scaled, 1)
                    if self.split is not None and t % 2 == 0 and 1 <= t - 1 < tiles:
                        dve.wait_ge(self.high_done, t)
                        nc.vector.tensor_tensor(out=self.split[:, 1, t - 1, :], in0=self.ring[:, (t - 1) % 4, :],
                                                in1=self.split[:, 0, t - 1, :].bitcast(f32),
                                                op=ALU.subtract).then_inc(self.low_odd, 1)
                    if self.sum_next and t >= 2:
                        self.accumulate(dve, self.before + t - 2, t - 2)

            def gpsimd(self, pool):
                if self.split is not None:
                    for t in range(0, self.tiles, 2):
                        pool.wait_ge(self.high_done, t + 1)
                        nc.gpsimd.tensor_tensor(out=self.split[:, 1, t, :], in0=self.ring[:, t % 4, :],
                                                in1=self.split[:, 0, t, :].bitcast(f32),
                                                op=ALU.subtract).then_inc(self.low_even, 1)
                if self.add_to is not None:
                    for t in range(self.tiles):
                        pool.wait_ge(self.scaled, t + 1)
                        nc.gpsimd.tensor_tensor(out=self.add_to[:, t, :], in0=self.add_to[:, t, :],
                                                in1=self.ring[:, t % 4, :], op=ALU.add).then_inc(self.added, 1)

        def norm_of(*what, **how):
            return lambda s: Norm(s, *what, **how)

        def rms_normalize(label, *what, **how):
            with stage(label) as s:
                norm = Norm(s, *what, **how)
                with nc.Block() as block:
                    block.scalar(norm.scalar)
                    block.tensor(norm.tensor)
                    block.vector(norm.vector)
                    block.gpsimd(norm.gpsimd)

        def linear(label, turns, act_in, finish_scalar=None, finish_vector=None, norm=None):
            start = weights.start[label]
            tiles0 = weights.tiles_before[start]
            with stage(label) as s:
                norm = norm and norm(s)
                scalar_done, bank_free = s.sem("scalar_done"), s.sem("bank_free")
                both = finish_scalar is not None and finish_vector is not None
                handed = s.sbuf("handed", [P, 2, T], f32) if both else None
                with nc.Block() as block:
                    @block.sync
                    def _(sp):
                        weights.load_for(sp, label)

                    @block.gpsimd
                    def _(pool):
                        if norm is not None:
                            norm.gpsimd(pool)
                        weights.split_low_all(pool, label)

                    @block.tensor
                    def _(pe):
                        if norm is not None:
                            norm.tensor(pe)
                        with pe.Fori(0, turns) as i:
                            for c in range(2):
                                chunk = Chunk(start + c, i, 2)
                                pe.wait_ge(weights.low_ready, chunk.number + 1)
                                high, low = weights.parts(chunk, DT)
                                for j in (2 * c, 2 * c + 1):
                                    pe.wait_ge(bank_free, i * 4 + (j + 1))
                                    sl = slice((j % 2) * P, (j % 2 + 1) * P)
                                    for k in range(DT):
                                        if j == 0 and norm is not None:
                                            norm.wait_tile(pe, k)
                                        last = product(psum[:, j, :], (high[:, k, sl], low[:, k, sl]),
                                                       (act_in[:, 0, k, :], act_in[:, 1, k, :]), k == 0, k == DT - 1)
                                    last.then_inc(weights.products, 1)

                    @block.scalar
                    def _(act):
                        if norm is not None:
                            norm.scalar(act)
                        with act.Fori(0, turns) as i:
                            for c in range(2):
                                weights.split_high(act, Chunk(start + c + 1, i, 2))
                                for j in (2 * c, 2 * c + 1) if finish_scalar else ():
                                    act.wait_ge(weights.products, i * 4 + (tiles0 + j + 1))
                                    if both:
                                        act.wait_ge(bank_free, i * 4 + (j + 3))
                                        finish_scalar(j, handed[:, j % 2, :], i * 4 + j).then_inc(scalar_done, 1)
                                    else:
                                        finish_scalar(j, None, i * 4 + j).then_inc(bank_free, 1)

                    @block.vector
                    def _(dve):
                        if norm is not None:
                            norm.vector(dve)
                        dve.sem_inc(bank_free, 4)
                        if finish_vector is not None:
                            with dve.Fori(0, turns) as i:
                                for j in range(4):
                                    if both:
                                        dve.wait_ge(scalar_done, i * 4 + (j + 1))
                                    else:
                                        dve.wait_ge(weights.products, i * 4 + (tiles0 + j + 1))
                                    finish_vector(j, handed[:, j % 2, :] if both else None,
                                                  i * 4 + j).then_inc(bank_free, 1)

        def block_one():
            gates = ctx1.enter_context(nc.sbuf_tensor("gates", [P, 2 * DT, T], f32))
            split = ctx1.enter_context(nc.sbuf_tensor("block1_split", [P, 2, DT, T], f32r))
            attn = ExitStack()
            with attn:
                def keep(name, shape, dtype=f32):
                    return attn.enter_context(nc.sbuf_tensor(name, shape, dtype))

                q_a = keep("q_a", [P, HEADS, T])
                k_a = keep("k_a", [P, HEADS, T])
                v_a = keep("v_a", [P, TT, HEADS * DV_A])
                qk_b = keep("qk_b", [P, 6, T])
                v_b = keep("v_b", [P, TT, KV_B * HD_B])
                until_rope = ExitStack()
                k_pe = until_rope.enter_context(nc.sbuf_tensor("k_pe", [P, T], f32))

                with ExitStack() as latents:
                    q_lat = latents.enter_context(nc.sbuf_tensor("q_lat", [P, 2, T], f32))
                    kv_lat = latents.enter_context(nc.sbuf_tensor("kv_lat", [P, 1, T], f32))
                    mixer_in(norm_of(x, DT, lambda t: gain("g_mix", t), split=split), split, gates, q_lat, kv_lat, qk_b, v_b, k_pe)
                    q_split, kv_split = split[:, :, 0:2, :], split[:, :, 2:3, :]
                    rms_normalize("norm_qa", q_lat, 2, lambda t: gain("g_qa", t), split=q_split)
                    rms_normalize("norm_kva", kv_lat, 1, lambda t: gain("g_kva"), split=kv_split)
                    latent_up(q_split, kv_split, q_a, k_a, v_a)
                rope_and_norms(q_a, k_a, k_pe, qk_b)
                until_rope.close()
                attention("attn_a", HEADS // 2, split, 0, q_a, k_a, v_a, DQ_A, DV_A, "latent")
                attention("attn_b", HEADS // 2, split, HEADS // 2, qk_b, qk_b, v_b, HD_B, HD_B, "grouped")
            with nc.sbuf_tensor("merged", [P, 2, DT, T], f32r) as merged:
                merge(split, gates, merged)

                def add_to_x(bank, _, tile):
                    return nc.vector.tensor_tensor(out=x[:, ds(tile, 1), :], in0=psum[:, bank:bank + 1, :],
                                                   in1=x[:, ds(tile, 1), :], op=ALU.add)

                linear("mixer_out", 2, merged, finish_vector=add_to_x)
            mlp(norm_of(x, DT, lambda t: gain("g_mlp", t), split=split), split)
            ple(norm_of(x, DT, lambda t: gain("g_ple", t), split=split), split, gates)
            rms_normalize("norm_final", x, DT, lambda t: gain("g_final", t), plain=x, sum_next=True)

        def mixer_in(norm, split, gates, q_lat, kv_lat, qk_b, v_b, k_pe):
            start = weights.start["mixer_in"]
            last_gate = 2 * DT
            with stage("mixer_in") as s:
                norm = norm(s)
                gate_bank_free, bank_free = s.sem("gate_bank_free"), s.sem("bank_free")
                lower, upper = slice(0, HD_B), slice(HD_B, P)
                whole = slice(0, P)
                targets = [[(q_lat[:, n, :], whole)] for n in range(2)] + [[(qk_b[:, n, :], whole)] for n in range(4)]
                targets += [[(qk_b[half, 4 + g, :], (lower, upper)[g]) for g in range(KV_B) for half in (lower, upper)],
                            [(v_b[:], whole)], [(kv_lat[:, 0, :], whole)], [(k_pe[:], whole)]]
                with nc.Block() as block:
                    @block.sync
                    def _(sp):
                        weights.load_for(sp, "mixer_in")

                    @block.gpsimd
                    def _(pool):
                        norm.gpsimd(pool)
                        weights.split_low_all(pool, "mixer_in")

                    @block.tensor
                    def _(pe):
                        norm.tensor(pe)
                        with pe.Fori(0, 4) as i:
                            for c in range(2):
                                chunk = Chunk(start + c, i, 2)
                                pe.wait_ge(weights.low_ready, chunk.number + 1)
                                high, low = weights.parts(chunk, DT)
                                for j in (2 * c, 2 * c + 1):
                                    pe.wait_ge(gate_bank_free, i * 4 + (j + 1))
                                    sl = slice((j % 2) * P, (j % 2 + 1) * P)
                                    for k in range(DT):
                                        if j == 0:
                                            norm.wait_tile(pe, k)
                                        last = product(psum[:, j, :], (high[:, k, sl], low[:, k, sl]),
                                                       (split[:, 0, k, :], split[:, 1, k, :]), k == 0, k == DT - 1)
                                    last.then_inc(weights.products, 1)
                        tile = 0

                        def feature_tile(parts, stationary):
                            nonlocal tile
                            if tile >= 4:
                                pe.wait_ge(bank_free, tile - 3)
                            for k in range(DT):
                                last = product(psum[:, 4 + tile % 4, :], [stationary(x, k) for x in parts],
                                               (split[:, 0, k, :], split[:, 1, k, :]), k == 0, k == DT - 1)
                            last.then_inc(weights.products, 1)
                            tile += 1

                        for c in range(3):
                            pe.wait_ge(weights.low_ready, start + 8 + c + 1)
                            parts = weights.parts(Chunk(start + 8 + c), DT)
                            for m in range(2):
                                feature_tile(parts, lambda x, k: x[:, k, m * P:(m + 1) * P])
                        pe.wait_ge(weights.low_ready, start + 12)
                        parts = weights.parts(Chunk(start + 11), DT)
                        feature_tile(parts, lambda x, k: x[:, k, 0:P])
                        pe.wait_ge(bank_free, tile - 3)
                        for j in range(TT):
                            for k in range(DT):
                                token = [split[:, n, k, j * P:(j + 1) * P] for n in range(2)]
                                last = product(psum[:, 4 + tile % 4, j * P:(j + 1) * P], token,
                                               [x[:, k, P:2 * P] for x in parts], k == 0, k == DT - 1)
                        last.then_inc(weights.products, 1)
                        tile += 1
                        pe.wait_ge(weights.low_ready, start + 13)
                        parts = weights.parts(Chunk(start + 12), DT)
                        feature_tile(parts, lambda x, k: x[:, k, 0:KV_LORA])
                        feature_tile(parts, lambda x, k: x[:, k, KV_LORA - NOPE:KV_LORA - NOPE + P])

                    @block.scalar
                    def _(act):
                        norm.scalar(act)
                        act.sem_inc(gate_bank_free, 4)
                        with act.Fori(0, 4) as i:
                            for c in range(2):
                                weights.split_high(act, Chunk(start + c + 1, i, 2))
                                for j in (2 * c, 2 * c + 1):
                                    act.wait_ge(weights.products, i * 4 + (j + 1))
                                    nc.scalar.activation(gates[:, ds(i * 4 + j, 1), :], psum[:, j:j + 1, :], ACT.Tanh,
                                                         scale=0.5).then_inc(gate_bank_free, 1)
                        for c in range(5):
                            weights.split_high(act, Chunk(start + 9 + c))

                    @block.vector
                    def _(dve):
                        norm.vector(dve)
                        for n, target in enumerate(targets):
                            dve.wait_ge(weights.products, last_gate + n + 1)
                            for to, rows in target:
                                source = psum[rows, 4 + n % 4, :]
                                if n == 7:
                                    source = source.rearrange("p (j c) -> p j c", j=TT)
                                last = nc.vector.tensor_copy(to, source)
                            last.then_inc(bank_free, 1)

        def latent_up(q_split, kv_split, q_a, k_a, v_a):
            start = weights.start["latent_up"]
            tiles0 = weights.tiles_before[start]
            with stage("latent_up") as s:
                bank_free = s.sem("bank_free")
                with nc.Block() as block:
                    @block.sync
                    def _(sp):
                        weights.load_for(sp, "latent_up")

                    @block.gpsimd
                    def _(pool):
                        weights.split_low_all(pool, "latent_up")

                    @block.scalar
                    def _(act):
                        for c in range(2):
                            weights.split_high(act, Chunk(start + c + 1))

                    @block.tensor
                    def _(pe):
                        tile = 0
                        pe.wait_ge(weights.low_ready, start + 1)
                        parts = weights.parts(Chunk(start), 2)
                        for h in range(HEADS):
                            if tile >= 4:
                                pe.wait_ge(bank_free, tile - 3)
                            for k in range(2):
                                last = product(psum[0:DQ_A, tile % 4, :],
                                               [y[:, k, h * DQ_A:(h + 1) * DQ_A] for y in parts],
                                               (q_split[:, 0, k, :], q_split[:, 1, k, :]), k == 0, k == 1)
                            last.then_inc(weights.products, 1)
                            tile += 1
                        pe.wait_ge(weights.low_ready, start + 2)
                        parts = weights.parts(Chunk(start + 1), 1)
                        latent = (kv_split[:, 0, 0, :], kv_split[:, 1, 0, :])
                        for h in range(HEADS):
                            pe.wait_ge(bank_free, tile - 3)
                            at = h * (NOPE + DV_A)
                            last = product(psum[:, tile % 4, :], [y[:, 0, at:at + P] for y in parts],
                                           latent, True, True)
                            last.then_inc(weights.products, 1)
                            tile += 1
                        for j in range(TT):
                            pe.wait_ge(bank_free, tile - 3)
                            last = product(psum[:, tile % 4, :].rearrange("p (h c) -> p h c", h=HEADS),
                                           [y[:, j * P:(j + 1) * P] for y in latent],
                                           [y[:, 0, :].rearrange("p (h c) -> p h c", h=HEADS)[:, :, NOPE:NOPE + DV_A]
                                            for y in parts], True, True)
                            last.then_inc(weights.products, 1)
                            tile += 1

                    @block.vector
                    def _(dve):
                        tile = 0
                        for target, rows in ((q_a, DQ_A), (k_a, NOPE)):
                            for h in range(HEADS):
                                dve.wait_ge(weights.products, tiles0 + tile + 1)
                                nc.vector.tensor_copy(target[0:rows, h, :], psum[0:rows, tile % 4, :]).then_inc(bank_free, 1)
                                tile += 1
                        for j in range(TT):
                            dve.wait_ge(weights.products, tiles0 + tile + 1)
                            nc.vector.tensor_copy(v_a[:, j, :], psum[:, tile % 4, :]).then_inc(bank_free, 1)
                            tile += 1

        def rope_and_norms(q_a, k_a, k_pe, qk_b):
            with stage("rope") as s:
                table = s.sbuf("table", [P, 4, T], f32)
                squares = s.sbuf("squares", [P, 2, T], f32)
                stat = s.sbuf("stat", [P, 3, 6 * TT * 2], f32)
                turned = s.sbuf("turned", [P, 2, T], f32)
                table_in, squared, summed, mean, root, rstd = [s.sem(n) for n in (
                    "table_in", "squared", "summed", "mean", "root", "rstd")]
                spread, normed, rotated, rotation_read = [s.sem(n) for n in (
                    "spread", "normed", "rotated", "rotation_read")]
                scaled, key_roped, turned_ready = s.sem("scaled"), s.sem("key_roped"), s.sem("turned_ready")
                in_place = s.sem("in_place")
                n_a = HEADS + 1
                jobs = [(q_a[0:DQ_A, h, :], DQ_A, 0, DQ_A ** -0.5) for h in range(HEADS)]
                jobs += [(k_pe[:], P, 0, 1.0)]
                jobs += [(qk_b[:, n, :], P, 2, HD_B ** -0.5 if n < 4 else 1.0) for n in range(6)]
                with nc.Block() as block:
                    @block.sync
                    def _(sp):
                        sp.dma_start(table[:], tables.rearrange("n p t -> p n t")).then_inc(table_in, 16)

                    @block.scalar
                    def _(act):
                        for n in range(6):
                            if n >= 2:
                                act.wait_ge(summed, n - 1)
                            nc.scalar.activation(squares[:, n % 2, :], qk_b[:, n, :], ACT.Square).then_inc(squared, 1)
                        act.wait_ge(mean, 1)
                        nc.scalar.activation(stat[:, 1, :], stat[:, 0, :], ACT.Sqrt).then_inc(root, 1)

                    @block.tensor
                    def _(pe):
                        for n in range(6):
                            pe.wait_ge(squared, n + 1)
                            for j in range(TT):
                                at = (n * TT + j) * 2
                                last = nc.tensor.matmul(psum[:, 0, at:at + 2], squares[:, n % 2, j * P:(j + 1) * P],
                                                        constant("heads_of_pair"), start=True, stop=True)
                            last.then_inc(summed, 1)

                        def rotate_tile(n):
                            tile, rows, _, _ = jobs[n]
                            if n >= 2:
                                pe.wait_ge(rotation_read, n - 1)
                            nc.tensor.matmul(psum[0:rows, 1 + n % 2, :], rotate[0:rows, 0:rows], tile,
                                             start=True, stop=True).then_inc(rotated, 1)

                        for n in range(n_a):
                            rotate_tile(n)
                        pe.wait_ge(rstd, 1)
                        for n in range(6):
                            if n >= 2:
                                pe.wait_ge(normed, n - 1)
                            for j in range(TT):
                                at = (n * TT + j) * 2
                                for half in range(2):
                                    last = nc.tensor.matmul(psum[half * HD_B:(half + 1) * HD_B, 3 + n % 2, j * P:(j + 1) * P],
                                                            stat[:, 2, at + half:at + half + 1].broadcast_to([P, HD_B]),
                                                            identity, start=True, stop=True)
                            last.then_inc(spread, 1)
                        for n in range(6):
                            pe.wait_ge(normed, n + 1)
                            rotate_tile(n_a + n)

                    @block.vector
                    def _(dve):
                        dve.wait_ge(summed, 6)
                        nc.vector.tensor_scalar(stat[:, 0, :], psum[:, 0, 0:6 * TT * 2], 1.0 / HD_B, EPS,
                                                ALU.mult, ALU.add).then_inc(mean, 1)
                        dve.wait_ge(root, 1)
                        nc.vector.reciprocal(stat[:, 2, :], stat[:, 1, :]).then_inc(rstd, 1)
                        dve.wait_ge(table_in, 16)

                        def rope_tile(n):
                            tile, rows, at, scale = jobs[n]
                            buffer = turned[0:rows, n % 2, :]
                            if n >= 2:
                                dve.wait_ge(in_place, n - 1)
                            dve.wait_ge(rotated, n + 1)
                            nc.vector.scalar_tensor_tensor(out=buffer, in0=psum[0:rows, 1 + n % 2, :], scalar=scale,
                                                           in1=table[0:rows, at + 1, :], op0=ALU.mult,
                                                           op1=ALU.mult).then_inc(rotation_read, 1)
                            nc.vector.scalar_tensor_tensor(out=tile, in0=tile, scalar=scale, in1=table[0:rows, at, :],
                                                           op0=ALU.mult, op1=ALU.mult).then_inc(scaled, 1)
                            dve.wait_ge(rotation_read, n + 1)
                            dve.wait_ge(scaled, n + 1)
                            nc.vector.tensor_tensor(out=tile, in0=tile, in1=buffer, op=ALU.add).then_inc(in_place, 1)

                        for n in range(HEADS + 1):
                            rope_tile(n)
                        for n in range(6):
                            dve.wait_ge(spread, n + 1)
                            tile = qk_b[:, n, :]
                            nc.vector.scalar_tensor_tensor(out=tile, in0=tile, scalar=gain("g_qn" if n < 4 else "g_kn"),
                                                           in1=psum[:, 3 + n % 2, :], op0=ALU.mult,
                                                           op1=ALU.mult).then_inc(normed, 1)
                        for n in range(n_a, n_a + 6):
                            rope_tile(n)

                    @block.gpsimd
                    def _(pool):
                        pool.wait_ge(in_place, n_a)
                        for h in range(HEADS):
                            nc.gpsimd.tensor_copy(k_a[NOPE:DQ_A, h, :], k_pe[NOPE:DQ_A, :])

        class Pair:

            def __init__(self, first, i=None):
                self.first, self.i, self.parity = first, i, first % 2

            def count(self, each, plus=0):
                if self.i is None:
                    return self.first * each + plus
                return self.i * (2 * each) + (self.first * each + plus)

            def following(self):
                return Pair(self.first + 1, self.i)

            def previous(self):
                return Pair(self.first - 1, self.i)

            def is_first(self):
                return self.i is None and self.first == 0

        def attention(label, pairs, out_split, out_base, q, k, v, rows, width_v, kind, decay=None):
            latent, forget = kind == "latent", kind == "forget"
            heads_on = 2 if latent else 1
            units = 2 * TT
            ahead = 3
            with stage(label) as s:
                q_st = s.sbuf("q_st", [P, 2, heads_on, T], f32)
                k_st = None if latent else s.sbuf("k_st", [P, 2, T], f32)
                v_st = s.sbuf("v_st", [P, 2, TT, P], f32)
                prob = s.sbuf("prob", [P, 4, T], f32)
                prob_t = s.sbuf("prob_t", [P, 2, TT, T], f32)
                small = s.sbuf("small", [P, 3, units], f32)
                diagonal = square_sum[:].rearrange("p (n c) -> p n c", n=4)
                names = ["q_staged", "v_staged", "scored", "max_ready", "exp_ready", "sum_inverted",
                         "prob_ready", "turned", "turned_read", "attended", "high_ready", "stored"]
                (q_staged, v_staged, scored, max_ready, exp_ready, sum_inverted,
                 prob_ready, turned, turned_read, attended, high_ready, stored) = [s.sem(n) for n in names]
                if forget:
                    rows_, cols_ = decay
                    picked = s.sbuf("picked", [FOX_HEADS, 2, T], f32)
                    c_col = s.sbuf("c_col", [P, 2, TT, 2], f32)
                    minus_c = s.sbuf("minus_c", [P, 2, T], f32)
                    decayed = s.sbuf("decayed", [P, 4, T], f32)
                    score_read, picked_ready, column_ready, decay_spread, decay_ready = [s.sem(n) for n in (
                        "score_read", "picked_ready", "column_ready", "decay_spread", "decay_ready")]

                def all_pairs(engine, pair):
                    pair(Pair(0), False)
                    with engine.Fori(0, (pairs - 2) // 2) as i:
                        pair(Pair(1, i), False)
                        pair(Pair(2, i), False)
                    pair(Pair(pairs - 1), True)

                def keys(qt):
                    return (qt + 1) * P if forget else T

                def query(pair, head, qt):
                    if latent:
                        return q_st[0:rows, pair.parity, head, qt * P:(qt + 1) * P]
                    return q_st[head * rows:(head + 1) * rows, pair.parity, 0, qt * P:(qt + 1) * P]

                def key(pair, head, n):
                    if latent:
                        return k[0:rows, ds(pair.count(2, head), 1), 0:n]
                    return k_st[head * rows:(head + 1) * rows, pair.parity:pair.parity + 1, 0:n]

                with nc.Block() as block:
                    @block.gpsimd
                    def _(pool):
                        def pair_of(p, _):
                            if not p.is_first():
                                pool.wait_ge(scored, p.previous().count(units, 1))
                            source = q[0:rows, ds(p.count(2), 2), :] if latent else q[:, ds(p.count(1), 1), :]
                            if not latent:
                                tile = p.count(1) if forget else p.count(1) // 2 + HEADS // 2
                                nc.gpsimd.tensor_copy(k_st[:, p.parity:p.parity + 1, :], k[:, ds(tile, 1), :])
                            nc.gpsimd.tensor_copy(q_st[0:rows if latent else P, p.parity], source).then_inc(q_staged, 1)
                            if forget:
                                for head in range(2):
                                    if not p.is_first():
                                        pool.wait_ge(decay_spread, p.previous().count(2, head + 1))
                                    own = identity[0:FOX_HEADS, ds(p.count(2, head), 1)].broadcast_to([FOX_HEADS, T])
                                    nc.gpsimd.tensor_tensor(out=picked[:, head, :], in0=rows_[:], in1=own,
                                                            op=ALU.mult).then_inc(picked_ready, 1)
                                    if head == 0:
                                        if not p.is_first():
                                            pool.wait_ge(score_read, p.previous().count(units, 1))
                                        nc.gpsimd.tensor_copy(c_col[:, p.parity], cols_[:, :, ds(p.count(2), 2)]
                                                              ).then_inc(column_ready, 1)
                            if not p.is_first():
                                pool.wait_ge(attended, p.previous().count(2, 1))
                            if kind == "grouped":
                                at = p.count(1) // 2 * width_v
                                nc.gpsimd.tensor_copy(v_st[:, p.parity, :, 0:width_v], v[:, :, ds(at, width_v)]
                                                      ).then_inc(v_staged, 1)
                            else:
                                nc.gpsimd.tensor_copy(v_st[:, p.parity], v[:, :, ds(p.count(P), P)]).then_inc(v_staged, 1)

                        all_pairs(pool, pair_of)

                    @block.tensor
                    def _(pe):
                        def score(p, u):
                            head, qt = divmod(u, TT)
                            if u == 0:
                                pe.wait_ge(q_staged, p.count(1, 1))
                            if not p.is_first() or u >= 4:
                                pe.wait_ge(score_read if forget else exp_ready, p.count(units, u - 3))
                            mm = nc.tensor.matmul(psum[:, u % 4:u % 4 + 1, 0:keys(qt)], query(p, head, qt),
                                                  key(p, head, keys(qt)), start=True, stop=not forget)
                            if forget:
                                mm = nc.tensor.matmul(psum[:, u % 4, qt * P:(qt + 1) * P], identity,
                                                      constant("causal_bias"), start=False, stop=True)
                            mm.then_inc(scored, 1)

                        def spread(p, head):
                            pe.wait_ge(picked_ready, p.count(2, head + 1))
                            if not p.is_first() or head:
                                pe.wait_ge(decay_ready, p.count(2, head))
                            nc.tensor.matmul(psum[:, 7, :], ones[0:FOX_HEADS].broadcast_to([FOX_HEADS, P]),
                                             picked[:, head, :], start=True, stop=True).then_inc(decay_spread, 1)

                        def turn(p, u):
                            head, qt = divmod(u, TT)
                            pe.wait_ge(prob_ready, p.count(units, u + 1))
                            if not p.is_first() or u >= 2:
                                pe.wait_ge(turned_read, p.count(units, u - 1))
                            for kt in range(keys(qt) // P):
                                target, source = psum[:, 4 + u % 2, kt * P:(kt + 1) * P], prob[:, u % 4, kt * P:(kt + 1) * P]
                                if forget:
                                    mm = nc.tensor.matmul(target, source, diagonal[:, u % 4, :], start=True, stop=True)
                                else:
                                    mm = nc.tensor.transpose(target, source, identity)
                            mm.then_inc(turned, 1)

                        def attend(p, head):
                            pe.wait_ge(turned_read, p.count(units, (head + 1) * TT))
                            if head == 0:
                                pe.wait_ge(v_staged, p.count(1, 1))
                                if not p.is_first():
                                    pe.wait_ge(stored, p.count(1))
                            for kt in range(TT):
                                at = kt * P if forget else 0
                                v_at = 0 if kind == "grouped" else head * width_v
                                mm = nc.tensor.matmul(psum[head * width_v:(head + 1) * width_v, 6, at:T],
                                                      v_st[:, p.parity, kt, v_at:v_at + width_v], prob_t[:, head, kt, at:T],
                                                      start=(kt == 0), stop=(kt == TT - 1))
                            mm.then_inc(attended, 1)

                        def pair_of(p, last):
                            if p.is_first():
                                if forget:
                                    spread(p, 0)
                                for u in range(ahead):
                                    score(p, u)
                            for u in range(units):
                                if u + ahead < units:
                                    score(p, u + ahead)
                                elif not last:
                                    score(p.following(), u + ahead - units)
                                turn(p, u)
                                if u == 1:
                                    if not p.is_first():
                                        attend(p.previous(), 1)
                                    if forget:
                                        spread(p, 1)
                                if u == TT:
                                    attend(p, 0)
                                if u == TT + 1 and forget and not last:
                                    spread(p.following(), 0)
                            if last:
                                attend(p, 1)

                        all_pairs(pe, pair_of)

                    @block.vector
                    def _(dve):
                        def normalize(p, u):
                            dve.wait_ge(exp_ready, p.count(units, u + 1))
                            nc.vector.reciprocal(small[:, 2, u:u + 1], small[:, 1, u:u + 1]).then_inc(sum_inverted, 1)
                            dve.wait_ge(sum_inverted, p.count(units, u + 1))
                            if forget:
                                if not p.is_first() or u >= 4:
                                    dve.wait_ge(turned, p.count(units, u - 3))
                                target, source = diagonal[:, u % 4, :], identity
                            else:
                                target = source = prob[:, u % 4, :]
                            nc.vector.tensor_scalar(target, source, small[:, 2, u:u + 1], None,
                                                    ALU.mult).then_inc(prob_ready, 1)

                        def finish(p):
                            dve.wait_ge(high_ready, p.count(1, 1))
                            at = ds(p.count(1, out_base), 1)
                            nc.vector.tensor_tensor(out=out_split[:, 1, at, :], in0=psum[:, 6:7, :],
                                                    in1=out_split[:, 0, at, :].bitcast(f32),
                                                    op=ALU.subtract).then_inc(stored, 1)

                        def pair_of(p, last):
                            for u in range(units):
                                head, qt = divmod(u, TT)
                                dve.wait_ge(scored, p.count(units, u + 1))
                                source = psum[:, u % 4, 0:keys(qt)]
                                if forget:
                                    if u == 0:
                                        dve.wait_ge(column_ready, p.count(1, 1))
                                    if qt == 0:
                                        dve.wait_ge(decay_ready, p.count(2, head + 1))
                                    nc.vector.scalar_tensor_tensor(out=decayed[:, u % 4, 0:keys(qt)], in0=source,
                                                                   scalar=c_col[:, p.parity, qt, head:head + 1],
                                                                   in1=minus_c[:, head, 0:keys(qt)], op0=ALU.add,
                                                                   op1=ALU.add).then_inc(score_read, 1)
                                    dve.wait_ge(score_read, p.count(units, u + 1))
                                    source = decayed[:, u % 4, 0:keys(qt)]
                                nc.vector.tensor_reduce(small[:, 0, u:u + 1], source, AX.X, ALU.max,
                                                        negate=True).then_inc(max_ready, 1)
                                if u >= 1:
                                    normalize(p, u - 1)
                                elif not p.is_first():
                                    normalize(p.previous(), units - 1)
                                if u == 3 and not p.is_first():
                                    finish(p.previous())
                            if last:
                                normalize(p, units - 1)
                                finish(p)

                        all_pairs(dve, pair_of)

                    @block.scalar
                    def _(act):
                        def read_turned(p, u):
                            head, qt = divmod(u, TT)
                            n = keys(qt) // P
                            act.wait_ge(turned, p.count(units, u + 1))
                            if qt == 0 and not p.is_first():
                                act.wait_ge(attended, p.previous().count(2, head + 1))
                            nc.scalar.copy(prob_t[:, head, 0:n, qt * P:(qt + 1) * P],
                                           psum[:, 4 + u % 2, 0:n * P].rearrange("p (k c) -> p k c", k=n)
                                           ).then_inc(turned_read, 1)

                        def copy_decay(p, head):
                            act.wait_ge(decay_spread, p.count(2, head + 1))
                            if not p.is_first():
                                act.wait_ge(score_read, p.previous().count(units, (head + 1) * TT))
                            nc.scalar.activation(minus_c[:, head, :], psum[:, 7, :], ACT.Copy,
                                                 scale=-1.0).then_inc(decay_ready, 1)

                        def finish(p):
                            act.wait_ge(attended, p.count(2, 2))
                            nc.scalar.copy(out_split[:, 0, ds(p.count(1, out_base), 1), :],
                                           psum[:, 6:7, :]).then_inc(high_ready, 1)

                        def pair_of(p, last):
                            if p.is_first() and forget:
                                copy_decay(p, 0)
                            for u in range(units):
                                head, qt = divmod(u, TT)
                                act.wait_ge(max_ready, p.count(units, u + 1))
                                if not p.is_first() or u >= 4:
                                    act.wait_ge(turned, p.count(units, u - 3))
                                source = decayed[:, u % 4, 0:keys(qt)] if forget else psum[:, u % 4, :]
                                e = nc.scalar.activation(prob[:, u % 4, 0:keys(qt)], source, ACT.Exp,
                                                         bias=small[:, 0, u:u + 1], accum_out=small[:, 1, u:u + 1])
                                e.then_inc(exp_ready, 1)
                                if u >= 1:
                                    read_turned(p, u - 1)
                                elif not p.is_first():
                                    read_turned(p.previous(), units - 1)
                                if u == 2 and forget:
                                    copy_decay(p, 1)
                                if u == 3 and not p.is_first():
                                    finish(p.previous())
                                if u == 6 and forget and not last:
                                    copy_decay(p.following(), 0)
                            if last:
                                read_turned(p, units - 1)
                                finish(p)

                        all_pairs(act, pair_of)

        def merge(attended, gates, merged):
            start = weights.start["merge"]
            tiles0 = weights.tiles_before[start]
            with stage("merge") as s:
                part = s.sbuf("part", [P, 2, 4, T], f32)
                product_read, summed, high_ready = s.sem("product_read"), s.sem("summed"), s.sem("high_ready")
                parts_ready, low_done = s.sem("parts_ready"), s.sem("low_done")
                with nc.Block() as block:
                    @block.sync
                    def _(sp):
                        weights.load_for(sp, "merge")

                    @block.gpsimd
                    def _(pool):
                        weights.split_low_all(pool, "merge")

                    @block.tensor
                    def _(pe):
                        with pe.Fori(0, 2) as i:
                            for c in range(2):
                                chunk = Chunk(start + c, i, 2)
                                pe.wait_ge(weights.low_ready, chunk.number + 1)
                                high, low = weights.parts(chunk, 4)
                                for m in range(4):
                                    pe.wait_ge(product_read, i * 8 + 1)
                                    sl = slice(m * P, (m + 1) * P)
                                    for k in range(4):
                                        a = 4 * c + k
                                        last = product(psum[:, 4 * c + m, :], (high[:, k, sl], low[:, k, sl]),
                                                       (attended[:, 0, a, :], attended[:, 1, a, :]), k == 0, k == 3)
                                    last.then_inc(weights.products, 1)

                    @block.scalar
                    def _(act):
                        act.sem_inc(high_ready, 1)
                        with act.Fori(0, 2) as i:
                            for c in range(2):
                                weights.split_high(act, Chunk(start + c + 1, i, 2))
                            for m in range(4):
                                act.wait_ge(summed, i * 4 + (m + 1))
                                nc.scalar.activation(merged[:, 0, ds(i * 4 + m, 1), :], part[:, 0, m:m + 1, :], ACT.Copy,
                                                     scale=0.5).then_inc(high_ready, 1)

                    @block.vector
                    def _(dve):
                        dve.sem_inc(product_read, 1)
                        dve.sem_inc(low_done, 1)
                        with dve.Fori(0, 2) as i:
                            for c in range(2):
                                for m in range(4):
                                    dve.wait_ge(weights.products, i * 8 + (tiles0 + 4 * c + m + 1))
                                    if c == 0 and m == 0:
                                        dve.wait_ge(high_ready, i * 4 + 1)
                                        dve.wait_ge(low_done, i * 4 + 1)
                                    nc.vector.scalar_tensor_tensor(out=part[:, c, m:m + 1, :],
                                                                   in0=gates[:, ds(i * 4 + (DT * c + m), 1), :], scalar=1.0,
                                                                   in1=psum[:, 4 * c + m:4 * c + m + 1, :], op0=ALU.add,
                                                                   op1=ALU.mult).then_inc(product_read, 1)
                            for m in range(4):
                                dve.wait_ge(product_read, i * 8 + (6 + m))
                                nc.vector.tensor_tensor(out=part[:, 0, m, :], in0=part[:, 0, m, :], in1=part[:, 1, m, :],
                                                        op=ALU.add).then_inc(summed, 1)
                            for m in range(4):
                                dve.wait_ge(high_ready, i * 4 + (m + 2))
                                nc.vector.scalar_tensor_tensor(out=merged[:, 1, ds(i * 4 + m, 1), :], in0=part[:, 0, m:m + 1, :],
                                                               scalar=0.5, in1=merged[:, 0, ds(i * 4 + m, 1), :].bitcast(f32),
                                                               op0=ALU.mult, op1=ALU.subtract).then_inc(low_done, 1)

        def mlp(norm, split):
            start = weights.start["mlp"]
            tiles0 = weights.tiles_before[start]
            blocks = D_FF // 256
            with stage("mlp") as s:
                norm = norm(s)
                hidden = s.sbuf("hidden", [P, 2, 2, 2, T], f32r)
                relu = s.sbuf("relu", [P, 2, T], f32)
                square = s.sbuf("square", [P, 2, T], f32)
                rectified, squared, high_ready, hidden_ready, added = [s.sem(n) for n in (
                    "rectified", "squared", "high_ready", "hidden_ready", "added")]

                with nc.Block() as block:
                    @block.sync
                    def _(sp):
                        weights.load_for(sp, "mlp")

                    @block.gpsimd
                    def _(pool):
                        norm.gpsimd(pool)
                        weights.split_low_all(pool, "mlp")

                    @block.tensor
                    def _(pe):
                        norm.tensor(pe)
                        def up(chunk, t, parity):
                            pe.wait_ge(weights.low_ready, chunk.number + 1)
                            high, low = weights.parts(chunk, DT)
                            for m in range(2):
                                if not isinstance(t, int) or t >= 1:
                                    pe.wait_ge(rectified, t * 2 + (m - 1))
                                sl = slice(m * P, (m + 1) * P)
                                for k in range(DT):
                                    if isinstance(t, int) and t == m == 0:
                                        norm.wait_tile(pe, k)
                                    last = product(psum[:, m, :], (high[:, k, sl], low[:, k, sl]),
                                                   (split[:, 0, k, :], split[:, 1, k, :]), k == 0, k == DT - 1)
                                last.then_inc(weights.products, 1)

                        def down(chunk, t, parity):
                            pe.wait_ge(weights.low_ready, chunk.number + 1)
                            high, low = weights.parts(chunk, 2)
                            pe.wait_ge(hidden_ready, t * 2 + 2)
                            for m in range(DT):
                                if not isinstance(t, int) or t * DT + m >= 4:
                                    pe.wait_ge(added, t * DT + (m - 3))
                                sl = slice(m * P, (m + 1) * P)
                                for k in range(2):
                                    last = product(psum[:, 4 + m % 4, :], (high[:, k, sl], low[:, k, sl]),
                                                   (hidden[:, parity, 0, k, :], hidden[:, parity, 1, k, :]),
                                                   k == 0, k == 1)
                                last.then_inc(weights.products, 1)

                        up(Chunk(start), 0, 0)
                        up(Chunk(start + 1), 1, 1)
                        down(Chunk(start + 2), 0, 0)
                        with pe.Fori(0, (blocks - 2) // 2) as i:
                            for b in range(2):
                                up(Chunk(start + 3 + 2 * b, i, 4), i * 2 + (2 + b), b)
                                down(Chunk(start + 4 + 2 * b, i, 4), i * 2 + (1 + b), (1 + b) % 2)
                        down(Chunk(start + 2 * blocks - 1), blocks - 1, 1)

                    @block.scalar
                    def _(act):
                        norm.scalar(act)
                        def high(t, parity):
                            base = t * 10 + (tiles0 - 8) if not isinstance(t, int) or t else tiles0
                            for m in range(2):
                                act.wait_ge(weights.products, base + (m + 1))
                                if not isinstance(t, int) or t >= 1:
                                    act.wait_ge(squared, t * 2 + (m - 1))
                                nc.scalar.activation(relu[:, m, :], psum[:, m, :], ACT.Relu).then_inc(rectified, 1)
                            for m in range(2):
                                act.wait_ge(squared, t * 2 + (m + 1))
                                nc.scalar.copy(hidden[:, parity, 0, m, :], square[:, m, :]).then_inc(high_ready, 1)

                        weights.split_high(act, Chunk(start + 1))
                        weights.split_high(act, Chunk(start + 2))
                        high(0, 0)
                        weights.split_high(act, Chunk(start + 3))
                        high(1, 1)
                        with act.Fori(0, (blocks - 2) // 2) as i:
                            for b in range(2):
                                weights.split_high(act, Chunk(start + 4 + 2 * b, i, 4))
                                weights.split_high(act, Chunk(start + 5 + 2 * b, i, 4))
                                high(i * 2 + (2 + b), b)
                        weights.split_high(act, Chunk(start + 2 * blocks))

                    @block.vector
                    def _(dve):
                        norm.vector(dve)
                        def hide(t, parity):
                            for m in range(2):
                                dve.wait_ge(rectified, t * 2 + (m + 1))
                                if not isinstance(t, int) or t >= 1:
                                    dve.wait_ge(hidden_ready, t * 2 + (m - 1))
                                nc.vector.tensor_tensor(out=square[:, m, :], in0=relu[:, m, :], in1=relu[:, m, :],
                                                        op=ALU.mult).then_inc(squared, 1)
                            for m in range(2):
                                dve.wait_ge(high_ready, t * 2 + (m + 1))
                                nc.vector.tensor_tensor(out=hidden[:, parity, 1, m, :], in0=square[:, m, :],
                                                        in1=hidden[:, parity, 0, m, :].bitcast(f32),
                                                        op=ALU.subtract).then_inc(hidden_ready, 1)

                        def accumulate(t):
                            last = isinstance(t, int) and t == blocks - 1
                            base = tiles0 + 10 * t + (2 if last else 4) if isinstance(t, int) else t * 10 + (tiles0 + 4)
                            for m in range(DT):
                                dve.wait_ge(weights.products, base + (m + 1))
                                nc.vector.tensor_tensor(out=x[:, m, :], in0=psum[:, 4 + m % 4, :], in1=x[:, m, :],
                                                        op=ALU.add).then_inc(added, 1)

                        hide(0, 0)
                        hide(1, 1)
                        accumulate(0)
                        with dve.Fori(0, (blocks - 2) // 2) as i:
                            for b in range(2):
                                hide(i * 2 + (2 + b), b)
                                accumulate(i * 2 + (1 + b))
                        accumulate(blocks - 1)

        def ple(norm, split, scratch):
            start = weights.start["ple"]
            tiles0 = weights.tiles_before[start]
            with stage("ple_in") as s:
                p_rows = s.sbuf("p_rows", [P, TT, 2 * P], f32)
                p_split = s.sbuf("p_split", [P, 2, 2, T], f32r)
                p_in, turned, high_ready = s.sem("p_in"), s.sem("turned"), s.sem("high_ready")
                bank_free = s.sem("bank_free")
                low_ready = s.sem("low_ready")
                with nc.Block() as block:
                    @block.sync
                    def _(sp):
                        sp.dma_start(p_rows[:], w["p"][0, 0].rearrange("(j q) c -> q j c", q=P)).then_inc(p_in, 16)
                        weights.load(sp, Chunk(start + 2), weights.plan_item("ple", 2), 0)

                    @block.gpsimd
                    def _(pool):
                        weights.split_low(pool, Chunk(start + 1))

                    @block.scalar
                    def _(act):
                        for t in range(2):
                            act.wait_ge(turned, t + 1)
                            nc.scalar.copy(p_split[:, 0, t, :], psum[:, t, :]).then_inc(high_ready, 1)
                        weights.split_high(act, Chunk(start + 1))

                    @block.tensor
                    def _(pe):
                        pe.wait_ge(p_in, 16)
                        for t in range(2):
                            for j in range(TT):
                                last = nc.tensor.transpose(psum[:, t, j * P:(j + 1) * P], p_rows[:, j, t * P:(t + 1) * P],
                                                           identity)
                            last.then_inc(turned, 1)
                        pe.wait_ge(low_ready, 2)
                        pe.wait_ge(weights.low_ready, start + 1)
                        parts = weights.parts(Chunk(start), 2)
                        for m in range(DT):
                            if m >= 4:
                                pe.wait_ge(bank_free, m - 3)
                            for k in range(2):
                                last = product(psum[:, 4 + m % 4, :], [y[:, k, m * P:(m + 1) * P] for y in parts],
                                               (p_split[:, 0, k, :], p_split[:, 1, k, :]), k == 0, k == 1)
                            last.then_inc(weights.products, 1)

                    @block.vector
                    def _(dve):
                        for t in range(2):
                            dve.wait_ge(high_ready, t + 1)
                            nc.vector.tensor_tensor(out=p_split[:, 1, t, :], in0=psum[:, t, :],
                                                    in1=p_split[:, 0, t, :].bitcast(f32), op=ALU.subtract).then_inc(low_ready, 1)
                        for m in range(DT):
                            dve.wait_ge(weights.products, tiles0 + m + 1)
                            nc.vector.tensor_scalar(scratch[:, m, :], psum[:, 4 + m % 4, :], 0.5, None,
                                                    ALU.mult).then_inc(bank_free, 1)

            start1 = start + 1
            with stage("ple") as s:
                norm = norm(s)
                gated = s.sbuf("gated", [P, 2, T], f32)
                handed = s.sbuf("handed", [P, 4, T], f32)
                tanh_ready, bank_free, product_ready = s.sem("tanh_ready"), s.sem("bank_free"), s.sem("product_ready")
                with nc.Block() as block:
                    @block.sync
                    def _(sp):
                        for n in (3, 4):
                            weights.load(sp, Chunk(start + n), weights.plan_item("ple", n), 0)
                        weights.load_segments(sp, start + 5, [(1, weights.after_two(dict(weights.plan)["gdn_in"])[0])])

                    @block.gpsimd
                    def _(pool):
                        norm.gpsimd(pool)
                        for n in range(4):
                            weights.split_low(pool, Chunk(start1 + n + 1))

                    @block.tensor
                    def _(pe):
                        norm.tensor(pe)
                        for n in range(4):
                            pe.wait_ge(weights.low_ready, start1 + n + 1)
                            high, low = weights.parts(Chunk(start1 + n), DT)
                            for m in range(2):
                                tile = 2 * n + m
                                if tile >= 4:
                                    pe.wait_ge(bank_free, tile - 3)
                                sl = slice(m * P, (m + 1) * P)
                                for k in range(DT):
                                    if tile == 0:
                                        norm.wait_tile(pe, k)
                                    last = product(psum[:, tile % 4, :], (high[:, k, sl], low[:, k, sl]),
                                                   (split[:, 0, k, :], split[:, 1, k, :]), k == 0, k == DT - 1)
                                last.then_inc(weights.products, 1)

                    @block.scalar
                    def _(act):
                        norm.scalar(act)
                        for n in range(4):
                            weights.split_high(act, Chunk(start1 + n + 1))
                            for m in range(2):
                                tile = 2 * n + m
                                act.wait_ge(weights.products, tiles0 + DT + tile + 1)
                                if tile >= 4:
                                    act.wait_ge(product_ready, tile - 3)
                                nc.scalar.activation(handed[:, tile % 4, :], psum[:, tile % 4, :], ACT.Tanh,
                                                     scale=0.5).then_inc(bank_free, 1)

                    @block.vector
                    def _(dve):
                        norm.vector(dve)
                        for tile in range(DT):
                            dve.wait_ge(bank_free, tile + 1)
                            nc.vector.scalar_tensor_tensor(out=gated[:, tile % 2, :], in0=handed[:, tile % 4, :], scalar=1.0,
                                                           in1=scratch[:, tile, :], op0=ALU.add,
                                                           op1=ALU.mult).then_inc(product_ready, 1)
                            dve.wait_ge(product_ready, tile + 1)
                            nc.vector.tensor_tensor(out=x[:, tile, :], in0=x[:, tile, :], in1=gated[:, tile % 2, :],
                                                    op=ALU.add).then_inc(tanh_ready, 1)

        def swiglu(label, norm, split, total):
            start = weights.start[label]
            tiles0 = weights.tiles_before[start]
            blocks = D_FF2 // 256
            with stage(label) as s:
                norm = norm(s)
                hidden = s.sbuf("hidden", [P, 2, 2, 2, T], f32r)
                tanh = s.sbuf("tanh", [P, 2, T], f32)
                gated = s.sbuf("gated", [P, 2, T], f32)
                inner = s.sbuf("inner", [P, 2, T], f32)
                tanh_ready, gated_ready, inner_ready, high_ready, hidden_ready, added = [s.sem(n) for n in (
                    "tanh_ready", "gated_ready", "inner_ready", "high_ready", "hidden_ready", "added")]

                def first(t):
                    return isinstance(t, int) and t == 0

                def gate_tiles(t):
                    return tiles0 if first(t) else t * 12 + (tiles0 - 8)

                def up_tiles(t):
                    return tiles0 + 2 if first(t) else t * 12 + (tiles0 - 6)

                with nc.Block() as block:
                    @block.sync
                    def _(sp):
                        weights.load_for(sp, label)

                    @block.gpsimd
                    def _(pool):
                        norm.gpsimd(pool)
                        weights.split_low_all(pool, label)

                    @block.tensor
                    def _(pe):
                        norm.tensor(pe)
                        def into_hidden(chunk, t, bank, read):
                            pe.wait_ge(weights.low_ready, chunk.number + 1)
                            high, low = weights.parts(chunk, DT)
                            for m in range(2):
                                if not first(t):
                                    pe.wait_ge(read, t * 2 + (m - 1))
                                sl = slice(m * P, (m + 1) * P)
                                for k in range(DT):
                                    if first(t) and bank == m == 0:
                                        norm.wait_tile(pe, k)
                                    last = product(psum[:, bank + m, :], (high[:, k, sl], low[:, k, sl]),
                                                   (split[:, 0, k, :], split[:, 1, k, :]), k == 0, k == DT - 1)
                                last.then_inc(weights.products, 1)

                        def down(chunk, t, parity):
                            pe.wait_ge(weights.low_ready, chunk.number + 1)
                            high, low = weights.parts(chunk, 2)
                            pe.wait_ge(hidden_ready, t * 2 + 2)
                            for m in range(DT):
                                pe.wait_ge(added, t * DT + (m + 5))
                                sl = slice(m * P, (m + 1) * P)
                                for k in range(2):
                                    last = product(psum[:, 4 + m % 4, :], (high[:, k, sl], low[:, k, sl]),
                                                   (hidden[:, parity, 0, k, :], hidden[:, parity, 1, k, :]),
                                                   k == 0, k == 1)
                                last.then_inc(weights.products, 1)

                        into_hidden(Chunk(start), 0, 0, gated_ready)
                        into_hidden(Chunk(start + 1), 0, 2, inner_ready)
                        with pe.Fori(0, blocks // 2) as i:
                            for b in range(2):
                                t = i * 2 + (b + 1)
                                into_hidden(Chunk(start + 2 + 3 * b, i, 6), t, 0, gated_ready)
                                into_hidden(Chunk(start + 3 + 3 * b, i, 6), t, 2, inner_ready)
                                down(Chunk(start + 4 + 3 * b, i, 6), i * 2 + b if b else i * 2, b)
                        down(Chunk(start + 3 * blocks - 1), blocks - 1, 0)

                    @block.scalar
                    def _(act):
                        norm.scalar(act)
                        def gate(t):
                            for m in range(2):
                                act.wait_ge(weights.products, gate_tiles(t) + (m + 1))
                                if not first(t):
                                    act.wait_ge(gated_ready, t * 2 + (m - 1))
                                nc.scalar.activation(tanh[:, m, :], psum[:, m, :], ACT.Tanh, scale=0.5).then_inc(tanh_ready, 1)

                        def high(t, parity):
                            for m in range(2):
                                act.wait_ge(inner_ready, t * 2 + (m + 1))
                                nc.scalar.copy(hidden[:, parity, 0, m, :], inner[:, m, :]).then_inc(high_ready, 1)

                        weights.split_high(act, Chunk(start + 1))
                        weights.split_high(act, Chunk(start + 2))
                        gate(0)
                        high(0, 0)
                        with act.Fori(0, blocks // 2) as i:
                            for b in range(2):
                                t = i * 2 + (b + 1)
                                weights.split_high(act, Chunk(start + 3 + 3 * b, i, 6))
                                weights.split_high(act, Chunk(start + 4 + 3 * b, i, 6))
                                gate(t)
                                weights.split_high(act, Chunk(start + 5 + 3 * b, i, 6))
                                high(t, (b + 1) % 2)
                        weights.split_high(act, Chunk(start + 3 * blocks))

                    @block.vector
                    def _(dve):
                        norm.vector(dve)
                        def hide(t, parity):
                            for m in range(2):
                                dve.wait_ge(tanh_ready, t * 2 + (m + 1))
                                if not first(t):
                                    dve.wait_ge(inner_ready, t * 2 + (m - 1))
                                nc.vector.scalar_tensor_tensor(out=gated[:, m, :], in0=tanh[:, m, :], scalar=1.0,
                                                               in1=psum[:, m, :], op0=ALU.add,
                                                               op1=ALU.mult).then_inc(gated_ready, 1)
                            for m in range(2):
                                dve.wait_ge(weights.products, up_tiles(t) + (m + 1))
                                dve.wait_ge(gated_ready, t * 2 + (m + 1))
                                if not first(t):
                                    dve.wait_ge(hidden_ready, t * 2 + (m - 1))
                                nc.vector.scalar_tensor_tensor(out=inner[:, m, :], in0=gated[:, m, :], scalar=0.5,
                                                               in1=psum[:, 2 + m, :], op0=ALU.mult,
                                                               op1=ALU.mult).then_inc(inner_ready, 1)
                            for m in range(2):
                                dve.wait_ge(high_ready, t * 2 + (m + 1))
                                nc.vector.tensor_tensor(out=hidden[:, parity, 1, m, :], in0=inner[:, m, :],
                                                        in1=hidden[:, parity, 0, m, :].bitcast(f32),
                                                        op=ALU.subtract).then_inc(hidden_ready, 1)

                        def accumulate(t):
                            last = isinstance(t, int) and t == blocks - 1
                            base = tiles0 + 12 * t + 4 if last else t * 12 + (tiles0 + 8)
                            for m in range(DT):
                                dve.wait_ge(weights.products, base + (m + 1))
                                dve.wait_ge(added, t * DT + (m + 1))
                                nc.vector.tensor_tensor(out=total[:, m, :], in0=psum[:, 4 + m % 4, :], in1=total[:, m, :],
                                                        op=ALU.add).then_inc(added, 1)

                        nc.vector.memset(total[:], 0.0).then_inc(added, DT)
                        hide(0, 0)
                        with dve.Fori(0, blocks // 2) as i:
                            for b in range(2):
                                hide(i * 2 + (b + 1), (b + 1) % 2)
                                accumulate(i * 2 + b if b else i * 2)
                        accumulate(blocks - 1)

        def copy_to(target, scale=None):
            def finish(bank, _, tile):
                if scale is None:
                    return nc.vector.tensor_copy(target[:, ds(tile, 1), :], psum[:, bank:bank + 1, :])
                return nc.vector.tensor_scalar(target[:, ds(tile, 1), :], psum[:, bank:bank + 1, :], scale, None, ALU.mult)
            return finish

        def gdn_in(norm, split, qkv, z2, conv, ba):
            start = weights.start["gdn_in"]
            tiles0 = weights.tiles_before[start]
            tiles_z = tiles0 + 3 * GH
            tiles_ba = tiles_z + GH
            with stage("gdn_in") as s:
                norm = norm(s)
                mixed = s.sbuf("mixed", [P, 2, T], f32)
                tanh = s.sbuf("tanh", [P, 2, T], f32)
                bank_free, tap_done, convolved, tanh_ready, activated = [s.sem(n) for n in (
                    "bank_free", "tap_done", "convolved", "tanh_ready", "activated")]
                z_tanh, z_ready = s.sem("z_tanh"), s.sem("z_ready")
                with nc.Block() as block:
                    @block.sync
                    def _(sp):
                        weights.load_for(sp, "gdn_in")

                    @block.gpsimd
                    def _(pool):
                        norm.gpsimd(pool)
                        weights.split_low_all(pool, "gdn_in")

                    @block.tensor
                    def _(pe):
                        norm.tensor(pe)
                        def turn(i, first_chunk, free, base):
                            for c in range(2):
                                chunk = Chunk(first_chunk + c, i, 2)
                                pe.wait_ge(weights.low_ready, chunk.number + 1)
                                high, low = weights.parts(chunk, DT)
                                for j in (2 * c, 2 * c + 1):
                                    pe.wait_ge(free, i * 4 + (j + 1))
                                    sl = slice((j % 2) * P, (j % 2 + 1) * P)
                                    for k in range(DT):
                                        if base == j == 0:
                                            norm.wait_tile(pe, k)
                                        last = product(psum[:, base + j, :], (high[:, k, sl], low[:, k, sl]),
                                                       (split[:, 0, k, :], split[:, 1, k, :]), k == 0, k == DT - 1)
                                    last.then_inc(weights.products, 1)

                        with pe.Fori(0, 6) as i:
                            turn(i, start, bank_free, 0)
                        with pe.Fori(0, 2) as i:
                            turn(i, start + 12, z_ready, 4)
                        pe.wait_ge(weights.low_ready, start + 17)
                        parts = weights.parts(Chunk(start + 16), DT)
                        for n, at in enumerate((256 - 2 * GH - 64, 256 - GH - 64)):
                            for k in range(DT):
                                last = product(psum[0:64 + GH, n, :], [y[:, k, at:at + 64 + GH] for y in parts],
                                               (split[:, 0, k, :], split[:, 1, k, :]), k == 0, k == DT - 1)
                            last.then_inc(weights.products, 1)

                    @block.scalar
                    def _(act):
                        norm.scalar(act)
                        act.sem_inc(z_ready, 4)
                        with act.Fori(0, 6) as i:
                            for c in range(2):
                                weights.split_high(act, Chunk(start + c + 1, i, 2))
                                for j in (2 * c, 2 * c + 1):
                                    act.wait_ge(weights.products, i * 4 + (tiles0 + j + 1))
                                    act.wait_ge(activated, i * 4 + (j + 1))
                                    nc.scalar.activation(mixed[:, j % 2, :], psum[:, j, :], ACT.Copy,
                                                         scale=conv[:, ds(i * 4 + (j + 3 * 3 * GH), 1)]).then_inc(tap_done, 1)
                                    act.wait_ge(bank_free, i * 4 + (j + 5))
                                    nc.scalar.activation(tanh[:, j % 2, :], mixed[:, j % 2, :], ACT.Tanh,
                                                         scale=0.5).then_inc(tanh_ready, 1)
                        act.wait_ge(activated, 3 * GH + 2)
                        with act.Fori(0, 2) as i:
                            for c in range(2):
                                weights.split_high(act, Chunk(start + 12 + c + 1, i, 2))
                                for j in (2 * c, 2 * c + 1):
                                    act.wait_ge(weights.products, i * 4 + (tiles_z + j + 1))
                                    act.wait_ge(z_ready, i * 4 + (j + 3))
                                    nc.scalar.activation(tanh[:, j % 2, :], psum[:, 4 + j, :], ACT.Tanh,
                                                         scale=0.5).then_inc(z_tanh, 1)
                        weights.split_high(act, Chunk(start + 17))

                    @block.vector
                    def _(dve):
                        norm.vector(dve)
                        dve.sem_inc(bank_free, 4)
                        dve.sem_inc(activated, 2)
                        with dve.Fori(0, 6) as i:
                            for j in range(4):
                                dve.wait_ge(tap_done, i * 4 + (j + 1))
                                for tap in (2, 1, 0):
                                    back = 3 - tap
                                    if tap < 2:
                                        dve.wait_ge(convolved, i * 8 + (2 * j + back - 1))
                                    nc.vector.scalar_tensor_tensor(
                                        out=mixed[:, j % 2, back:T], in0=psum[:, j, 0:T - back],
                                        scalar=conv[:, ds(i * 4 + (j + tap * 3 * GH), 1)],
                                        in1=mixed[:, j % 2, back:T], op0=ALU.mult, op1=ALU.add).then_inc(bank_free if tap == 0 else convolved, 1)
                                dve.wait_ge(tanh_ready, i * 4 + (j + 1))
                                nc.vector.scalar_tensor_tensor(out=qkv[:, ds(i * 4 + j, 1), :], in0=tanh[:, j % 2:j % 2 + 1, :],
                                                               scalar=1.0, in1=mixed[:, j % 2:j % 2 + 1, :], op0=ALU.add,
                                                               op1=ALU.mult).then_inc(activated, 1)
                        with dve.Fori(0, 2) as i:
                            for j in range(4):
                                dve.wait_ge(z_tanh, i * 4 + (j + 1))
                                nc.vector.scalar_tensor_tensor(out=z2[:, ds(i * 4 + j, 1), :], in0=tanh[:, j % 2:j % 2 + 1, :],
                                                               scalar=1.0, in1=psum[:, 4 + j:5 + j, :], op0=ALU.add,
                                                               op1=ALU.mult).then_inc(z_ready, 1)
                        for n in range(2):
                            dve.wait_ge(weights.products, tiles_ba + n + 1)
                            nc.vector.tensor_copy(ba[:, n, :], psum[64:64 + GH, n, :])

        def gdn_rows(qkv, ba, rows, columns):
            with stage("gdn_rows") as s:
                squares = s.sbuf("squares", [P, 2, T], f32)
                work = s.sbuf("work", [GH, 8, T], f32)
                head_col = s.sbuf("head_col", [GH, 3], f32)
                loaded, squared, summed, act_done, dve_done = [s.sem(n) for n in (
                    "loaded", "squared", "summed", "act_done", "dve_done")]
                turned = s.sem("turned")
                b_raw, a_raw = ba[:, 0, :], ba[:, 1, :]
                y, size, e, sp, q_mean, k_mean, decay, one = [work[:, n, :] for n in range(8)]
                big_g = rows[:, 3, :]

                def by_chunk(row, n):
                    return row[:, n * P:(n + 1) * P]

                with nc.Block() as block:
                    @block.sync
                    def _(sp):
                        sp.dma_start(head_col[:, 0:1], w["gdn_a_log_2"].rearrange("l h -> h l")).then_inc(loaded, 16)
                        sp.dma_start(head_col[:, 1:2], w["gdn_dt_bias_2"].rearrange("l h -> h l")).then_inc(loaded, 16)

                    @block.tensor
                    def _(pe):
                        for n in range(2 * GH):
                            pe.wait_ge(squared, n + 1)
                            nc.tensor.matmul(psum[0:GH, n // GH, :], constant("head_select")[:, n % GH * GH:(n % GH + 1) * GH],
                                             squares[:, n % 2, :], start=(n % GH == 0), stop=(n % GH == GH - 1)
                                             ).then_inc(summed, 1)
                        pe.wait_ge(dve_done, 12)
                        pe.wait_ge(act_done, 7)
                        for m, row in enumerate((big_g, y, decay)):
                            for n in range(TT):
                                at = (n * 3 + m) * GH
                                last = nc.tensor.transpose(psum[:, 2, at:at + GH], by_chunk(row, n), identity[0:GH, 0:GH])
                        last.then_inc(turned, 1)

                    @block.scalar
                    def _(act):
                        for n in range(2 * GH):
                            if n >= 2:
                                act.wait_ge(summed, n - 1)
                            nc.scalar.activation(squares[:, n % 2, :], qkv[:, n, :], ACT.Square).then_inc(squared, 1)
                        act.wait_ge(loaded, 32)
                        nc.scalar.activation(head_col[:, 2:3], head_col[:, 0:1], ACT.Exp).then_inc(act_done, 1)
                        nc.scalar.activation(sp, b_raw, ACT.Exp, scale=-1.0).then_inc(act_done, 1)
                        act.wait_ge(dve_done, 2)
                        nc.scalar.activation(e, size, ACT.Exp, scale=-1.0).then_inc(act_done, 1)
                        act.wait_ge(dve_done, 3)
                        nc.scalar.activation(e, e, ACT.Ln).then_inc(act_done, 1)
                        act.wait_ge(dve_done, 9)
                        for n, mean in enumerate((q_mean, k_mean)):
                            nc.scalar.activation(mean, mean, ACT.Sqrt).then_inc(act_done, 1)
                        act.wait_ge(dve_done, 10)
                        nc.scalar.activation(decay, decay, ACT.Exp).then_inc(act_done, 1)

                    @block.vector
                    def _(dve):
                        dve.wait_ge(loaded, 32)
                        nc.vector.memset(one, 1.0)
                        nc.vector.tensor_scalar(y, a_raw, head_col[:, 1:2], None, ALU.add).then_inc(dve_done, 1)
                        dve.wait_ge(dve_done, 1)
                        nc.vector.scalar_tensor_tensor(out=size, in0=y, scalar=-1.0, in1=y, op0=ALU.mult,
                                                       op1=ALU.max).then_inc(dve_done, 1)
                        dve.wait_ge(act_done, 3)
                        nc.vector.tensor_scalar(e, e, 1.0, None, ALU.add).then_inc(dve_done, 1)
                        dve.wait_ge(act_done, 4)
                        nc.vector.scalar_tensor_tensor(out=size, in0=y, scalar=0.0, in1=e, op0=ALU.max,
                                                       op1=ALU.add).then_inc(dve_done, 1)
                        dve.wait_ge(dve_done, 4)
                        nc.vector.tensor_scalar(size, size, head_col[:, 2:3], -1.0, ALU.mult, ALU.mult).then_inc(dve_done, 1)
                        dve.wait_ge(dve_done, 5)
                        for n in range(TT):
                            last = nc.vector.tensor_tensor_scan(by_chunk(big_g, n), by_chunk(one, n), by_chunk(size, n), 0.0,
                                                                ALU.mult, ALU.add)
                        last.then_inc(dve_done, 1)
                        nc.vector.tensor_scalar(sp, sp, 1.0, None, ALU.add).then_inc(dve_done, 1)
                        dve.wait_ge(summed, 2 * GH)
                        for n, mean in enumerate((q_mean, k_mean)):
                            nc.vector.tensor_scalar(mean, psum[0:GH, n, :], 0.25, EPS, ALU.mult, ALU.add).then_inc(dve_done, 1)
                        dve.wait_ge(dve_done, 6)
                        for n in range(TT):
                            last = nc.vector.tensor_scalar(by_chunk(decay, n), by_chunk(big_g, n), -1.0,
                                                           big_g[:, (n + 1) * P - 1:(n + 1) * P], ALU.mult, ALU.add)
                        last.then_inc(dve_done, 1)
                        dve.wait_ge(dve_done, 7)
                        nc.vector.reciprocal(rows[:, 2, :], sp).then_inc(dve_done, 1)
                        dve.wait_ge(dve_done, 11)
                        nc.vector.tensor_scalar(y, rows[:, 2, :], 0.5, None, ALU.mult).then_inc(dve_done, 1)
                        dve.wait_ge(act_done, 6)
                        nc.vector.reciprocal(rows[:, 0, :], q_mean).then_inc(dve_done, 1)
                        nc.vector.reciprocal(rows[:, 1, :], k_mean).then_inc(dve_done, 1)
                        dve.wait_ge(dve_done, 14)
                        nc.vector.tensor_scalar(rows[:, 0, :], rows[:, 0, :], 0.5 * P ** -0.5, None, ALU.mult)
                        nc.vector.tensor_scalar(rows[:, 1, :], rows[:, 1, :], 0.5, None, ALU.mult)
                        dve.wait_ge(turned, 1)
                        nc.vector.tensor_copy(columns[:], psum[:, 2, 0:TT * 3 * GH].rearrange("p (n m h) -> p n m h", n=TT, m=3))

        def gdn_chunks(qkv, rows, columns):
            H = GH
            with stage("gdn_chunks") as s:
                def matrix(name):
                    return s.sbuf(name, [P, H, P], f32)

                (qn, kn, kb, kbg, qg, grow, decay, part0, part1, kd, bv, lt, aq, u_, t_, y_, state) = [matrix(n) for n in (
                    "query", "key", "key_beta", "key_beta_grown", "query_grown", "grown", "decay", "part0", "part1",
                    "key_decayed", "value_beta", "lower_t", "query_key", "inverse_t", "inverse", "product", "state")]
                parts = (part0, part1)
                last_growth = s.sbuf("last_growth", [P, H], f32)
                cols = s.sbuf("cols", [P, 3, H], f32)
                mask = s.sbuf("mask", [P, 8, P], f32)
                names = ["masks_in", "cols_in", "q_spread", "k_spread", "b_spread", "g_spread", "q_ready", "k_ready",
                         "kb_ready", "grown_ready", "diff_ready", "diff_exp", "decay_ready", "v_staged", "qg_ready",
                         "kbg_ready", "k_turned", "kd_ready", "v_turned", "bv_ready", "kk_done", "lt_ready", "qk_done",
                         "aq_ready", "u_ready", "t_ready", "part_ready", "part_turned", "y_done", "y_ready", "zt_done",
                         "z_done", "ks_done", "r_ready", "vn_done", "vn_ready", "o_done", "o_read", "ds_done",
                         "state_ready", "last_ready", "part_first"]
                S = {n: s.sem(n) for n in names}

                def pair(n):
                    return psum[:, 2 * n:2 * n + 2, :].rearrange("p b (h c) -> p (b h) c", h=4)

                A, B, C, E = [pair(n) for n in range(4)]

                def chunk_of(first_tile, i):
                    return qkv[:, first_tile:first_tile + H, ds(i * P, P)]

                def over_heads(m):
                    return m.unsqueeze(1).broadcast_to([P, H, P])

                def over_columns(c):
                    return c.unsqueeze(2).broadcast_to([P, H, P])

                with nc.Block() as block:
                    @block.sync
                    def _(sp):
                        at = CONST_AT["earlier"][0]
                        sp.dma_start(mask[:].rearrange("p n c -> p (n c)"), constants[:, at:at + 8 * P]).then_inc(S["masks_in"], 16)

                    @block.tensor
                    def _(pe):
                        for name in ("ds_done", "zt_done", "o_done"):
                            pe.sem_inc(S[name], 1)
                        with pe.Fori(0, TT) as i:
                            def spread(target, row, done):
                                for h in range(H):
                                    last = nc.tensor.matmul(target[:, h, :], identity[0:H, h:h + 1].broadcast_to([H, P]),
                                                            rows[:, row, ds(i * P, P)], start=True, stop=True)
                                last.then_inc(S[done], 1)

                            def heads(target, left, right, done):
                                for h in range(H):
                                    last = nc.tensor.matmul(target[:, h, :], left[:, h, :], right[:, h, :], start=True, stop=True)
                                last.then_inc(S[done], 1)

                            def turn(target, source, done):
                                for h in range(H):
                                    last = nc.tensor.transpose(target[:, h, :], source[:, h, :], identity)
                                last.then_inc(S[done], 1)

                            pe.wait_ge(S["vn_ready"], i + 1)
                            spread(A, 0, "q_spread")
                            pe.wait_ge(S["o_read"], i + 1)
                            spread(B, 1, "k_spread")
                            pe.wait_ge(S["state_ready"], i + 1)
                            spread(C, 2, "b_spread")
                            spread(E, 3, "g_spread")
                            pe.wait_ge(S["k_ready"], i + 1)
                            turn(A, kn, "k_turned")
                            pe.wait_ge(S["v_staged"], i + 1)
                            turn(B, y_, "v_turned")
                            pe.wait_ge(S["kb_ready"], i + 1)
                            heads(C, kn, kb, "kk_done")
                            pe.wait_ge(S["diff_ready"], i + 1)
                            pe.wait_ge(S["grown_ready"], i + 1)
                            heads(E, kn, qn, "qk_done")
                            pe.wait_ge(S["part_first"], i + 1)
                            pe.wait_ge(S["kd_ready"], i + 1)
                            turn(A, part0, "part_turned")
                            for level in range(1, 7):
                                n = i * 6 + level
                                pe.wait_ge(S["part_ready"], n)
                                pe.wait_ge(S["t_ready"], n)
                                heads(A, parts[level % 2], t_, "y_done")
                                pe.wait_ge(S["y_ready"], n)
                                pe.wait_ge(S["u_ready"], i * 7 + level)
                                heads(B, y_, u_, "zt_done")
                                if level < 6:
                                    heads(C, u_, y_, "z_done")
                            pe.wait_ge(S["aq_ready"], i + 1)
                            pe.wait_ge(S["kbg_ready"], i + 1)
                            heads(E, kbg, state, "ks_done")
                            pe.wait_ge(S["u_ready"], i * 7 + 7)
                            pe.wait_ge(S["r_ready"], i + 1)
                            heads(A, u_, kb, "vn_done")
                            pe.wait_ge(S["qg_ready"], i + 1)
                            pe.wait_ge(S["vn_ready"], i + 2)
                            for h in range(H):
                                nc.tensor.matmul(B[:, h, :], state[:, h, :], qg[:, h, :], start=True, stop=False)
                                last = nc.tensor.matmul(B[:, h, :], grow[:, h, :], aq[:, h, :], start=False, stop=True)
                            last.then_inc(S["o_done"], 1)
                            heads(C, kd, grow, "ds_done")

                    @block.vector
                    def _(dve):
                        def tt(out_, in0, in1, op, done):
                            nc.vector.tensor_tensor(out=out_, in0=in0, in1=in1, op=op).then_inc(S[done], 1)

                        nc.vector.memset(state[:], 0.0).then_inc(S["last_ready"], 1)
                        dve.wait_ge(S["masks_in"], 16)
                        dve.sem_inc(S["state_ready"], 1)
                        with dve.Fori(0, TT) as i:
                            nc.vector.tensor_copy(cols[:].unsqueeze(1), columns[:, ds(i, 1), :, :]).then_inc(S["cols_in"], 1)
                            dve.wait_ge(S["q_spread"], i + 1)
                            tt(qn[:], chunk_of(0, i), A, ALU.mult, "q_ready")
                            dve.wait_ge(S["k_spread"], i + 1)
                            tt(kn[:], chunk_of(H, i), B, ALU.mult, "k_ready")
                            dve.wait_ge(S["b_spread"], i + 1)
                            dve.wait_ge(S["k_ready"], i + 1)
                            tt(kb[:], kn[:], C, ALU.mult, "kb_ready")
                            dve.wait_ge(S["g_spread"], i + 1)
                            dve.wait_ge(S["cols_in"], i + 1)
                            for h in range(H):
                                last = nc.vector.tensor_scalar(decay[:, h, :], E[:, h, :], cols[:, 0, h:h + 1], 0.0,
                                                               ALU.subtract, ALU.min)
                            last.then_inc(S["diff_ready"], 1)
                            dve.wait_ge(S["diff_exp"], i + 1)
                            tt(decay[:], decay[:], over_heads(mask[:, 0, :]), ALU.mult, "decay_ready")
                            dve.wait_ge(S["kk_done"], i + 1)
                            dve.wait_ge(S["decay_ready"], i + 1)
                            tt(lt[:], decay[:], C, ALU.mult, "lt_ready")
                            dve.wait_ge(S["lt_ready"], i + 1)
                            tt(part0[:], lt[:], over_heads(mask[:, 1, :]), ALU.mult, "part_first")
                            dve.wait_ge(S["part_first"], i + 1)
                            tt(u_[:], over_heads(identity), part0[:], ALU.subtract, "u_ready")
                            dve.wait_ge(S["k_turned"], i + 1)
                            tt(kd[:], A, over_columns(cols[:, 2, :]), ALU.mult, "kd_ready")
                            dve.wait_ge(S["v_turned"], i + 1)
                            tt(bv[:], B, over_columns(cols[:, 1, :]), ALU.mult, "bv_ready")
                            dve.wait_ge(S["part_turned"], i + 1)
                            tt(t_[:], over_heads(identity), A, ALU.subtract, "t_ready")
                            dve.wait_ge(S["qk_done"], i + 1)
                            tt(aq[:], decay[:], E, ALU.mult, "aq_ready")
                            dve.wait_ge(S["grown_ready"], i + 1)
                            nc.vector.tensor_copy(last_growth[:].unsqueeze(2), grow[:, :, P - 1:P]).then_inc(S["last_ready"], 1)
                            for level in range(1, 7):
                                if level < 6:
                                    dve.wait_ge(S["z_done"], i * 5 + level)
                                    dve.wait_ge(S["t_ready"], i * 6 + level)
                                    dve.wait_ge(S["zt_done"], i * 6 + (level + 1))
                                    dve.wait_ge(S["u_ready"], i * 7 + level)
                                    tt(t_[:], t_[:], C, ALU.subtract, "t_ready")
                                    tt(u_[:], u_[:], B, ALU.subtract, "u_ready")
                                else:
                                    dve.wait_ge(S["zt_done"], i * 6 + (level + 1))
                                    dve.wait_ge(S["u_ready"], i * 7 + level)
                                    tt(u_[:], u_[:], B, ALU.subtract, "u_ready")
                            dve.wait_ge(S["ks_done"], i + 1)
                            dve.wait_ge(S["bv_ready"], i + 1)
                            dve.wait_ge(S["kbg_ready"], i + 1)
                            tt(kb[:], bv[:], E, ALU.subtract, "r_ready")
                            dve.wait_ge(S["ds_done"], i + 2)
                            dve.wait_ge(S["last_ready"], i + 2)
                            for h in range(H):
                                last = nc.vector.scalar_tensor_tensor(out=state[:, h, :], in0=state[:, h, :],
                                                                      scalar=last_growth[:, h:h + 1], in1=C[:, h, :],
                                                                      op0=ALU.mult, op1=ALU.add)
                            last.then_inc(S["state_ready"], 1)

                    @block.scalar
                    def _(act):
                        for name in ("vn_ready", "o_read"):
                            act.sem_inc(S[name], 1)
                        with act.Fori(0, TT) as i:
                            act.wait_ge(S["g_spread"], i + 1)
                            act.wait_ge(S["ds_done"], i + 1)
                            act.wait_ge(S["diff_ready"], i + 1)
                            nc.scalar.activation(grow[:], E, ACT.Exp).then_inc(S["grown_ready"], 1)
                            nc.scalar.activation(decay[:], decay[:], ACT.Exp).then_inc(S["diff_exp"], 1)
                            for level in range(1, 7):
                                act.wait_ge(S["y_done"], i * 6 + level)
                                nc.scalar.copy(y_[:], A).then_inc(S["y_ready"], 1)
                            act.wait_ge(S["vn_done"], i + 1)
                            act.wait_ge(S["kbg_ready"], i + 1)
                            act.wait_ge(S["last_ready"], i + 2)
                            nc.scalar.copy(grow[:], A).then_inc(S["vn_ready"], 1)
                            act.wait_ge(S["o_done"], i + 2)
                            nc.scalar.copy(chunk_of(0, i), B).then_inc(S["o_read"], 1)

                    @block.gpsimd
                    def _(pool):
                        pool.wait_ge(S["masks_in"], 16)
                        with pool.Fori(0, TT) as i:
                            pool.wait_ge(S["zt_done"], i * 6 + 1)
                            nc.gpsimd.tensor_copy(y_[:], chunk_of(2 * H, i)).then_inc(S["v_staged"], 1)
                            pool.wait_ge(S["lt_ready"], i + 1)
                            for level in range(1, 7):
                                if level == 2:
                                    pool.wait_ge(S["part_turned"], i + 1)
                                    pool.wait_ge(S["u_ready"], i * 7 + 1)
                                if level >= 3:
                                    pool.wait_ge(S["y_done"], i * 6 + (level - 2))
                                nc.gpsimd.tensor_tensor(out=parts[level % 2][:], in0=lt[:], in1=over_heads(mask[:, 1 + level, :]),
                                                        op=ALU.mult).then_inc(S["part_ready"], 1)
                                if level == 1:
                                    pool.wait_ge(S["grown_ready"], i + 1)
                                    pool.wait_ge(S["q_ready"], i + 1)
                                    pool.wait_ge(S["o_done"], i + 1)
                                    nc.gpsimd.tensor_tensor(out=qg[:], in0=qn[:], in1=grow[:], op=ALU.mult).then_inc(S["qg_ready"], 1)
                                    pool.wait_ge(S["kb_ready"], i + 1)
                                    nc.gpsimd.tensor_tensor(out=kbg[:], in0=kb[:], in1=grow[:], op=ALU.mult).then_inc(S["kbg_ready"], 1)

        def gdn_post(qkv, z2, split):
            with stage("gdn_post") as s:
                squares = s.sbuf("squares", [P, 2, T], f32)
                row = s.sbuf("row", [GH, T], f32)
                factor = s.sbuf("factor", [GH, T], f32)
                normed = s.sbuf("normed", [P, 2, T], f32)
                gated = s.sbuf("gated", [P, 2, T], f32)
                squared, summed, mean, root, ready, spread, normed_ready, gated_ready, high_ready, low_done = [s.sem(n) for n in (
                    "squared", "summed", "mean", "root", "ready", "spread", "normed_ready", "gated_ready", "high_ready", "low_done")]
                with nc.Block() as block:
                    @block.scalar
                    def _(act):
                        for h in range(GH):
                            if h >= 2:
                                act.wait_ge(summed, h - 1)
                            nc.scalar.activation(squares[:, h % 2, :], qkv[:, h, :], ACT.Square).then_inc(squared, 1)
                        act.wait_ge(mean, 1)
                        nc.scalar.activation(row[:], row[:], ACT.Sqrt).then_inc(root, 1)
                        for h in range(GH):
                            act.wait_ge(gated_ready, h + 1)
                            nc.scalar.copy(split[:, 0, h, :], gated[:, h % 2, :]).then_inc(high_ready, 1)

                    @block.tensor
                    def _(pe):
                        for h in range(GH):
                            pe.wait_ge(squared, h + 1)
                            nc.tensor.matmul(psum[0:GH, 0, :], constant("head_select")[:, h * GH:(h + 1) * GH],
                                             squares[:, h % 2, :], start=(h == 0), stop=(h == GH - 1)).then_inc(summed, 1)
                        pe.wait_ge(ready, 1)
                        for h in range(GH):
                            if h >= 2:
                                pe.wait_ge(normed_ready, h - 1)
                            nc.tensor.matmul(psum[:, 1 + h % 2, :], identity[0:GH, h:h + 1].broadcast_to([GH, P]), factor[:],
                                             start=True, stop=True).then_inc(spread, 1)

                    @block.vector
                    def _(dve):
                        dve.wait_ge(summed, GH)
                        nc.vector.tensor_scalar(row[:], psum[0:GH, 0, :], 1.0 / P, EPS, ALU.mult, ALU.add).then_inc(mean, 1)
                        dve.wait_ge(root, 1)
                        nc.vector.reciprocal(factor[:], row[:]).then_inc(ready, 1)
                        for h in range(GH):
                            dve.wait_ge(spread, h + 1)
                            if h >= 2:
                                dve.wait_ge(gated_ready, h - 1)
                            nc.vector.scalar_tensor_tensor(out=normed[:, h % 2, :], in0=qkv[:, h, :], scalar=gain("gdn_out_norm_2"),
                                                           in1=psum[:, 1 + h % 2, :], op0=ALU.mult, op1=ALU.mult
                                                           ).then_inc(normed_ready, 1)
                            dve.wait_ge(normed_ready, h + 1)
                            if h >= 2:
                                dve.wait_ge(low_done, h - 1)
                            nc.vector.scalar_tensor_tensor(out=gated[:, h % 2, :], in0=normed[:, h % 2, :], scalar=0.5,
                                                           in1=z2[:, h, :], op0=ALU.mult, op1=ALU.mult).then_inc(gated_ready, 1)

                    @block.gpsimd
                    def _(pool):
                        for h in range(GH):
                            pool.wait_ge(high_ready, h + 1)
                            nc.gpsimd.tensor_tensor(out=split[:, 1, h, :], in0=gated[:, h % 2, :],
                                                    in1=split[:, 0, h, :].bitcast(f32), op=ALU.subtract).then_inc(low_done, 1)

        def fox_kv(norm, split, keys, values, f_raw):
            start = weights.start["fox_kv"]
            tiles0 = weights.tiles_before[start]
            with stage("fox_kv") as s:
                norm = norm(s)
                key_bank_free, value_bank_free = s.sem("key_bank_free"), s.sem("value_bank_free")
                with nc.Block() as block:
                    @block.sync
                    def _(sp):
                        weights.load_for(sp, "fox_kv")

                    @block.gpsimd
                    def _(pool):
                        norm.gpsimd(pool)
                        weights.split_low_all(pool, "fox_kv")

                    @block.scalar
                    def _(act):
                        norm.scalar(act)
                        for first in (0, 4):
                            with act.Fori(0, 2) as i:
                                for c in range(2):
                                    weights.split_high(act, Chunk(start + first + c + 1, i, 2))
                        weights.split_high(act, Chunk(start + 9))

                    @block.tensor
                    def _(pe):
                        norm.tensor(pe)
                        with pe.Fori(0, 2) as i:
                            for c in range(2):
                                chunk = Chunk(start + c, i, 2)
                                pe.wait_ge(weights.low_ready, chunk.number + 1)
                                high, low = weights.parts(chunk, DT)
                                for j in (2 * c, 2 * c + 1):
                                    pe.wait_ge(key_bank_free, i * 4 + (j + 1))
                                    sl = slice((j % 2) * P, (j % 2 + 1) * P)
                                    for k in range(DT):
                                        if j == 0:
                                            norm.wait_tile(pe, k)
                                        last = product(psum[:, j, :], (high[:, k, sl], low[:, k, sl]),
                                                       (split[:, 0, k, :], split[:, 1, k, :]), k == 0, k == DT - 1)
                                    last.then_inc(weights.products, 1)
                        with pe.Fori(0, 2) as i:
                            for half in range(2):
                                chunk = Chunk(start + 4 + half, i, 2)
                                pe.wait_ge(weights.low_ready, chunk.number + 1)
                                parts = weights.parts(chunk, 4)
                                for j in range(TT):
                                    if half == 0:
                                        pe.wait_ge(value_bank_free, i * 4 + (j + 1))
                                    for k in range(4):
                                        a = 4 * half + k
                                        token = [split[:, n, a, j * P:(j + 1) * P] for n in range(2)]
                                        last = product(psum[:, 4 + j, :], token, [y[:, k, :] for y in parts], a == 0, a == DT - 1)
                                    last.then_inc(weights.products, 1)
                        pe.wait_ge(weights.low_ready, start + 9)
                        parts = weights.parts(Chunk(start + 8), DT)
                        at = 256 - FOX_HEADS - 64
                        for k in range(DT):
                            last = product(psum[0:64 + FOX_HEADS, 0, :], [y[:, k, at:at + 64 + FOX_HEADS] for y in parts],
                                           (split[:, 0, k, :], split[:, 1, k, :]), k == 0, k == DT - 1)
                        last.then_inc(weights.products, 1)

                    @block.vector
                    def _(dve):
                        norm.vector(dve)
                        dve.sem_inc(key_bank_free, 4)
                        dve.sem_inc(value_bank_free, 4)
                        with dve.Fori(0, 2) as i:
                            for j in range(4):
                                dve.wait_ge(weights.products, i * 4 + (tiles0 + j + 1))
                                nc.vector.tensor_copy(keys[:, ds(i * 4 + j, 1), :], psum[:, j:j + 1, :]).then_inc(key_bank_free, 1)
                        with dve.Fori(0, 2) as i:
                            for j in range(TT):
                                dve.wait_ge(weights.products, i * 8 + (tiles0 + 8 + 4 + j + 1))
                                nc.vector.tensor_copy(values[:, j, ds(i * T, T)], psum[:, 4 + j, :]).then_inc(value_bank_free, 1)
                        dve.wait_ge(weights.products, tiles0 + 8 + 16 + 1)
                        nc.vector.tensor_copy(f_raw[:], psum[64:64 + FOX_HEADS, 0, :])

        def fox_rows(f_raw, c_rows, c_cols):
            with stage("fox_rows") as s:
                bias = s.sbuf("bias", [FOX_HEADS, 1], f32)
                work = s.sbuf("work", [FOX_HEADS, 4, T], f32)
                y, size, e, one = [work[:, n, :] for n in range(4)]
                loaded, step, exp_ready, ln_ready, turned = [s.sem(n) for n in ("loaded", "step", "exp_ready", "ln_ready", "turned")]
                with nc.Block() as block:
                    @block.sync
                    def _(sp):
                        sp.dma_start(bias[:], w["b_forget_2"].rearrange("(h a) -> h a", a=1)).then_inc(loaded, 16)

                    @block.scalar
                    def _(act):
                        act.wait_ge(step, 2)
                        nc.scalar.activation(e, size, ACT.Exp, scale=-1.0).then_inc(exp_ready, 1)
                        act.wait_ge(step, 3)
                        nc.scalar.activation(e, e, ACT.Ln).then_inc(ln_ready, 1)

                    @block.tensor
                    def _(pe):
                        pe.wait_ge(step, 5)
                        for n in range(TT):
                            last = nc.tensor.transpose(psum[:, 0, n * FOX_HEADS:(n + 1) * FOX_HEADS], c_rows[:, n * P:(n + 1) * P],
                                                       identity[0:FOX_HEADS, 0:FOX_HEADS])
                        last.then_inc(turned, 1)

                    @block.vector
                    def _(dve):
                        nc.vector.memset(one, 1.0)
                        dve.wait_ge(loaded, 16)
                        nc.vector.tensor_scalar(y, f_raw[:], bias[:], None, ALU.add).then_inc(step, 1)
                        dve.wait_ge(step, 1)
                        nc.vector.scalar_tensor_tensor(out=size, in0=y, scalar=-1.0, in1=y, op0=ALU.mult, op1=ALU.max).then_inc(step, 1)
                        dve.wait_ge(exp_ready, 1)
                        nc.vector.tensor_scalar(e, e, 1.0, None, ALU.add).then_inc(step, 1)
                        dve.wait_ge(ln_ready, 1)
                        nc.vector.scalar_tensor_tensor(out=y, in0=y, scalar=0.0, in1=e, op0=ALU.min, op1=ALU.subtract).then_inc(step, 1)
                        dve.wait_ge(step, 4)
                        nc.vector.tensor_tensor_scan(c_rows[:], one, y, 0.0, ALU.mult, ALU.add).then_inc(step, 1)
                        dve.wait_ge(turned, 1)
                        nc.vector.tensor_copy(c_cols[:], psum[:, 0, 0:TT * FOX_HEADS].rearrange("p (n h) -> p n h", n=TT))


        def block_two():
            with ExitStack() as gdn:
                def keep(name, shape, dtype=f32):
                    return gdn.enter_context(nc.sbuf_tensor(name, shape, dtype))

                qkv = keep("gdn_qkv", [P, 3 * GH, T])
                z2 = keep("gdn_z2", [P, GH, T])
                rows = keep("gdn_rows_kept", [GH, 4, T])
                columns = keep("gdn_columns", [P, TT, 3, GH])
                with ExitStack() as early:
                    conv = early.enter_context(nc.sbuf_tensor("conv", [P, N_CONV], f32))
                    ba = early.enter_context(nc.sbuf_tensor("gdn_ba", [GH, 2, T], f32))
                    with stage("conv") as s:
                        conv_rows = s.sbuf("conv_rows", [N_CONV, P], f32)
                        loaded, turned = s.sem("loaded"), s.sem("turned")
                        with nc.Block() as block:
                            @block.sync
                            def _(sp):
                                sp.dma_start(conv_rows[:], w["gdn_conv_2"][0].rearrange("k (t p) -> (k t) p", p=P)).then_inc(loaded, 16)

                            @block.tensor
                            def _(pe):
                                pe.wait_ge(loaded, 16)
                                nc.tensor.transpose(psum[:, 0, 0:N_CONV], conv_rows[:], identity[0:N_CONV, 0:N_CONV]).then_inc(turned, 1)

                            @block.vector
                            def _(dve):
                                dve.wait_ge(turned, 1)
                                nc.vector.tensor_copy(conv[:], psum[:, 0, 0:N_CONV])
                    with nc.sbuf_tensor("gdn_split", [P, 2, DT, T], f32r) as split:
                        gdn_in(norm_of(x, DT, lambda t: gain("pre_mix_norm_2", t), split=split, given=True), split, qkv, z2, conv, ba)
                    gdn_rows(qkv, ba, rows, columns)
                gdn_chunks(qkv, rows, columns)
                with nc.sbuf_tensor("gdn_out_split", [P, 2, DT, T], f32r) as split, \
                        nc.sbuf_tensor("gdn_mix", [P, DT, T], f32) as mix:
                    gdn_post(qkv, z2, split)
                    linear("gdn_out", 2, split, finish_vector=copy_to(mix))
                    rms_normalize("norm_gdn_out", mix, DT, lambda t: gain("post_mix_norm_2", t), add_to=x, sum_next=True)

            def feed_forward(layer):
                with nc.sbuf_tensor(f"ffn_split{layer}", [P, 2, DT, T], f32r) as split, \
                        nc.sbuf_tensor(f"ffn_total{layer}", [P, DT, T], f32) as total:
                    swiglu(f"ffn{layer}", norm_of(x, DT, lambda t: gain("pre_ffn_norm_2", layer * DT + t), split=split,
                                                  given=True), split, total)
                    rms_normalize(f"norm_ffn_out{layer}", total, DT, lambda t: gain("post_ffn_norm_2", layer * DT + t), add_to=x,
                                  sum_next=(layer == 0))

            feed_forward(0)
            with ExitStack() as fox:
                def keep_fox(name, shape, dtype=f32):
                    return fox.enter_context(nc.sbuf_tensor(name, shape, dtype))

                split = keep_fox("fox_split", [P, 2, DT, T], f32r)
                keys = keep_fox("fox_keys", [P, DT, T])
                queries = keep_fox("fox_queries", [P, DT, T])
                values = keep_fox("fox_values", [P, TT, D])
                c_rows = keep_fox("fox_c_rows", [FOX_HEADS, T])
                c_cols = keep_fox("fox_c_cols", [P, TT, FOX_HEADS])
                with nc.sbuf_tensor("fox_f_raw", [FOX_HEADS, T], f32) as f_raw:
                    fox_kv(norm_of(x, DT, lambda t: gain("kv_norm_2", t), split=split, given=True), split, keys, values, f_raw)
                    fox_rows(f_raw, c_rows, c_cols)
                linear("fox_q", 2, split, norm=norm_of(x, DT, lambda t: gain("pre_mix_norm_2", DT + t), split=split, given=True),
                        finish_vector=copy_to(queries, FOX_HD ** -0.5))
                attention("fox", FOX_HEADS // 2, split, 0, queries, keys, values, FOX_HD, FOX_HD, "forget",
                          decay=(c_rows, c_cols))
                linear("fox_out", 2, split, finish_vector=copy_to(queries))
                rms_normalize("norm_fox_out", queries, DT, lambda t: gain("post_mix_norm_2", DT + t), add_to=x, sum_next=True)
            feed_forward(1)

        def write_out():
            with stage("write") as s:
                rows_out = s.sbuf("rows", [P, TT, D], f32)
                turned, copied, stored = s.sem("turned"), s.sem("copied"), s.sem("stored")
                with nc.Block() as block:
                    @block.tensor
                    def _(pe):
                        for n in range(2 * TT):
                            j, half = divmod(n, 2)
                            if n >= 4:
                                pe.wait_ge(copied, n - 3)
                            for t in range(4):
                                last = nc.tensor.transpose(psum[:, n % 4, t * P:(t + 1) * P],
                                                           x[:, half * 4 + t, j * P:(j + 1) * P], identity)
                            last.then_inc(turned, 1)

                    @block.vector
                    def _(dve):
                        for n in range(2 * TT):
                            j, half = divmod(n, 2)
                            dve.wait_ge(turned, n + 1)
                            nc.vector.tensor_copy(rows_out[:, j, half * T:(half + 1) * T], psum[:, n % 4, :]).then_inc(copied, 1)

                    @block.sync
                    def _(sp):
                        for j in range(TT):
                            sp.wait_ge(copied, 2 * j + 2)
                            sp.dma_start(out[0, j * P:(j + 1) * P, :], rows_out[:, j, :]).then_inc(stored, 16)
                        sp.wait_ge(stored, 16 * TT)

        ctx1 = ExitStack()
        with ctx1:
            block_one()
        block_two()
        write_out()


_OUT_SHAPE = (1, T, D)


def kernel(**inputs):
    import concourse.bacc as bacc
    from concourse import mybir
    from concourse.bass_utils import run_bass_kernel_spmd

    nc = bacc.Bacc("TRN2", target_bir_lowering=False, num_devices=1, dynamic_dma_scratch_size=1024)
    arrays, handles = {}, {}
    for name, value in inputs.items():
        a = np.ascontiguousarray(value)
        arrays[f"in_{name}"] = a
        handles[name] = nc.dram_tensor(f"in_{name}", a.shape, mybir.dt.from_np(a.dtype), kind="ExternalInput").ap()
    arrays["shape_constants"] = shape_constants()
    arrays["rope_tables"] = rope_tables()
    constants = nc.dram_tensor("shape_constants", (P, N_CONST), mybir.dt.float32, kind="ExternalInput").ap()
    tables = nc.dram_tensor("rope_tables", (4, P, T), mybir.dt.float32, kind="ExternalInput").ap()
    out = nc.dram_tensor("out", _OUT_SHAPE, mybir.dt.float32, kind="ExternalOutput").ap()
    build_program(nc, handles, constants, tables, out)
    result = run_bass_kernel_spmd(nc, [arrays], core_ids=[0])
    return result.results[0]["out"]
```

```python
import numpy as np

P = 128
T = 512
TT = T // P
D = 1024
DT = D // P
EPS = 1e-6
GRID_W = 64
ROPE_THETA = 10000.0

HEADS = 8
NOPE, ROPE, DV_A = 64, 32, 64
DQ_A = NOPE + ROPE
Q_LORA, KV_LORA = 256, 128
HD_B, KV_B = 64, 2
D_FF = 4 * D
COL_QLAT, COL_KV = 0, Q_LORA
COL_QB = COL_KV + KV_LORA + ROPE
COL_KB = COL_QB + HEADS * HD_B
COL_VB = COL_KB + KV_B * HD_B
COL_GATES = COL_VB + KV_B * HD_B

GH = 8
GDN_QKV = 3 * GH * P
FOX_HEADS, FOX_HD = 16, 64
D_FF2 = 2816
CHUNK = 2048
NEG = -1.0e30

GAIN_ROWS = [("g_mix", 8), ("g_qa", 2), ("g_kva", 1), ("g_mlp", 8), ("g_ple", 8), ("g_final", 8),
             ("pre_mix_norm_2", 16), ("post_mix_norm_2", 16), ("pre_ffn_norm_2", 16),
             ("post_ffn_norm_2", 16), ("kv_norm_2", 8), ("gdn_out_norm_2", 1)]
GAIN_AT = {}
_row = 0
for _name, _tiles in GAIN_ROWS:
    GAIN_AT[_name] = _row
    _row += _tiles
GAIN_AT["g_qn"] = _row
GAIN_AT["g_kn"] = _row + 1
N_GAINS = _row + 2
CONV_TAPS = 4
N_CONV = CONV_TAPS * 3 * GH

CONST_AT = {}
_col = 0
for _name, _n in [("identity", P), ("rotate", P), ("heads_of_pair", 2), ("ones", 1), ("causal_bias", P),
                  ("head_select", GH * GH), ("earlier", P), ("level", 7 * P)]:
    CONST_AT[_name] = (_col, _n)
    _col += _n
N_CONST = _col
N_SMALL_CONST = CONST_AT["earlier"][0]


def shape_constants():
    c = np.zeros((P, N_CONST), np.float32)

    def put(name, value):
        at, n = CONST_AT[name]
        c[:, at:at + n] = value

    row, col = np.arange(P)[:, None], np.arange(P)[None, :]
    put("identity", row == col)
    half = ROPE // 2
    first = (col % ROPE) < half
    put("rotate", np.where(first & (row == col + half), -1.0, 0.0) + np.where(~first & (row == col - half), 1.0, 0.0))
    put("heads_of_pair", (row // HD_B) == np.arange(2)[None, :])
    put("ones", 1.0)
    put("head_select", np.eye(GH).reshape(1, GH * GH))
    put("causal_bias", np.where(col > row, NEG, 0.0))
    put("earlier", row <= col)
    levels = [((row // (2 * b)) == (col // (2 * b))) & ((row // b) % 2 == 0) & ((col // b) % 2 == 1)
              for b in (1, 2, 4, 8, 16, 32, 64)]
    put("level", np.concatenate(levels, axis=1))
    return c


def rope_tables():
    t = np.arange(T)
    out = np.zeros((4, P, T), np.float32)
    inv = (ROPE_THETA ** (-np.arange(0, ROPE, 2, dtype=np.float32) / np.float32(ROPE))).astype(np.float32)
    ang = (t.astype(np.float32)[None, :] * inv[:, None]).astype(np.float32)
    out[0, :, :] = 1.0
    for half in range(2):
        at = NOPE + half * (ROPE // 2)
        out[0, at:at + ROPE // 2] = np.cos(ang)
        out[1, at:at + ROPE // 2] = np.sin(ang)
    row_ang = ((t // GRID_W).astype(np.float32)[None, :] * inv[:, None]).astype(np.float32)
    col_ang = ((t % GRID_W).astype(np.float32)[None, :] * inv[:, None]).astype(np.float32)
    for group in range(P // 16):
        a = row_ang if (group // 2) % 2 == 0 else col_ang
        out[2, group * 16:(group + 1) * 16] = np.cos(a)
        out[3, group * 16:(group + 1) * 16] = np.sin(a)
    return out


class Chunk:

    def __init__(self, first, i=0, per_turn=0):
        assert per_turn % 2 == 0
        self.slot = first % 2
        self.number = first + i * per_turn if per_turn else first
        self.uses = first // 2 + 1 + i * (per_turn // 2) if per_turn else first // 2 + 1
        self.first, self.i, self.per_turn = first, i, per_turn


class Stage:

    def __init__(self, nc, label):
        from contextlib import ExitStack
        self.nc, self.label, self.stack, self.sems = nc, label, ExitStack(), []

    def sem(self, name):
        s = self.stack.enter_context(self.nc.semaphore(f"{self.label}_{name}"))
        self.sems.append(s)
        return s

    def sbuf(self, name, shape, dtype):
        return self.stack.enter_context(self.nc.sbuf_tensor(f"{self.label}_{name}", shape, dtype))

    def __enter__(self):
        self.stack.__enter__()
        return self

    def __exit__(self, *exc):
        if exc[0] is None:
            numbers = sorted(s.num for s in self.sems)
            at = 0
            while at < len(numbers):
                end = at
                while end + 1 < len(numbers) and numbers[end + 1] == numbers[end] + 1:
                    end += 1
                self.nc.all_engine_barrier(sems_to_clear=range(numbers[at], numbers[end] + 1))
                at = end + 1
        return self.stack.__exit__(*exc)


class Weights:

    def __init__(self, nc, enter, plan):
        from concourse import mybir
        self.nc, self.plan = nc, plan
        f32, f32r = mybir.dt.float32, mybir.dt.float32r
        self.f32, self.sub = f32, mybir.AluOpType.subtract
        self.raw = enter(nc.sbuf_tensor("weights_raw", [P, 2, CHUNK], f32))
        self.high = enter(nc.sbuf_tensor("weights_high", [P, 2, CHUNK], f32r))
        self.low = enter(nc.sbuf_tensor("weights_low", [P, 2, CHUNK], f32r))
        self.loaded = [enter(nc.semaphore(f"weights_loaded_{s}")) for s in range(2)]
        self.high_ready = enter(nc.semaphore("weights_high_ready"))
        self.low_ready = enter(nc.semaphore("weights_low_ready"))
        self.products = enter(nc.semaphore("products_done"))
        self.start = {}
        n = 0
        for name, segments in plan:
            self.start[name] = n
            n += sum(turns * len(items) for turns, items in segments)
        self.total = n
        self.width, self.tiles_before, tiles, self.turn = [], [0], 0, []
        for _, segments in plan:
            for turns, items in segments:
                for i in range(turns):
                    for kt, cols, _, count in items:
                        self.width.append(kt * cols)
                        tiles += count
                        self.tiles_before.append(tiles)

    def load(self, sp, chunk, item, i):
        kt, cols, source, _ = item
        if chunk.first >= 2:
            sp.wait_ge(self.low_ready, chunk.number - 1)
        sp.dma_start(self.raw[:, chunk.slot, 0:kt * cols].rearrange("p (k c) -> p k c", k=kt),
                     source(i)).then_inc(self.loaded[chunk.slot], 16)

    def load_segments(self, sp, first, segments):
        for turns, items in segments:
            if turns == 1:
                for item in items:
                    self.load(sp, Chunk(first), item, 0)
                    first += 1
            else:
                with sp.Fori(0, turns) as i:
                    for pos, item in enumerate(items):
                        self.load(sp, Chunk(first + pos, i, len(items)), item, i)
                first += turns * len(items)

    @staticmethod
    def shifted(items, by):
        def later(source):
            return lambda i: source(i + by)
        return [(kt, cols, later(source), count) for kt, cols, source, count in items]

    def after_two(self, segments):
        rest, head, need = [], [], 2
        for turns, items in segments:
            if need == 0:
                rest.append((turns, items))
                continue
            skipped = 0
            while need and skipped < turns:
                turn = self.shifted(items, skipped)
                take = min(need, len(items))
                head += turn[:take]
                need -= take
                skipped += 1
                if take < len(items):
                    rest.append((1, turn[take:]))
            if skipped < turns:
                rest.append((turns - skipped, self.shifted(items, skipped)))
        return head, rest

    def load_for(self, sp, name):
        names = [n for n, _ in self.plan]
        at = names.index(name)
        _, rest = self.after_two(self.plan[at][1])
        self.load_segments(sp, self.start[name] + 2, rest)
        if at + 1 < len(names):
            head, _ = self.after_two(self.plan[at + 1][1])
            self.load_segments(sp, self.start[names[at + 1]], [(1, head)])

    def plan_item(self, name, n):
        for turns, items in dict(self.plan)[name]:
            if n < turns * len(items):
                return self.shifted(items, n // len(items))[n % len(items)]
            n -= turns * len(items)

    def split_high(self, act, chunk):
        if chunk.first >= self.total:
            return
        width = self.width[chunk.first]
        act.wait_ge(self.loaded[chunk.slot], 16 * chunk.uses)
        if chunk.first >= 2:
            act.wait_ge(self.products, self.tiles_at(chunk, -1))
        self.nc.scalar.copy(self.high[:, chunk.slot, 0:width],
                            self.raw[:, chunk.slot, 0:width]).then_inc(self.high_ready, 1)

    def tiles_at(self, chunk, by=0):
        at = self.tiles_before[chunk.first + by]
        if chunk.per_turn:
            step = chunk.per_turn
            slope = self.tiles_before[chunk.first + by + step] - at
            return chunk.i * slope + at
        return at

    def split_low(self, pool, chunk):
        if chunk.first >= self.total:
            return
        width = self.width[chunk.first]
        pool.wait_ge(self.high_ready, chunk.number + 1)
        self.nc.gpsimd.tensor_tensor(out=self.low[:, chunk.slot, 0:width],
                                     in0=self.raw[:, chunk.slot, 0:width],
                                     in1=self.high[:, chunk.slot, 0:width].bitcast(self.f32),
                                     op=self.sub).then_inc(self.low_ready, 1)

    def split_low_all(self, pool, name):
        first = self.start[name] + 1
        for turns, items in dict(self.plan)[name]:
            if turns == 1:
                for pos in range(len(items)):
                    self.split_low(pool, Chunk(first + pos))
            else:
                with pool.Fori(0, turns) as i:
                    for pos in range(len(items)):
                        self.split_low(pool, Chunk(first + pos, i, len(items)))
            first += turns * len(items)

    def parts(self, chunk, kt):
        width = self.width[chunk.first]
        return [x[:, chunk.slot, 0:width].rearrange("p (k c) -> p k c", k=kt) for x in (self.high, self.low)]


def weight_plan(w):
    import concourse.bass as bass

    def cols(matrix, kt, n, at, tiles=2):
        view = matrix.rearrange("(k p) c -> p k c", p=P)
        return (kt, n, lambda i: view[:, :, bass.ds(at(i), n)], tiles)

    def rows(matrix, at):
        view = matrix.rearrange("(k p) c -> p k c", p=P)
        return (2, D, lambda i: view[:, bass.ds(at(i), 2), :], DT)

    def halves(matrix, n, at, half):
        view = matrix.rearrange("(k p) c -> p k c", p=P)
        return (4, n, lambda i: view[:, 4 * half:4 * half + 4, bass.ds(at(i), n)], TT)

    def pairs(matrix, turns, start=0):
        return (turns, [cols(matrix, DT, 256, lambda i: i * 512 + start),
                        cols(matrix, DT, 256, lambda i: i * 512 + (start + 256))])

    def once(*items):
        return (1, list(items))

    w_in, qb, kvb = w["w_in"][0], w["w_qb"][0], w["w_kvb"][0]
    up, down = w["w_up"][0], w["w_down"][0]

    def u1(t0, step):
        return cols(up, DT, 256, lambda i: i * (256 * step) + 256 * t0)

    def d1(t0, step):
        return rows(down, lambda i: i * (2 * step) + 2 * t0)

    def swiglu(layer):
        inner, outer = w["w_ffn_in_2"][layer], w["w_ffn_out_2"][layer]

        def g(t0, step):
            return cols(inner, DT, 256, lambda i: i * (256 * step) + 256 * t0)

        def u(t0, step):
            return cols(inner, DT, 256, lambda i: i * (256 * step) + (256 * t0 + D_FF2))

        def d(t0, step):
            return rows(outer, lambda i: i * (2 * step) + 2 * t0)

        return [once(g(0, 0), u(0, 0)), (5, [g(1, 2), u(1, 2), d(0, 2), g(2, 2), u(2, 2), d(1, 2)]), once(d(10, 0))]

    gdn, kv = w["gdn_w_in_2"][0], w["w_kv_2"]
    return [
        ("mixer_in", [pairs(w_in, 4, COL_GATES),
                      once(cols(w_in, DT, 256, lambda i: COL_QLAT),
                           cols(w_in, DT, 256, lambda i: COL_QB), cols(w_in, DT, 256, lambda i: COL_QB + 256),
                           cols(w_in, DT, 256, lambda i: COL_KB),
                           cols(w_in, DT, 256, lambda i: COL_KV))]),
        ("latent_up", [once(cols(qb, 2, HEADS * DQ_A, lambda i: 0, HEADS), cols(kvb, 1, D, lambda i: 0, HEADS + TT))]),
        ("merge", [(2, [cols(w["w_oa"][0], 4, 512, lambda i: i * 512, 4),
                        cols(w["w_ob"][0], 4, 512, lambda i: i * 512, 4)])]),
        ("mixer_out", [pairs(w["w_o"][0], 2)]),
        ("mlp", [once(u1(0, 0), u1(1, 0), d1(0, 0)), (7, [u1(2, 2), d1(1, 2), u1(3, 2), d1(2, 2)]), once(d1(15, 0))]),
        ("ple", [once(cols(w["w_ple"][0], 2, D, lambda i: 0, DT)), pairs(w["w_ple_gate"][0], 2)]),
        ("gdn_in", [pairs(gdn, 6), pairs(gdn, 2, GDN_QKV), once(cols(gdn, DT, 256, lambda i: GDN_QKV + D + 2 * GH - 256))]),
        ("gdn_out", [pairs(w["gdn_w_out_2"][0], 2)]),
        ("ffn0", swiglu(0)),
        ("fox_kv", [pairs(kv, 2),
                    (2, [halves(kv, 512, lambda i: i * 512 + D, 0), halves(kv, 512, lambda i: i * 512 + D, 1)]),
                    once(cols(kv, DT, 256, lambda i: 2 * D + FOX_HEADS - 256, 1))]),
        ("fox_q", [pairs(w["fox_w_q_2"][0], 2)]),
        ("fox_out", [pairs(w["fox_w_o_2"][0], 2)]),
        ("ffn1", swiglu(1)),
    ]


def build_program(nc, w, constants, tables, out):
    import concourse.bass as bass
    from concourse import mybir
    from contextlib import ExitStack

    f32, f32r = mybir.dt.float32, mybir.dt.float32r
    ALU, ACT, AX = mybir.AluOpType, mybir.ActivationFunctionType, mybir.AxisListType
    ds = bass.ds
    ctx = ExitStack()
    enter = ctx.enter_context


    def stage(label):
        return Stage(nc, label)


    with ctx:
        weights = Weights(nc, enter, weight_plan(w))
        const = enter(nc.sbuf_tensor("const", [P, N_SMALL_CONST], f32))
        gains = enter(nc.sbuf_tensor("gains", [P, N_GAINS], f32))
        conv = enter(nc.sbuf_tensor("conv", [P, N_CONV], f32))
        x = enter(nc.sbuf_tensor("x_stream", [P, DT, T], f32))
        square_sum = enter(nc.sbuf_tensor("square_sum", [P, T], f32))
        psum = enter(nc.psum_tensor("psum", [P, 8, T], f32))

        def constant(name):
            at, n = CONST_AT[name]
            return const[:, at:at + n]

        identity, rotate, ones = constant("identity"), constant("rotate"), constant("ones")

        def gain(name, tile=0):
            at = GAIN_AT[name] + tile
            return gains[:, at:at + 1]

        def product(bank, w_parts, a_parts, first, last):
            (wh, wl), (ah, al) = w_parts, a_parts
            nc.tensor.matmul(bank, wh, ah, start=first, stop=False)
            nc.tensor.matmul(bank, wh, al, start=False, stop=False)
            return nc.tensor.matmul(bank, wl, ah, start=False, stop=last)

        with stage("init") as s:
            rows_in = s.sbuf("gain_rows", [P, P], f32)
            x_rows = s.sbuf("x_rows", [P, TT, D], f32)
            conv_rows = s.sbuf("conv_rows", [N_CONV, P], f32)
            conv_in = s.sem("conv_loaded")
            loaded, gains_in, x_in = s.sem("const_loaded"), s.sem("gains_loaded"), s.sem("x_loaded")
            zeroed, turned, copied = s.sem("gain_rows_zeroed"), s.sem("turned"), s.sem("copied")
            with nc.Block() as block:
                @block.sync
                def _(sp):
                    sp.dma_start(const[:], constants[:, 0:N_SMALL_CONST]).then_inc(loaded, 16)
                    for j in range(TT):
                        sp.dma_start(x_rows[:, j, :], w["x"][0, j * P:(j + 1) * P, :]).then_inc(x_in, 16)
                    head, _ = weights.after_two(weights.plan[0][1])
                    weights.load_segments(sp, 0, [(1, head)])
                    sp.dma_start(conv_rows[:], w["gdn_conv_2"][0].rearrange("k (t p) -> (k t) p", p=P)).then_inc(conv_in, 16)

                @block.scalar
                def _(act):
                    act.wait_ge(zeroed, 1)
                    for name, tiles in GAIN_ROWS:
                        at = GAIN_AT[name]
                        g = w[name]
                        if len(g.shape) == 2:
                            g = g.rearrange("l (t p) -> (l t) p", p=P)
                        else:
                            g = g.rearrange("(t p) -> t p", p=P)
                        act.dma_start(rows_in[at:at + tiles, :], g).then_inc(gains_in, 16)
                    for name in ("g_qn", "g_kn"):
                        at = GAIN_AT[name]
                        for half in range(2):
                            act.dma_start(rows_in[at:at + 1, half * HD_B:(half + 1) * HD_B],
                                          w[name]).then_inc(gains_in, 16)
                    weights.split_high(act, Chunk(0))

                @block.gpsimd
                def _(pool):
                    nc.gpsimd.memset(rows_in[:], 0.0).then_inc(zeroed, 1)
                    weights.split_low(pool, Chunk(0))

                @block.tensor
                def _(pe):
                    pe.wait_ge(loaded, 16)
                    pe.wait_ge(x_in, 16 * TT)
                    for t in range(DT):
                        if t >= 4:
                            pe.wait_ge(copied, t - 3)
                        for j in range(TT):
                            last = nc.tensor.transpose(psum[:, t % 4, j * P:(j + 1) * P],
                                                       x_rows[:, j, t * P:(t + 1) * P], identity)
                        last.then_inc(turned, 1)
                    pe.wait_ge(gains_in, 16 * (len(GAIN_ROWS) + 4))
                    nc.tensor.transpose(psum[:, 4, 0:P], rows_in[:], identity).then_inc(turned, 1)
                    pe.wait_ge(conv_in, 16)
                    nc.tensor.transpose(psum[:, 5, 0:N_CONV], conv_rows[:], identity[0:N_CONV, 0:N_CONV]).then_inc(turned, 1)

                @block.vector
                def _(dve):
                    for t in range(DT):
                        dve.wait_ge(turned, t + 1)
                        nc.vector.tensor_copy(x[:, t, :], psum[:, t % 4, :]).then_inc(copied, 1)
                    dve.wait_ge(turned, DT + 1)
                    nc.vector.tensor_copy(gains[:], psum[:, 4, 0:N_GAINS])
                    dve.wait_ge(turned, DT + 2)
                    nc.vector.tensor_copy(conv[:], psum[:, 5, 0:N_CONV])

        class Norm:

            def __init__(self, s, source, tiles, gain_at, split=None, plain=None, add_to=None, given=False,
                         sum_next=False, prefix="norm"):
                self.source, self.tiles, self.gain_at, self.split = source, tiles, gain_at, split
                self.plain, self.add_to, self.given, self.sum_next = plain, add_to, given, sum_next
                self.squares = s.sbuf(prefix + "_squares", [P, 2, T], f32)
                if plain is None:
                    self.ring = s.sbuf(prefix + "_ring", [P, 4, T], f32)
                self.stat = s.sbuf(prefix + "_stat", [P, 3, TT], f32)
                (self.squared, self.accumulated, self.summed, self.mean, self.root, self.rstd, self.spread,
                 self.scaled, self.high_done, self.even_done, self.odd_done, self.added) = [s.sem(f"{prefix}_{n}") for n in (
                    "squared", "accumulated", "summed", "mean", "root", "rstd", "spread", "scaled", "high_done",
                    "even_done", "odd_done", "added")]
                self.before = 0 if given else tiles

            def wait_tile(self, pe, t):
                pe.wait_ge((self.even_done, self.odd_done)[t % 2], t // 2 + 1)

            def square(self, act, n, source, t):
                if t == 0 or n < 2:
                    target = square_sum[:] if t == 0 else self.squares[:, t % 2, :]
                else:
                    target = self.squares[:, t % 2, :]
                    act.wait_ge(self.accumulated, n - 1)
                nc.scalar.activation(target, source[:, t, :], ACT.Square).then_inc(self.squared, 1)

            def accumulate(self, dve, n, t):
                dve.wait_ge(self.squared, n + 1)
                if n >= 1:
                    dve.wait_ge(self.accumulated, n)
                if t == 0:
                    dve.sem_inc(self.accumulated, 1)
                else:
                    nc.vector.tensor_tensor(out=square_sum[:], in0=square_sum[:], in1=self.squares[:, t % 2, :],
                                            op=ALU.add).then_inc(self.accumulated, 1)

            def scalar(self, act):
                if not self.given:
                    for t in range(self.tiles):
                        self.square(act, t, self.source, t)
                act.wait_ge(self.mean, 1)
                nc.scalar.activation(self.stat[:, 1, :], self.stat[:, 0, :], ACT.Sqrt).then_inc(self.root, 1)
                if self.split is not None:
                    for t in range(self.tiles):
                        act.wait_ge(self.scaled, t + 1)
                        nc.scalar.copy(self.split[:, 0, t, :], self.ring[:, t % 4, :]).then_inc(self.high_done, 1)
                if self.sum_next:
                    for t in range(self.tiles):
                        result, ready = (self.plain, self.scaled) if self.add_to is None else (self.add_to, self.added)
                        act.wait_ge(ready, t + 1)
                        self.square(act, self.before + t, result, t)

            def tensor(self, pe):
                if not self.given:
                    pe.wait_ge(self.accumulated, self.tiles)
                for j in range(TT):
                    last = nc.tensor.matmul(psum[:, 6, j:j + 1], square_sum[:, j * P:(j + 1) * P], ones,
                                            start=True, stop=True)
                last.then_inc(self.summed, 1)
                pe.wait_ge(self.rstd, 1)
                for j in range(TT):
                    last = nc.tensor.matmul(psum[:, 7, j * P:(j + 1) * P],
                                            self.stat[:, 2, j:j + 1].broadcast_to([P, P]), identity,
                                            start=True, stop=True)
                last.then_inc(self.spread, 1)

            def vector(self, dve):
                tiles = self.tiles
                if not self.given:
                    for t in range(tiles):
                        self.accumulate(dve, t, t)
                dve.wait_ge(self.summed, 1)
                nc.vector.tensor_scalar(self.stat[:, 0, :], psum[:, 6, 0:TT], 1.0 / (tiles * P), EPS,
                                        ALU.mult, ALU.add).then_inc(self.mean, 1)
                dve.wait_ge(self.root, 1)
                nc.vector.reciprocal(self.stat[:, 2, :], self.stat[:, 1, :]).then_inc(self.rstd, 1)
                dve.wait_ge(self.spread, 1)
                for t in range(tiles + 2):
                    if t < tiles:
                        if self.plain is None and t >= 4:
                            if self.split is None and self.sum_next:
                                dve.wait_ge(self.added, t - 3)
                            else:
                                self.wait_tile(dve, t - 4)
                        target = self.plain[:, t, :] if self.plain is not None else self.ring[:, t % 4, :]
                        nc.vector.scalar_tensor_tensor(out=target, in0=self.source[:, t, :], scalar=self.gain_at(t),
                                                       in1=psum[:, 7, :], op0=ALU.mult,
                                                       op1=ALU.mult).then_inc(self.scaled, 1)
                    if self.split is not None and t % 2 == 0 and 1 <= t - 1 < tiles:
                        dve.wait_ge(self.high_done, t)
                        nc.vector.tensor_tensor(out=self.split[:, 1, t - 1, :], in0=self.ring[:, (t - 1) % 4, :],
                                                in1=self.split[:, 0, t - 1, :].bitcast(f32),
                                                op=ALU.subtract).then_inc(self.odd_done, 1)
                    if self.add_to is not None and not self.sum_next and t % 2 == 0 and 1 <= t - 1 < tiles:
                        dve.wait_ge(self.scaled, t)
                        nc.vector.tensor_tensor(out=self.add_to[:, t - 1, :], in0=self.add_to[:, t - 1, :],
                                                in1=self.ring[:, (t - 1) % 4, :], op=ALU.add).then_inc(self.odd_done, 1)
                    if self.sum_next and t >= 2:
                        self.accumulate(dve, self.before + t - 2, t - 2)

            def gpsimd(self, pool):
                if self.split is not None:
                    for t in range(0, self.tiles, 2):
                        pool.wait_ge(self.high_done, t + 1)
                        nc.gpsimd.tensor_tensor(out=self.split[:, 1, t, :], in0=self.ring[:, t % 4, :],
                                                in1=self.split[:, 0, t, :].bitcast(f32),
                                                op=ALU.subtract).then_inc(self.even_done, 1)
                if self.add_to is not None:
                    for t in range(0, self.tiles, 1 if self.sum_next else 2):
                        pool.wait_ge(self.scaled, t + 1)
                        nc.gpsimd.tensor_tensor(out=self.add_to[:, t, :], in0=self.add_to[:, t, :],
                                                in1=self.ring[:, t % 4, :], op=ALU.add
                                                ).then_inc(self.added if self.sum_next else self.even_done, 1)

        class SquareSum:

            def __init__(self, s):
                self.squares = s.sbuf("result_squares", [P, 2, T], f32)
                self.squared, self.accumulated = s.sem("result_squared"), s.sem("result_accumulated")

            def start(self, dve):
                nc.vector.memset(square_sum[:], 0.0).then_inc(self.accumulated, 2)

            def square(self, act, n, parity, tile):
                act.wait_ge(self.accumulated, n + 1)
                nc.scalar.activation(self.squares[:, parity:parity + 1, :], tile, ACT.Square).then_inc(self.squared, 1)

            def add(self, dve, n, parity):
                dve.wait_ge(self.squared, n + 1)
                dve.wait_ge(self.accumulated, n + 2)
                nc.vector.tensor_tensor(out=square_sum[:], in0=square_sum[:], in1=self.squares[:, parity, :],
                                        op=ALU.add).then_inc(self.accumulated, 1)

        def norm_of(*what, **how):
            return lambda s: Norm(s, *what, **how)

        def rms_normalize(label, *what, **how):
            with stage(label) as s:
                norm = Norm(s, *what, **how)
                with nc.Block() as block:
                    block.scalar(norm.scalar)
                    block.tensor(norm.tensor)
                    block.vector(norm.vector)
                    block.gpsimd(norm.gpsimd)

        def linear(label, turns, act_in, finish, norm=None, result=None):
            start = weights.start[label]
            tiles0 = weights.tiles_before[start]
            with stage(label) as s:
                norm = norm and norm(s)
                sums = SquareSum(s) if result is not None else None
                bank_free = s.sem("bank_free")
                with nc.Block() as block:
                    @block.sync
                    def _(sp):
                        weights.load_for(sp, label)

                    @block.gpsimd
                    def _(pool):
                        if norm is not None:
                            norm.gpsimd(pool)
                        weights.split_low_all(pool, label)

                    @block.tensor
                    def _(pe):
                        if norm is not None:
                            norm.tensor(pe)
                        with pe.Fori(0, turns) as i:
                            for c in range(2):
                                chunk = Chunk(start + c, i, 2)
                                pe.wait_ge(weights.low_ready, chunk.number + 1)
                                high, low = weights.parts(chunk, DT)
                                for j in (2 * c, 2 * c + 1):
                                    pe.wait_ge(bank_free, i * 4 + (j + 1))
                                    sl = slice((j % 2) * P, (j % 2 + 1) * P)
                                    for k in range(DT):
                                        if j == 0 and norm is not None:
                                            norm.wait_tile(pe, k)
                                        last = product(psum[:, j, :], (high[:, k, sl], low[:, k, sl]),
                                                       (act_in[:, 0, k, :], act_in[:, 1, k, :]), k == 0, k == DT - 1)
                                    last.then_inc(weights.products, 1)

                    @block.scalar
                    def _(act):
                        if norm is not None:
                            norm.scalar(act)
                        with act.Fori(0, turns) as i:
                            for c in range(2):
                                weights.split_high(act, Chunk(start + c + 1, i, 2))
                                for j in (2 * c, 2 * c + 1) if result is not None else ():
                                    act.wait_ge(bank_free, i * 4 + (j + 5))
                                    sums.square(act, i * 4 + j, j % 2, result[:, ds(i * 4 + j, 1), :])

                    @block.vector
                    def _(dve):
                        dve.sem_inc(bank_free, 4)
                        if norm is not None:
                            norm.vector(dve)
                        if result is not None:
                            sums.start(dve)
                        with dve.Fori(0, turns) as i:
                            for j in range(4):
                                dve.wait_ge(weights.products, i * 4 + (tiles0 + j + 1))
                                finish(j, i * 4 + j).then_inc(bank_free, 1)
                                if result is not None:
                                    sums.add(dve, i * 4 + j, j % 2)

        def block_one(memory):
            keep_one = memory.enter_context
            gates = keep_one(nc.sbuf_tensor("gates", [P, 2 * DT, T], f32))
            split = keep_one(nc.sbuf_tensor("block1_split", [P, 2, DT, T], f32r))
            attn = ExitStack()
            with attn:
                def keep(name, shape, dtype=f32):
                    return attn.enter_context(nc.sbuf_tensor(name, shape, dtype))

                q_a = keep("q_a", [P, HEADS, T])
                k_a = keep("k_a", [P, HEADS, T])
                v_a = keep("v_a", [P, TT, HEADS * DV_A])
                qk_b = keep("qk_b", [P, 6, T])
                v_b = keep("v_b", [P, TT, KV_B * HD_B])
                until_rope = ExitStack()
                k_pe = until_rope.enter_context(nc.sbuf_tensor("k_pe", [P, T], f32))

                with ExitStack() as latents:
                    q_lat = latents.enter_context(nc.sbuf_tensor("q_lat", [P, 2, T], f32))
                    kv_lat = latents.enter_context(nc.sbuf_tensor("kv_lat", [P, 1, T], f32))
                    mixer_in(norm_of(x, DT, lambda t: gain("g_mix", t), split=split), split, gates, q_lat, kv_lat, qk_b, v_b, k_pe)
                    q_split, kv_split = split[:, :, 0:2, :], split[:, :, 2:3, :]
                    latent_up(norm_of(q_lat, 2, lambda t: gain("g_qa", t), split=q_split, prefix="query"),
                              norm_of(kv_lat, 1, lambda t: gain("g_kva"), split=kv_split, prefix="key"), q_split, kv_split, q_a, k_a, v_a)
                rope_and_norms(q_a, k_a, k_pe, qk_b)
                until_rope.close()
                attention("attn_a", HEADS // 2, split, 0, q_a, k_a, v_a, DQ_A, DV_A, "latent")
                attention("attn_b", HEADS // 2, split, HEADS // 2, qk_b, qk_b, v_b, HD_B, HD_B, "grouped")
            with nc.sbuf_tensor("merged", [P, 2, DT, T], f32r) as merged:
                merge(split, gates, merged)

                def add_to_x(bank, tile):
                    return nc.vector.tensor_tensor(out=x[:, ds(tile, 1), :], in0=psum[:, bank:bank + 1, :],
                                                   in1=x[:, ds(tile, 1), :], op=ALU.add)

                linear("mixer_out", 2, merged, add_to_x, result=x)
            mlp(norm_of(x, DT, lambda t: gain("g_mlp", t), split=split, given=True), split)
            ple(norm_of(x, DT, lambda t: gain("g_ple", t), split=split, given=True), split, gates)
            rms_normalize("norm_final", x, DT, lambda t: gain("g_final", t), plain=x, given=True, sum_next=True)

        def mixer_in(norm, split, gates, q_lat, kv_lat, qk_b, v_b, k_pe):
            start = weights.start["mixer_in"]
            last_gate = 2 * DT
            with stage("mixer_in") as s:
                norm = norm(s)
                gate_bank_free, bank_free = s.sem("gate_bank_free"), s.sem("bank_free")
                lower, upper = slice(0, HD_B), slice(HD_B, P)
                whole = slice(0, P)
                targets = [[(q_lat[:, n, :], whole)] for n in range(2)] + [[(qk_b[:, n, :], whole)] for n in range(4)]
                targets += [[(qk_b[half, 4 + g, :], (lower, upper)[g]) for g in range(KV_B) for half in (lower, upper)],
                            [(v_b[:], whole)], [(kv_lat[:, 0, :], whole)], [(k_pe[:], whole)]]
                with nc.Block() as block:
                    @block.sync
                    def _(sp):
                        weights.load_for(sp, "mixer_in")

                    @block.gpsimd
                    def _(pool):
                        norm.gpsimd(pool)
                        weights.split_low_all(pool, "mixer_in")

                    @block.tensor
                    def _(pe):
                        norm.tensor(pe)
                        with pe.Fori(0, 4) as i:
                            for c in range(2):
                                chunk = Chunk(start + c, i, 2)
                                pe.wait_ge(weights.low_ready, chunk.number + 1)
                                high, low = weights.parts(chunk, DT)
                                for j in (2 * c, 2 * c + 1):
                                    pe.wait_ge(gate_bank_free, i * 4 + (j + 1))
                                    sl = slice((j % 2) * P, (j % 2 + 1) * P)
                                    for k in range(DT):
                                        if j == 0:
                                            norm.wait_tile(pe, k)
                                        last = product(psum[:, j, :], (high[:, k, sl], low[:, k, sl]),
                                                       (split[:, 0, k, :], split[:, 1, k, :]), k == 0, k == DT - 1)
                                    last.then_inc(weights.products, 1)
                        tile = 0

                        def feature_tile(parts, stationary):
                            nonlocal tile
                            if tile >= 4:
                                pe.wait_ge(bank_free, tile - 3)
                            for k in range(DT):
                                last = product(psum[:, 4 + tile % 4, :], [stationary(x, k) for x in parts],
                                               (split[:, 0, k, :], split[:, 1, k, :]), k == 0, k == DT - 1)
                            last.then_inc(weights.products, 1)
                            tile += 1

                        for c in range(3):
                            pe.wait_ge(weights.low_ready, start + 8 + c + 1)
                            parts = weights.parts(Chunk(start + 8 + c), DT)
                            for m in range(2):
                                feature_tile(parts, lambda x, k: x[:, k, m * P:(m + 1) * P])
                        pe.wait_ge(weights.low_ready, start + 12)
                        parts = weights.parts(Chunk(start + 11), DT)
                        feature_tile(parts, lambda x, k: x[:, k, 0:P])
                        pe.wait_ge(bank_free, tile - 3)
                        for j in range(TT):
                            for k in range(DT):
                                token = [split[:, n, k, j * P:(j + 1) * P] for n in range(2)]
                                last = product(psum[:, 4 + tile % 4, j * P:(j + 1) * P], token,
                                               [x[:, k, P:2 * P] for x in parts], k == 0, k == DT - 1)
                        last.then_inc(weights.products, 1)
                        tile += 1
                        pe.wait_ge(weights.low_ready, start + 13)
                        parts = weights.parts(Chunk(start + 12), DT)
                        feature_tile(parts, lambda x, k: x[:, k, 0:KV_LORA])
                        feature_tile(parts, lambda x, k: x[:, k, KV_LORA - NOPE:KV_LORA - NOPE + P])

                    @block.scalar
                    def _(act):
                        act.sem_inc(gate_bank_free, 4)
                        norm.scalar(act)
                        with act.Fori(0, 4) as i:
                            for c in range(2):
                                weights.split_high(act, Chunk(start + c + 1, i, 2))
                                for j in (2 * c, 2 * c + 1):
                                    act.wait_ge(weights.products, i * 4 + (j + 1))
                                    nc.scalar.activation(gates[:, ds(i * 4 + j, 1), :], psum[:, j:j + 1, :], ACT.Tanh,
                                                         scale=0.5).then_inc(gate_bank_free, 1)
                        for c in range(5):
                            weights.split_high(act, Chunk(start + 9 + c))

                    @block.vector
                    def _(dve):
                        norm.vector(dve)
                        for n, target in enumerate(targets):
                            dve.wait_ge(weights.products, last_gate + n + 1)
                            for to, rows in target:
                                source = psum[rows, 4 + n % 4, :]
                                if n == 7:
                                    source = source.rearrange("p (j c) -> p j c", j=TT)
                                last = nc.vector.tensor_copy(to, source)
                            last.then_inc(bank_free, 1)

        def latent_up(query_norm, key_norm, q_split, kv_split, q_a, k_a, v_a):
            start = weights.start["latent_up"]
            tiles0 = weights.tiles_before[start]
            with stage("latent_up") as s:
                bank_free = s.sem("bank_free")
                norms = (query_norm(s), key_norm(s))
                with nc.Block() as block:
                    @block.sync
                    def _(sp):
                        weights.load_for(sp, "latent_up")

                    @block.gpsimd
                    def _(pool):
                        for norm in norms:
                            norm.gpsimd(pool)
                        weights.split_low_all(pool, "latent_up")

                    @block.scalar
                    def _(act):
                        for norm in norms:
                            norm.scalar(act)
                        for c in range(2):
                            weights.split_high(act, Chunk(start + c + 1))

                    @block.tensor
                    def _(pe):
                        for norm in norms:
                            norm.tensor(pe)
                        tile = 0
                        pe.wait_ge(weights.low_ready, start + 1)
                        parts = weights.parts(Chunk(start), 2)
                        for h in range(HEADS):
                            if tile >= 4:
                                pe.wait_ge(bank_free, tile - 3)
                            for k in range(2):
                                if h == 0:
                                    norms[0].wait_tile(pe, k)
                                last = product(psum[0:DQ_A, tile % 4, :],
                                               [y[:, k, h * DQ_A:(h + 1) * DQ_A] for y in parts],
                                               (q_split[:, 0, k, :], q_split[:, 1, k, :]), k == 0, k == 1)
                            last.then_inc(weights.products, 1)
                            tile += 1
                        pe.wait_ge(weights.low_ready, start + 2)
                        parts = weights.parts(Chunk(start + 1), 1)
                        norms[1].wait_tile(pe, 0)
                        latent = (kv_split[:, 0, 0, :], kv_split[:, 1, 0, :])
                        for h in range(HEADS):
                            pe.wait_ge(bank_free, tile - 3)
                            at = h * (NOPE + DV_A)
                            last = product(psum[:, tile % 4, :], [y[:, 0, at:at + P] for y in parts],
                                           latent, True, True)
                            last.then_inc(weights.products, 1)
                            tile += 1
                        for j in range(TT):
                            pe.wait_ge(bank_free, tile - 3)
                            last = product(psum[:, tile % 4, :].rearrange("p (h c) -> p h c", h=HEADS),
                                           [y[:, j * P:(j + 1) * P] for y in latent],
                                           [y[:, 0, :].rearrange("p (h c) -> p h c", h=HEADS)[:, :, NOPE:NOPE + DV_A]
                                            for y in parts], True, True)
                            last.then_inc(weights.products, 1)
                            tile += 1

                    @block.vector
                    def _(dve):
                        for norm in norms:
                            norm.vector(dve)
                        tile = 0
                        for target, rows in ((q_a, DQ_A), (k_a, NOPE)):
                            for h in range(HEADS):
                                dve.wait_ge(weights.products, tiles0 + tile + 1)
                                nc.vector.tensor_copy(target[0:rows, h, :], psum[0:rows, tile % 4, :]).then_inc(bank_free, 1)
                                tile += 1
                        for j in range(TT):
                            dve.wait_ge(weights.products, tiles0 + tile + 1)
                            nc.vector.tensor_copy(v_a[:, j, :], psum[:, tile % 4, :]).then_inc(bank_free, 1)
                            tile += 1

        def rope_and_norms(q_a, k_a, k_pe, qk_b):
            with stage("rope") as s:
                table = s.sbuf("table", [P, 4, T], f32)
                squares = s.sbuf("squares", [P, 2, T], f32)
                stat = s.sbuf("stat", [P, 3, 6 * TT * 2], f32)
                turned = s.sbuf("turned", [P, 2, T], f32)
                table_in, squared, summed, mean, root, rstd = [s.sem(n) for n in (
                    "table_in", "squared", "summed", "mean", "root", "rstd")]
                spread, normed, rotated, rotation_read = [s.sem(n) for n in (
                    "spread", "normed", "rotated", "rotation_read")]
                scaled, key_roped, turned_ready = s.sem("scaled"), s.sem("key_roped"), s.sem("turned_ready")
                in_place = s.sem("in_place")
                n_a = HEADS + 1
                jobs = [(q_a[0:DQ_A, h, :], DQ_A, 0, DQ_A ** -0.5) for h in range(HEADS)]
                jobs += [(k_pe[:], P, 0, 1.0)]
                jobs += [(qk_b[:, n, :], P, 2, HD_B ** -0.5 if n < 4 else 1.0) for n in range(6)]
                with nc.Block() as block:
                    @block.sync
                    def _(sp):
                        sp.dma_start(table[:], tables.rearrange("n p t -> p n t")).then_inc(table_in, 16)

                    @block.scalar
                    def _(act):
                        for n in range(6):
                            if n >= 2:
                                act.wait_ge(summed, n - 1)
                            nc.scalar.activation(squares[:, n % 2, :], qk_b[:, n, :], ACT.Square).then_inc(squared, 1)
                        act.wait_ge(mean, 1)
                        nc.scalar.activation(stat[:, 1, :], stat[:, 0, :], ACT.Sqrt).then_inc(root, 1)

                    @block.tensor
                    def _(pe):
                        for n in range(6):
                            pe.wait_ge(squared, n + 1)
                            for j in range(TT):
                                at = (n * TT + j) * 2
                                last = nc.tensor.matmul(psum[:, 0, at:at + 2], squares[:, n % 2, j * P:(j + 1) * P],
                                                        constant("heads_of_pair"), start=True, stop=True)
                            last.then_inc(summed, 1)

                        def rotate_tile(n):
                            tile, rows, _, _ = jobs[n]
                            if n >= 2:
                                pe.wait_ge(rotation_read, n - 1)
                            nc.tensor.matmul(psum[0:rows, 1 + n % 2, :], rotate[0:rows, 0:rows], tile,
                                             start=True, stop=True).then_inc(rotated, 1)

                        for n in range(n_a):
                            rotate_tile(n)
                        pe.wait_ge(rstd, 1)
                        for n in range(6):
                            if n >= 2:
                                pe.wait_ge(normed, n - 1)
                            for j in range(TT):
                                at = (n * TT + j) * 2
                                for half in range(2):
                                    last = nc.tensor.matmul(psum[half * HD_B:(half + 1) * HD_B, 3 + n % 2, j * P:(j + 1) * P],
                                                            stat[:, 2, at + half:at + half + 1].broadcast_to([P, HD_B]),
                                                            identity, start=True, stop=True)
                            last.then_inc(spread, 1)
                        for n in range(6):
                            pe.wait_ge(normed, n + 1)
                            rotate_tile(n_a + n)

                    @block.vector
                    def _(dve):
                        dve.wait_ge(summed, 6)
                        nc.vector.tensor_scalar(stat[:, 0, :], psum[:, 0, 0:6 * TT * 2], 1.0 / HD_B, EPS,
                                                ALU.mult, ALU.add).then_inc(mean, 1)
                        dve.wait_ge(root, 1)
                        nc.vector.reciprocal(stat[:, 2, :], stat[:, 1, :]).then_inc(rstd, 1)
                        dve.wait_ge(table_in, 16)

                        def rope_tile(n):
                            tile, rows, at, scale = jobs[n]
                            buffer = turned[0:rows, n % 2, :]
                            if n >= 2:
                                dve.wait_ge(in_place, n - 1)
                            dve.wait_ge(rotated, n + 1)
                            nc.vector.scalar_tensor_tensor(out=buffer, in0=psum[0:rows, 1 + n % 2, :], scalar=scale,
                                                           in1=table[0:rows, at + 1, :], op0=ALU.mult,
                                                           op1=ALU.mult).then_inc(rotation_read, 1)
                            nc.vector.scalar_tensor_tensor(out=tile, in0=tile, scalar=scale, in1=table[0:rows, at, :],
                                                           op0=ALU.mult, op1=ALU.mult).then_inc(scaled, 1)
                            dve.wait_ge(rotation_read, n + 1)
                            dve.wait_ge(scaled, n + 1)
                            nc.vector.tensor_tensor(out=tile, in0=tile, in1=buffer, op=ALU.add).then_inc(in_place, 1)

                        for n in range(HEADS + 1):
                            rope_tile(n)
                        for n in range(6):
                            dve.wait_ge(spread, n + 1)
                            tile = qk_b[:, n, :]
                            nc.vector.scalar_tensor_tensor(out=tile, in0=tile, scalar=gain("g_qn" if n < 4 else "g_kn"),
                                                           in1=psum[:, 3 + n % 2, :], op0=ALU.mult,
                                                           op1=ALU.mult).then_inc(normed, 1)
                        for n in range(n_a, n_a + 6):
                            rope_tile(n)

                    @block.gpsimd
                    def _(pool):
                        pool.wait_ge(in_place, n_a)
                        for h in range(HEADS):
                            nc.gpsimd.tensor_copy(k_a[NOPE:DQ_A, h, :], k_pe[NOPE:DQ_A, :])

        class Pair:

            def __init__(self, first, i=None):
                self.first, self.i, self.parity = first, i, first % 2

            def count(self, each, plus=0):
                if self.i is None:
                    return self.first * each + plus
                return self.i * (2 * each) + (self.first * each + plus)

            def following(self):
                return Pair(self.first + 1, self.i)

            def previous(self):
                return Pair(self.first - 1, self.i)

            def is_first(self):
                return self.i is None and self.first == 0

        def attention(label, pairs, out_split, out_base, q, k, v, rows, width_v, kind, decay=None):
            latent, forget = kind == "latent", kind == "forget"
            units = 2 * TT
            ahead = 3
            with stage(label) as s:
                q_st = s.sbuf("q_st", [P, 2, 2, T], f32)
                v_st = s.sbuf("v_st", [P, 2, TT, P], f32)
                prob = s.sbuf("prob", [P, 4, T], f32)
                prob_t = s.sbuf("prob_t", [P, 2, TT, T], f32)
                small = s.sbuf("small", [P, 3, units], f32)
                diagonal = square_sum[:].rearrange("p (n c) -> p n c", n=4)
                names = ["q_staged", "v_staged", "scored", "max_ready", "exp_ready", "sum_inverted",
                         "prob_ready", "turned", "turned_read", "attended", "high_ready", "stored"]
                (q_staged, v_staged, scored, max_ready, exp_ready, sum_inverted,
                 prob_ready, turned, turned_read, attended, high_ready, stored) = [s.sem(n) for n in names]
                zeroed = s.sem("zeroed")
                if forget:
                    rows_, cols_ = decay
                    picked = s.sbuf("picked", [P, 2, T], f32)
                    c_col = s.sbuf("c_col", [P, 2, TT, 2], f32)
                    minus_c = s.sbuf("minus_c", [P, 2, T], f32)
                    decayed = s.sbuf("decayed", [P, 4, T], f32)
                    score_read, picked_ready, column_ready, decay_spread, decay_ready = [s.sem(n) for n in (
                        "score_read", "picked_ready", "column_ready", "decay_spread", "decay_ready")]

                def all_pairs(engine, pair):
                    pair(Pair(0), False)
                    with engine.Fori(0, (pairs - 2) // 2) as i:
                        pair(Pair(1, i), False)
                        pair(Pair(2, i), False)
                    pair(Pair(pairs - 1), True)

                def keys(qt):
                    return (qt + 1) * P if forget else T

                contracted = rows if latent else P

                def query(pair, head, qt):
                    return q_st[0:contracted, pair.parity, head, qt * P:(qt + 1) * P]

                def key(pair, head, n):
                    if latent:
                        tile = pair.count(2, head)
                    elif forget:
                        tile = pair.count(1)
                    else:
                        tile = pair.count(1) // 2 + HEADS // 2
                    return k[0:contracted, ds(tile, 1), 0:n]

                with nc.Block() as block:
                    @block.gpsimd
                    def _(pool):
                        def pair_of(p, _):
                            if not p.is_first():
                                pool.wait_ge(scored, p.previous().count(units, 1))
                            if latent:
                                nc.gpsimd.tensor_copy(q_st[0:rows, p.parity], q[0:rows, ds(p.count(2), 2), :]).then_inc(q_staged, 2)
                            else:
                                for head in range(2):
                                    at = slice(head * rows, (head + 1) * rows)
                                    nc.gpsimd.tensor_copy(q_st[at, p.parity, head:head + 1, :],
                                                          q[at, ds(p.count(1), 1), :]).then_inc(q_staged, 1)
                                    pool.wait_ge(q_staged, p.count(2, head + 1))
                            if forget:
                                for head in range(2):
                                    if not p.is_first():
                                        pool.wait_ge(decay_spread, p.previous().count(2, head + 1))
                                    own = identity[0:FOX_HEADS, ds(p.count(2, head), 1)].broadcast_to([FOX_HEADS, T])
                                    nc.gpsimd.tensor_tensor(out=picked[0:FOX_HEADS, head, :], in0=rows_[:], in1=own,
                                                            op=ALU.mult).then_inc(picked_ready, 1)
                                    if head == 0:
                                        if not p.is_first():
                                            pool.wait_ge(score_read, p.previous().count(units, 1))
                                        nc.gpsimd.tensor_copy(c_col[:, p.parity], cols_[:, :, ds(p.count(2), 2)]
                                                              ).then_inc(column_ready, 1)
                            if not p.is_first():
                                pool.wait_ge(attended, p.previous().count(2, 1))
                            if kind == "grouped":
                                at = p.count(1) // 2 * width_v
                                nc.gpsimd.tensor_copy(v_st[:, p.parity, :, 0:width_v], v[:, :, ds(at, width_v)]
                                                      ).then_inc(v_staged, 1)
                            else:
                                nc.gpsimd.tensor_copy(v_st[:, p.parity], v[:, :, ds(p.count(P), P)]).then_inc(v_staged, 1)

                        if not latent:
                            nc.gpsimd.memset(q_st[:], 0.0).then_inc(zeroed, 1)
                            pool.wait_ge(zeroed, 1)
                        if forget:
                            nc.gpsimd.memset(picked[:], 0.0).then_inc(zeroed, 1)
                            pool.wait_ge(zeroed, 2)
                        all_pairs(pool, pair_of)

                    @block.tensor
                    def _(pe):
                        def score(p, u):
                            head, qt = divmod(u, TT)
                            if u == 0:
                                pe.wait_ge(q_staged, p.count(2, 2))
                            if not p.is_first() or u >= 4:
                                pe.wait_ge(score_read if forget else exp_ready, p.count(units, u - 3))
                            mm = nc.tensor.matmul(psum[:, u % 4:u % 4 + 1, 0:keys(qt)], query(p, head, qt),
                                                  key(p, head, keys(qt)), start=True, stop=not forget)
                            if forget:
                                mm = nc.tensor.matmul(psum[:, u % 4, qt * P:(qt + 1) * P], identity,
                                                      constant("causal_bias"), start=False, stop=True)
                            mm.then_inc(scored, 1)

                        def spread(p, head):
                            pe.wait_ge(picked_ready, p.count(2, head + 1))
                            if not p.is_first() or head:
                                pe.wait_ge(decay_ready, p.count(2, head))
                            nc.tensor.matmul(psum[:, 7, :], ones.broadcast_to([P, P]),
                                             picked[:, head, :], start=True, stop=True).then_inc(decay_spread, 1)

                        def turn(p, u):
                            head, qt = divmod(u, TT)
                            pe.wait_ge(prob_ready, p.count(units, u + 1))
                            if not p.is_first() or u >= 2:
                                pe.wait_ge(turned_read, p.count(units, u - 1))
                            for kt in range(keys(qt) // P):
                                target, source = psum[:, 4 + u % 2, kt * P:(kt + 1) * P], prob[:, u % 4, kt * P:(kt + 1) * P]
                                if forget:
                                    mm = nc.tensor.matmul(target, source, diagonal[:, u % 4, :], start=True, stop=True)
                                else:
                                    mm = nc.tensor.transpose(target, source, identity)
                            mm.then_inc(turned, 1)

                        def attend(p, head):
                            pe.wait_ge(turned_read, p.count(units, (head + 1) * TT))
                            if head == 0:
                                pe.wait_ge(v_staged, p.count(1, 1))
                                if not p.is_first():
                                    pe.wait_ge(stored, p.count(1))
                            for kt in range(TT):
                                at = kt * P if forget else 0
                                v_at = 0 if kind == "grouped" else head * width_v
                                mm = nc.tensor.matmul(psum[head * width_v:(head + 1) * width_v, 6, at:T],
                                                      v_st[:, p.parity, kt, v_at:v_at + width_v], prob_t[:, head, kt, at:T],
                                                      start=(kt == 0), stop=(kt == TT - 1))
                            mm.then_inc(attended, 1)

                        def pair_of(p, last):
                            if p.is_first():
                                if forget:
                                    spread(p, 0)
                                for u in range(ahead):
                                    score(p, u)
                            for u in range(units):
                                if u + ahead < units:
                                    score(p, u + ahead)
                                elif not last:
                                    score(p.following(), u + ahead - units)
                                turn(p, u)
                                if u == 1:
                                    if forget:
                                        spread(p, 1)
                                    if not p.is_first():
                                        attend(p.previous(), 1)
                                if u == TT:
                                    attend(p, 0)
                                if u == TT + 1 and forget and not last:
                                    spread(p.following(), 0)
                            if last:
                                attend(p, 1)

                        all_pairs(pe, pair_of)

                    @block.vector
                    def _(dve):
                        def normalize(p, u):
                            dve.wait_ge(exp_ready, p.count(units, u + 1))
                            nc.vector.reciprocal(small[:, 2, u:u + 1], small[:, 1, u:u + 1]).then_inc(sum_inverted, 1)
                            dve.wait_ge(sum_inverted, p.count(units, u + 1))
                            if forget:
                                if not p.is_first() or u >= 4:
                                    dve.wait_ge(turned, p.count(units, u - 3))
                                target, source = diagonal[:, u % 4, :], identity
                            else:
                                target = source = prob[:, u % 4, :]
                            nc.vector.tensor_scalar(target, source, small[:, 2, u:u + 1], None,
                                                    ALU.mult).then_inc(prob_ready, 1)

                        def finish(p):
                            dve.wait_ge(high_ready, p.count(1, 1))
                            at = ds(p.count(1, out_base), 1)
                            nc.vector.tensor_tensor(out=out_split[:, 1, at, :], in0=psum[:, 6:7, :],
                                                    in1=out_split[:, 0, at, :].bitcast(f32),
                                                    op=ALU.subtract).then_inc(stored, 1)

                        def pair_of(p, last):
                            for u in range(units):
                                head, qt = divmod(u, TT)
                                dve.wait_ge(scored, p.count(units, u + 1))
                                source = psum[:, u % 4, 0:keys(qt)]
                                if forget:
                                    if u == 0:
                                        dve.wait_ge(column_ready, p.count(1, 1))
                                    if qt == 0:
                                        dve.wait_ge(decay_ready, p.count(2, head + 1))
                                    nc.vector.scalar_tensor_tensor(out=decayed[:, u % 4, 0:keys(qt)], in0=source,
                                                                   scalar=c_col[:, p.parity, qt, head:head + 1],
                                                                   in1=minus_c[:, head, 0:keys(qt)], op0=ALU.add,
                                                                   op1=ALU.add).then_inc(score_read, 1)
                                    dve.wait_ge(score_read, p.count(units, u + 1))
                                    source = decayed[:, u % 4, 0:keys(qt)]
                                nc.vector.tensor_reduce(small[:, 0, u:u + 1], source, AX.X, ALU.max,
                                                        negate=True).then_inc(max_ready, 1)
                                if u >= 1:
                                    normalize(p, u - 1)
                                elif not p.is_first():
                                    normalize(p.previous(), units - 1)
                                if u == 3 and not p.is_first():
                                    finish(p.previous())
                            if last:
                                normalize(p, units - 1)
                                finish(p)

                        all_pairs(dve, pair_of)

                    @block.scalar
                    def _(act):
                        def read_turned(p, u):
                            head, qt = divmod(u, TT)
                            n = keys(qt) // P
                            act.wait_ge(turned, p.count(units, u + 1))
                            if qt == 0 and not p.is_first():
                                act.wait_ge(attended, p.previous().count(2, head + 1))
                            nc.scalar.copy(prob_t[:, head, 0:n, qt * P:(qt + 1) * P],
                                           psum[:, 4 + u % 2, 0:n * P].rearrange("p (k c) -> p k c", k=n)
                                           ).then_inc(turned_read, 1)

                        def copy_decay(p, head):
                            act.wait_ge(decay_spread, p.count(2, head + 1))
                            if not p.is_first():
                                act.wait_ge(score_read, p.previous().count(units, (head + 1) * TT))
                            nc.scalar.activation(minus_c[:, head, :], psum[:, 7, :], ACT.Copy,
                                                 scale=-1.0).then_inc(decay_ready, 1)

                        def finish(p):
                            act.wait_ge(attended, p.count(2, 2))
                            nc.scalar.copy(out_split[:, 0, ds(p.count(1, out_base), 1), :],
                                           psum[:, 6:7, :]).then_inc(high_ready, 1)

                        def pair_of(p, last):
                            if p.is_first() and forget:
                                copy_decay(p, 0)
                            for u in range(units):
                                head, qt = divmod(u, TT)
                                act.wait_ge(max_ready, p.count(units, u + 1))
                                if not p.is_first() or u >= 4:
                                    act.wait_ge(turned, p.count(units, u - 3))
                                source = decayed[:, u % 4, 0:keys(qt)] if forget else psum[:, u % 4, :]
                                e = nc.scalar.activation(prob[:, u % 4, 0:keys(qt)], source, ACT.Exp,
                                                         bias=small[:, 0, u:u + 1], accum_out=small[:, 1, u:u + 1])
                                e.then_inc(exp_ready, 1)
                                if u >= 1:
                                    read_turned(p, u - 1)
                                elif not p.is_first():
                                    read_turned(p.previous(), units - 1)
                                if u == 2 and forget:
                                    copy_decay(p, 1)
                                if u == 2 and not p.is_first():
                                    finish(p.previous())
                                if u == 6 and forget and not last:
                                    copy_decay(p.following(), 0)
                            if last:
                                read_turned(p, units - 1)
                                finish(p)

                        all_pairs(act, pair_of)

        def merge(attended, gates, merged):
            start = weights.start["merge"]
            tiles0 = weights.tiles_before[start]
            with stage("merge") as s:
                part = s.sbuf("part", [P, 2, 4, T], f32)
                product_read, summed, high_ready = s.sem("product_read"), s.sem("summed"), s.sem("high_ready")
                parts_ready, low_done = s.sem("parts_ready"), s.sem("low_done")
                with nc.Block() as block:
                    @block.sync
                    def _(sp):
                        weights.load_for(sp, "merge")

                    @block.gpsimd
                    def _(pool):
                        weights.split_low_all(pool, "merge")

                    @block.tensor
                    def _(pe):
                        with pe.Fori(0, 2) as i:
                            for c in range(2):
                                chunk = Chunk(start + c, i, 2)
                                pe.wait_ge(weights.low_ready, chunk.number + 1)
                                high, low = weights.parts(chunk, 4)
                                for m in range(4):
                                    pe.wait_ge(product_read, i * 8 + 1)
                                    sl = slice(m * P, (m + 1) * P)
                                    for k in range(4):
                                        a = 4 * c + k
                                        last = product(psum[:, 4 * c + m, :], (high[:, k, sl], low[:, k, sl]),
                                                       (attended[:, 0, a, :], attended[:, 1, a, :]), k == 0, k == 3)
                                    last.then_inc(weights.products, 1)

                    @block.scalar
                    def _(act):
                        act.sem_inc(high_ready, 1)
                        with act.Fori(0, 2) as i:
                            for c in range(2):
                                weights.split_high(act, Chunk(start + c + 1, i, 2))
                            for m in range(4):
                                act.wait_ge(summed, i * 4 + (m + 1))
                                nc.scalar.activation(merged[:, 0, ds(i * 4 + m, 1), :], part[:, 0, m:m + 1, :], ACT.Copy,
                                                     scale=0.5).then_inc(high_ready, 1)

                    @block.vector
                    def _(dve):
                        dve.sem_inc(product_read, 1)
                        dve.sem_inc(low_done, 1)
                        with dve.Fori(0, 2) as i:
                            for c in range(2):
                                for m in range(4):
                                    dve.wait_ge(weights.products, i * 8 + (tiles0 + 4 * c + m + 1))
                                    if c == 0 and m == 0:
                                        dve.wait_ge(high_ready, i * 4 + 1)
                                        dve.wait_ge(low_done, i * 4 + 1)
                                    nc.vector.scalar_tensor_tensor(out=part[:, c, m:m + 1, :],
                                                                   in0=gates[:, ds(i * 4 + (DT * c + m), 1), :], scalar=1.0,
                                                                   in1=psum[:, 4 * c + m:4 * c + m + 1, :], op0=ALU.add,
                                                                   op1=ALU.mult).then_inc(product_read, 1)
                            for m in range(4):
                                dve.wait_ge(product_read, i * 8 + (6 + m))
                                nc.vector.tensor_tensor(out=part[:, 0, m, :], in0=part[:, 0, m, :], in1=part[:, 1, m, :],
                                                        op=ALU.add).then_inc(summed, 1)
                            for m in range(4):
                                dve.wait_ge(high_ready, i * 4 + (m + 2))
                                nc.vector.scalar_tensor_tensor(out=merged[:, 1, ds(i * 4 + m, 1), :], in0=part[:, 0, m:m + 1, :],
                                                               scalar=0.5, in1=merged[:, 0, ds(i * 4 + m, 1), :].bitcast(f32),
                                                               op0=ALU.mult, op1=ALU.subtract).then_inc(low_done, 1)

        def mlp(norm, split):
            start = weights.start["mlp"]
            tiles0 = weights.tiles_before[start]
            blocks = D_FF // 256
            with stage("mlp") as s:
                norm = norm(s)
                sums = SquareSum(s)
                hidden = s.sbuf("hidden", [P, 2, 2, 2, T], f32r)
                relu = s.sbuf("relu", [P, 2, T], f32)
                square = s.sbuf("square", [P, 2, T], f32)
                rectified, squared, high_ready, hidden_ready, added = [s.sem(n) for n in (
                    "rectified", "squared", "high_ready", "hidden_ready", "added")]

                with nc.Block() as block:
                    @block.sync
                    def _(sp):
                        weights.load_for(sp, "mlp")

                    @block.gpsimd
                    def _(pool):
                        norm.gpsimd(pool)
                        weights.split_low_all(pool, "mlp")

                    @block.tensor
                    def _(pe):
                        norm.tensor(pe)
                        def up(chunk, t, parity):
                            pe.wait_ge(weights.low_ready, chunk.number + 1)
                            high, low = weights.parts(chunk, DT)
                            for m in range(2):
                                if not isinstance(t, int) or t >= 1:
                                    pe.wait_ge(rectified, t * 2 + (m - 1))
                                sl = slice(m * P, (m + 1) * P)
                                for k in range(DT):
                                    if isinstance(t, int) and t == m == 0:
                                        norm.wait_tile(pe, k)
                                    last = product(psum[:, m, :], (high[:, k, sl], low[:, k, sl]),
                                                   (split[:, 0, k, :], split[:, 1, k, :]), k == 0, k == DT - 1)
                                last.then_inc(weights.products, 1)

                        def down(chunk, t, parity):
                            pe.wait_ge(weights.low_ready, chunk.number + 1)
                            high, low = weights.parts(chunk, 2)
                            pe.wait_ge(hidden_ready, t * 2 + 2)
                            for m in range(DT):
                                if not isinstance(t, int) or t * DT + m >= 4:
                                    pe.wait_ge(added, t * DT + (m - 3))
                                sl = slice(m * P, (m + 1) * P)
                                for k in range(2):
                                    last = product(psum[:, 4 + m % 4, :], (high[:, k, sl], low[:, k, sl]),
                                                   (hidden[:, parity, 0, k, :], hidden[:, parity, 1, k, :]),
                                                   k == 0, k == 1)
                                last.then_inc(weights.products, 1)

                        up(Chunk(start), 0, 0)
                        up(Chunk(start + 1), 1, 1)
                        down(Chunk(start + 2), 0, 0)
                        with pe.Fori(0, (blocks - 2) // 2) as i:
                            for b in range(2):
                                up(Chunk(start + 3 + 2 * b, i, 4), i * 2 + (2 + b), b)
                                down(Chunk(start + 4 + 2 * b, i, 4), i * 2 + (1 + b), (1 + b) % 2)
                        down(Chunk(start + 2 * blocks - 1), blocks - 1, 1)

                    @block.scalar
                    def _(act):
                        norm.scalar(act)
                        def high(t, parity):
                            base = t * 10 + (tiles0 - 8) if not isinstance(t, int) or t else tiles0
                            for m in range(2):
                                act.wait_ge(weights.products, base + (m + 1))
                                if not isinstance(t, int) or t >= 1:
                                    act.wait_ge(squared, t * 2 + (m - 1))
                                nc.scalar.activation(relu[:, m, :], psum[:, m, :], ACT.Relu).then_inc(rectified, 1)
                            for m in range(2):
                                act.wait_ge(squared, t * 2 + (m + 1))
                                nc.scalar.copy(hidden[:, parity, 0, m, :], square[:, m, :]).then_inc(high_ready, 1)

                        weights.split_high(act, Chunk(start + 1))
                        weights.split_high(act, Chunk(start + 2))
                        high(0, 0)
                        weights.split_high(act, Chunk(start + 3))
                        high(1, 1)
                        with act.Fori(0, (blocks - 2) // 2) as i:
                            for b in range(2):
                                weights.split_high(act, Chunk(start + 4 + 2 * b, i, 4))
                                weights.split_high(act, Chunk(start + 5 + 2 * b, i, 4))
                                high(i * 2 + (2 + b), b)
                        weights.split_high(act, Chunk(start + 2 * blocks))
                        for m in range(DT):
                            act.wait_ge(added, (blocks - 1) * DT + m + 1)
                            sums.square(act, m, m % 2, x[:, m:m + 1, :])

                    @block.vector
                    def _(dve):
                        norm.vector(dve)
                        def hide(t, parity):
                            for m in range(2):
                                dve.wait_ge(rectified, t * 2 + (m + 1))
                                if not isinstance(t, int) or t >= 1:
                                    dve.wait_ge(hidden_ready, t * 2 + (m - 1))
                                nc.vector.tensor_tensor(out=square[:, m, :], in0=relu[:, m, :], in1=relu[:, m, :],
                                                        op=ALU.mult).then_inc(squared, 1)
                            for m in range(2):
                                dve.wait_ge(high_ready, t * 2 + (m + 1))
                                nc.vector.tensor_tensor(out=hidden[:, parity, 1, m, :], in0=square[:, m, :],
                                                        in1=hidden[:, parity, 0, m, :].bitcast(f32),
                                                        op=ALU.subtract).then_inc(hidden_ready, 1)

                        def accumulate(t):
                            last = isinstance(t, int) and t == blocks - 1
                            base = tiles0 + 10 * t + (2 if last else 4) if isinstance(t, int) else t * 10 + (tiles0 + 4)
                            for m in range(DT):
                                dve.wait_ge(weights.products, base + (m + 1))
                                nc.vector.tensor_tensor(out=x[:, m, :], in0=psum[:, 4 + m % 4, :], in1=x[:, m, :],
                                                        op=ALU.add).then_inc(added, 1)
                                if last and m >= 1:
                                    sums.add(dve, m - 1, (m - 1) % 2)

                        hide(0, 0)
                        hide(1, 1)
                        accumulate(0)
                        with dve.Fori(0, (blocks - 2) // 2) as i:
                            for b in range(2):
                                accumulate(i * 2 + (1 + b))
                                hide(i * 2 + (2 + b), b)
                        sums.start(dve)
                        accumulate(blocks - 1)
                        sums.add(dve, DT - 1, (DT - 1) % 2)

        def ple(norm, split, scratch):
            start = weights.start["ple"]
            tiles0 = weights.tiles_before[start]
            with stage("ple_in") as s:
                p_rows = s.sbuf("p_rows", [P, TT, 2 * P], f32)
                p_split = s.sbuf("p_split", [P, 2, 2, T], f32r)
                p_in, turned, high_ready = s.sem("p_in"), s.sem("turned"), s.sem("high_ready")
                bank_free = s.sem("bank_free")
                low_ready = s.sem("low_ready")
                with nc.Block() as block:
                    @block.sync
                    def _(sp):
                        sp.dma_start(p_rows[:], w["p"][0, 0].rearrange("(j q) c -> q j c", q=P)).then_inc(p_in, 16)
                        weights.load(sp, Chunk(start + 2), weights.plan_item("ple", 2), 0)

                    @block.gpsimd
                    def _(pool):
                        weights.split_low(pool, Chunk(start + 1))

                    @block.scalar
                    def _(act):
                        for t in range(2):
                            act.wait_ge(turned, t + 1)
                            nc.scalar.copy(p_split[:, 0, t, :], psum[:, t, :]).then_inc(high_ready, 1)
                        weights.split_high(act, Chunk(start + 1))

                    @block.tensor
                    def _(pe):
                        pe.wait_ge(p_in, 16)
                        for t in range(2):
                            for j in range(TT):
                                last = nc.tensor.transpose(psum[:, t, j * P:(j + 1) * P], p_rows[:, j, t * P:(t + 1) * P],
                                                           identity)
                            last.then_inc(turned, 1)
                        pe.wait_ge(low_ready, 2)
                        pe.wait_ge(weights.low_ready, start + 1)
                        parts = weights.parts(Chunk(start), 2)
                        for m in range(DT):
                            if m >= 4:
                                pe.wait_ge(bank_free, m - 3)
                            for k in range(2):
                                last = product(psum[:, 4 + m % 4, :], [y[:, k, m * P:(m + 1) * P] for y in parts],
                                               (p_split[:, 0, k, :], p_split[:, 1, k, :]), k == 0, k == 1)
                            last.then_inc(weights.products, 1)

                    @block.vector
                    def _(dve):
                        for t in range(2):
                            dve.wait_ge(high_ready, t + 1)
                            nc.vector.tensor_tensor(out=p_split[:, 1, t, :], in0=psum[:, t, :],
                                                    in1=p_split[:, 0, t, :].bitcast(f32), op=ALU.subtract).then_inc(low_ready, 1)
                        for m in range(DT):
                            dve.wait_ge(weights.products, tiles0 + m + 1)
                            nc.vector.tensor_scalar(scratch[:, m, :], psum[:, 4 + m % 4, :], 0.5, None,
                                                    ALU.mult).then_inc(bank_free, 1)

            start1 = start + 1
            with stage("ple") as s:
                norm = norm(s)
                sums = SquareSum(s)
                gated = s.sbuf("gated", [P, 2, T], f32)
                handed = s.sbuf("handed", [P, 4, T], f32)
                tile_ready, bank_free, product_ready = s.sem("tile_ready"), s.sem("bank_free"), s.sem("product_ready")
                with nc.Block() as block:
                    @block.sync
                    def _(sp):
                        for n in (3, 4):
                            weights.load(sp, Chunk(start + n), weights.plan_item("ple", n), 0)
                        weights.load_segments(sp, start + 5, [(1, weights.after_two(dict(weights.plan)["gdn_in"])[0])])

                    @block.gpsimd
                    def _(pool):
                        norm.gpsimd(pool)
                        for n in range(4):
                            weights.split_low(pool, Chunk(start1 + n + 1))

                    @block.tensor
                    def _(pe):
                        norm.tensor(pe)
                        for n in range(4):
                            pe.wait_ge(weights.low_ready, start1 + n + 1)
                            high, low = weights.parts(Chunk(start1 + n), DT)
                            for m in range(2):
                                tile = 2 * n + m
                                if tile >= 4:
                                    pe.wait_ge(bank_free, tile - 3)
                                sl = slice(m * P, (m + 1) * P)
                                for k in range(DT):
                                    if tile == 0:
                                        norm.wait_tile(pe, k)
                                    last = product(psum[:, tile % 4, :], (high[:, k, sl], low[:, k, sl]),
                                                   (split[:, 0, k, :], split[:, 1, k, :]), k == 0, k == DT - 1)
                                last.then_inc(weights.products, 1)

                    @block.scalar
                    def _(act):
                        norm.scalar(act)

                        def square(tile):
                            act.wait_ge(tile_ready, tile + 1)
                            sums.square(act, tile, tile % 2, x[:, tile:tile + 1, :])

                        for n in range(4):
                            weights.split_high(act, Chunk(start1 + n + 1))
                            for m in range(2):
                                tile = 2 * n + m
                                act.wait_ge(weights.products, tiles0 + DT + tile + 1)
                                if tile >= 4:
                                    act.wait_ge(product_ready, tile - 3)
                                nc.scalar.activation(handed[:, tile % 4, :], psum[:, tile % 4, :], ACT.Tanh,
                                                     scale=0.5).then_inc(bank_free, 1)
                            if n >= 1:
                                square(2 * n - 2)
                                square(2 * n - 1)
                        square(DT - 2)
                        square(DT - 1)

                    @block.vector
                    def _(dve):
                        norm.vector(dve)
                        sums.start(dve)
                        for tile in range(DT):
                            dve.wait_ge(bank_free, tile + 1)
                            nc.vector.scalar_tensor_tensor(out=gated[:, tile % 2, :], in0=handed[:, tile % 4, :], scalar=1.0,
                                                           in1=scratch[:, tile, :], op0=ALU.add,
                                                           op1=ALU.mult).then_inc(product_ready, 1)
                            dve.wait_ge(product_ready, tile + 1)
                            nc.vector.tensor_tensor(out=x[:, tile, :], in0=x[:, tile, :], in1=gated[:, tile % 2, :],
                                                    op=ALU.add).then_inc(tile_ready, 1)
                            if tile >= 2:
                                sums.add(dve, tile - 2, tile % 2)
                        sums.add(dve, DT - 2, 0)
                        sums.add(dve, DT - 1, 1)

        def swiglu(label, norm, split, total):
            start = weights.start[label]
            tiles0 = weights.tiles_before[start]
            blocks = D_FF2 // 256
            with stage(label) as s:
                norm = norm(s)
                sums = SquareSum(s)
                hidden = s.sbuf("hidden", [P, 2, 2, 2, T], f32r)
                tanh = s.sbuf("tanh", [P, 2, T], f32)
                gated = s.sbuf("gated", [P, 2, T], f32)
                inner = s.sbuf("inner", [P, 2, T], f32)
                tanh_ready, gated_ready, inner_ready, high_ready, hidden_ready, added = [s.sem(n) for n in (
                    "tanh_ready", "gated_ready", "inner_ready", "high_ready", "hidden_ready", "added")]

                def first(t):
                    return isinstance(t, int) and t == 0

                def gate_tiles(t):
                    return tiles0 if first(t) else t * 12 + (tiles0 - 8)

                def up_tiles(t):
                    return tiles0 + 2 if first(t) else t * 12 + (tiles0 - 6)

                with nc.Block() as block:
                    @block.sync
                    def _(sp):
                        weights.load_for(sp, label)

                    @block.gpsimd
                    def _(pool):
                        norm.gpsimd(pool)
                        weights.split_low_all(pool, label)

                    @block.tensor
                    def _(pe):
                        norm.tensor(pe)
                        def into_hidden(chunk, t, bank, read):
                            pe.wait_ge(weights.low_ready, chunk.number + 1)
                            high, low = weights.parts(chunk, DT)
                            for m in range(2):
                                if not first(t):
                                    pe.wait_ge(read, t * 2 + (m - 1))
                                sl = slice(m * P, (m + 1) * P)
                                for k in range(DT):
                                    if first(t) and bank == m == 0:
                                        norm.wait_tile(pe, k)
                                    last = product(psum[:, bank + m, :], (high[:, k, sl], low[:, k, sl]),
                                                   (split[:, 0, k, :], split[:, 1, k, :]), k == 0, k == DT - 1)
                                last.then_inc(weights.products, 1)

                        def down(chunk, t, parity):
                            pe.wait_ge(weights.low_ready, chunk.number + 1)
                            high, low = weights.parts(chunk, 2)
                            pe.wait_ge(hidden_ready, t * 2 + 2)
                            for m in range(DT):
                                pe.wait_ge(added, t * DT + (m + 5))
                                sl = slice(m * P, (m + 1) * P)
                                for k in range(2):
                                    last = product(psum[:, 4 + m % 4, :], (high[:, k, sl], low[:, k, sl]),
                                                   (hidden[:, parity, 0, k, :], hidden[:, parity, 1, k, :]),
                                                   k == 0, k == 1)
                                last.then_inc(weights.products, 1)

                        into_hidden(Chunk(start), 0, 0, gated_ready)
                        into_hidden(Chunk(start + 1), 0, 2, inner_ready)
                        with pe.Fori(0, blocks // 2) as i:
                            for b in range(2):
                                t = i * 2 + (b + 1)
                                into_hidden(Chunk(start + 2 + 3 * b, i, 6), t, 0, gated_ready)
                                into_hidden(Chunk(start + 3 + 3 * b, i, 6), t, 2, inner_ready)
                                down(Chunk(start + 4 + 3 * b, i, 6), i * 2 + b if b else i * 2, b)
                        down(Chunk(start + 3 * blocks - 1), blocks - 1, 0)

                    @block.scalar
                    def _(act):
                        norm.scalar(act)
                        def gate(t):
                            for m in range(2):
                                act.wait_ge(weights.products, gate_tiles(t) + (m + 1))
                                if not first(t):
                                    act.wait_ge(gated_ready, t * 2 + (m - 1))
                                nc.scalar.activation(tanh[:, m, :], psum[:, m, :], ACT.Tanh, scale=0.5).then_inc(tanh_ready, 1)

                        def high(t, parity):
                            for m in range(2):
                                act.wait_ge(inner_ready, t * 2 + (m + 1))
                                nc.scalar.copy(hidden[:, parity, 0, m, :], inner[:, m, :]).then_inc(high_ready, 1)

                        weights.split_high(act, Chunk(start + 1))
                        weights.split_high(act, Chunk(start + 2))
                        gate(0)
                        high(0, 0)
                        with act.Fori(0, blocks // 2) as i:
                            for b in range(2):
                                t = i * 2 + (b + 1)
                                weights.split_high(act, Chunk(start + 3 + 3 * b, i, 6))
                                weights.split_high(act, Chunk(start + 4 + 3 * b, i, 6))
                                gate(t)
                                weights.split_high(act, Chunk(start + 5 + 3 * b, i, 6))
                                high(t, (b + 1) % 2)
                        weights.split_high(act, Chunk(start + 3 * blocks))
                        for m in range(DT):
                            act.wait_ge(added, blocks * DT + m + 1)
                            sums.square(act, m, m % 2, total[:, m:m + 1, :])

                    @block.vector
                    def _(dve):
                        norm.vector(dve)
                        def hide(t, parity):
                            for m in range(2):
                                dve.wait_ge(tanh_ready, t * 2 + (m + 1))
                                if not first(t):
                                    dve.wait_ge(inner_ready, t * 2 + (m - 1))
                                nc.vector.scalar_tensor_tensor(out=gated[:, m, :], in0=tanh[:, m, :], scalar=1.0,
                                                               in1=psum[:, m, :], op0=ALU.add,
                                                               op1=ALU.mult).then_inc(gated_ready, 1)
                            for m in range(2):
                                dve.wait_ge(weights.products, up_tiles(t) + (m + 1))
                                dve.wait_ge(gated_ready, t * 2 + (m + 1))
                                if not first(t):
                                    dve.wait_ge(hidden_ready, t * 2 + (m - 1))
                                nc.vector.scalar_tensor_tensor(out=inner[:, m, :], in0=gated[:, m, :], scalar=0.5,
                                                               in1=psum[:, 2 + m, :], op0=ALU.mult,
                                                               op1=ALU.mult).then_inc(inner_ready, 1)
                            for m in range(2):
                                dve.wait_ge(high_ready, t * 2 + (m + 1))
                                nc.vector.tensor_tensor(out=hidden[:, parity, 1, m, :], in0=inner[:, m, :],
                                                        in1=hidden[:, parity, 0, m, :].bitcast(f32),
                                                        op=ALU.subtract).then_inc(hidden_ready, 1)

                        def accumulate(t):
                            last = isinstance(t, int) and t == blocks - 1
                            base = tiles0 + 12 * t + 4 if last else t * 12 + (tiles0 + 8)
                            for m in range(DT):
                                dve.wait_ge(weights.products, base + (m + 1))
                                dve.wait_ge(added, t * DT + (m + 1))
                                nc.vector.tensor_tensor(out=total[:, m, :], in0=psum[:, 4 + m % 4, :], in1=total[:, m, :],
                                                        op=ALU.add).then_inc(added, 1)
                                if last and m >= 1:
                                    sums.add(dve, m - 1, (m - 1) % 2)

                        nc.vector.memset(total[:], 0.0).then_inc(added, DT)
                        hide(0, 0)
                        with dve.Fori(0, blocks // 2) as i:
                            for b in range(2):
                                hide(i * 2 + (b + 1), (b + 1) % 2)
                                accumulate(i * 2 + b if b else i * 2)
                        sums.start(dve)
                        accumulate(blocks - 1)
                        sums.add(dve, DT - 1, (DT - 1) % 2)

        def copy_to(target, scale=None):
            def finish(bank, tile):
                if scale is None:
                    return nc.vector.tensor_copy(target[:, ds(tile, 1), :], psum[:, bank:bank + 1, :])
                return nc.vector.tensor_scalar(target[:, ds(tile, 1), :], psum[:, bank:bank + 1, :], scale, None, ALU.mult)
            return finish

        def gdn_in(norm, split, qkv, z2, conv, ba):
            start = weights.start["gdn_in"]
            tiles0 = weights.tiles_before[start]
            tiles_z = tiles0 + 3 * GH
            tiles_ba = tiles_z + GH
            with stage("gdn_in") as s:
                norm = norm(s)
                mixed = s.sbuf("mixed", [P, 2, T], f32)
                tanh = s.sbuf("tanh", [P, 2, T], f32)
                bank_free, tap_done, convolved, tanh_ready, activated = [s.sem(n) for n in (
                    "bank_free", "tap_done", "convolved", "tanh_ready", "activated")]
                z_tanh, z_ready = s.sem("z_tanh"), s.sem("z_ready")
                with nc.Block() as block:
                    @block.sync
                    def _(sp):
                        weights.load_for(sp, "gdn_in")

                    @block.gpsimd
                    def _(pool):
                        norm.gpsimd(pool)
                        weights.split_low_all(pool, "gdn_in")

                    @block.tensor
                    def _(pe):
                        norm.tensor(pe)
                        def turn(i, first_chunk, free, base):
                            for c in range(2):
                                chunk = Chunk(first_chunk + c, i, 2)
                                pe.wait_ge(weights.low_ready, chunk.number + 1)
                                high, low = weights.parts(chunk, DT)
                                for j in (2 * c, 2 * c + 1):
                                    pe.wait_ge(free, i * 4 + (j + 1))
                                    sl = slice((j % 2) * P, (j % 2 + 1) * P)
                                    for k in range(DT):
                                        if base == j == 0:
                                            norm.wait_tile(pe, k)
                                        last = product(psum[:, base + j, :], (high[:, k, sl], low[:, k, sl]),
                                                       (split[:, 0, k, :], split[:, 1, k, :]), k == 0, k == DT - 1)
                                    last.then_inc(weights.products, 1)

                        with pe.Fori(0, 6) as i:
                            turn(i, start, bank_free, 0)
                        with pe.Fori(0, 2) as i:
                            turn(i, start + 12, z_ready, 4)
                        pe.wait_ge(weights.low_ready, start + 17)
                        parts = weights.parts(Chunk(start + 16), DT)
                        for n, at in enumerate((256 - 2 * GH - 64, 256 - GH - 64)):
                            for k in range(DT):
                                last = product(psum[0:64 + GH, n, :], [y[:, k, at:at + 64 + GH] for y in parts],
                                               (split[:, 0, k, :], split[:, 1, k, :]), k == 0, k == DT - 1)
                            last.then_inc(weights.products, 1)

                    @block.scalar
                    def _(act):
                        norm.scalar(act)
                        act.sem_inc(z_ready, 4)
                        weights.split_high(act, Chunk(start + 1))
                        with act.Fori(0, 6) as i:
                            for j in range(4):
                                act.wait_ge(weights.products, i * 4 + (tiles0 + j + 1))
                                act.wait_ge(activated, i * 4 + (j + 1))
                                nc.scalar.activation(mixed[:, j % 2, :], psum[:, j, :], ACT.Copy,
                                                     scale=conv[:, ds(i * 4 + (j + 3 * 3 * GH), 1)]).then_inc(tap_done, 1)
                                if j % 2:
                                    weights.split_high(act, Chunk(start + j // 2 + 2, i, 2))
                                act.wait_ge(bank_free, i * 4 + (j + 5))
                                nc.scalar.activation(tanh[:, j % 2, :], mixed[:, j % 2, :], ACT.Tanh,
                                                     scale=0.5).then_inc(tanh_ready, 1)
                        act.wait_ge(activated, 3 * GH + 2)
                        with act.Fori(0, 2) as i:
                            for j in range(4):
                                act.wait_ge(weights.products, i * 4 + (tiles_z + j + 1))
                                act.wait_ge(z_ready, i * 4 + (j + 3))
                                nc.scalar.activation(tanh[:, j % 2, :], psum[:, 4 + j, :], ACT.Tanh,
                                                     scale=0.5).then_inc(z_tanh, 1)
                                if j % 2:
                                    weights.split_high(act, Chunk(start + 12 + j // 2 + 2, i, 2))

                    @block.vector
                    def _(dve):
                        dve.sem_inc(bank_free, 4)
                        norm.vector(dve)
                        dve.sem_inc(activated, 2)
                        with dve.Fori(0, 6) as i:
                            for j in range(4):
                                dve.wait_ge(tap_done, i * 4 + (j + 1))
                                for tap in (2, 1, 0):
                                    back = 3 - tap
                                    if tap < 2:
                                        dve.wait_ge(convolved, i * 8 + (2 * j + back - 1))
                                    nc.vector.scalar_tensor_tensor(
                                        out=mixed[:, j % 2, back:T], in0=psum[:, j, 0:T - back],
                                        scalar=conv[:, ds(i * 4 + (j + tap * 3 * GH), 1)],
                                        in1=mixed[:, j % 2, back:T], op0=ALU.mult, op1=ALU.add).then_inc(bank_free if tap == 0 else convolved, 1)
                                dve.wait_ge(tanh_ready, i * 4 + (j + 1))
                                nc.vector.scalar_tensor_tensor(out=qkv[:, ds(i * 4 + j, 1), :], in0=tanh[:, j % 2:j % 2 + 1, :],
                                                               scalar=1.0, in1=mixed[:, j % 2:j % 2 + 1, :], op0=ALU.add,
                                                               op1=ALU.mult).then_inc(activated, 1)
                        with dve.Fori(0, 2) as i:
                            for j in range(4):
                                dve.wait_ge(z_tanh, i * 4 + (j + 1))
                                nc.vector.scalar_tensor_tensor(out=z2[:, ds(i * 4 + j, 1), :], in0=tanh[:, j % 2:j % 2 + 1, :],
                                                               scalar=1.0, in1=psum[:, 4 + j:5 + j, :], op0=ALU.add,
                                                               op1=ALU.mult).then_inc(z_ready, 1)
                        for n in range(2):
                            dve.wait_ge(weights.products, tiles_ba + n + 1)
                            nc.vector.tensor_copy(ba[:, n, :], psum[64:64 + GH, n, :])

        def gdn_rows(qkv, ba, rows, columns):
            with stage("gdn_rows") as s:
                squares = s.sbuf("squares", [P, 2, T], f32)
                work = s.sbuf("work", [GH, 8, T], f32)
                head_col = s.sbuf("head_col", [GH, 3], f32)
                loaded, squared, summed, act_done, dve_done = [s.sem(n) for n in (
                    "loaded", "squared", "summed", "act_done", "dve_done")]
                zeroed = s.sem("zeroed")
                turned, factors_ready, spread, scaled = [s.sem(n) for n in ("turned", "factors_ready", "spread", "scaled")]
                b_raw, a_raw = ba[:, 0, :], ba[:, 1, :]
                y, size, e, sp, q_mean, k_mean, decay, one = [work[:, n, :] for n in range(8)]
                big_g = rows[0:GH, 3, :]

                def by_chunk(row, n):
                    return row[:, n * P:(n + 1) * P]

                with nc.Block() as block:
                    @block.sync
                    def _(sp):
                        sp.dma_start(head_col[:, 0:1], w["gdn_a_log_2"].rearrange("l h -> h l")).then_inc(loaded, 16)
                        sp.dma_start(head_col[:, 1:2], w["gdn_dt_bias_2"].rearrange("l h -> h l")).then_inc(loaded, 16)

                    @block.tensor
                    def _(pe):
                        for n in range(2 * GH):
                            pe.wait_ge(squared, n + 1)
                            nc.tensor.matmul(psum[0:GH, n // GH, :], constant("head_select")[:, n % GH * GH:(n % GH + 1) * GH],
                                             squares[:, n % 2, :], start=(n % GH == 0), stop=(n % GH == GH - 1)
                                             ).then_inc(summed, 1)
                        pe.wait_ge(dve_done, 10)
                        pe.wait_ge(act_done, 5)
                        for m, row in enumerate((big_g, y, decay)):
                            for n in range(TT):
                                at = (n * 3 + m) * GH
                                last = nc.tensor.transpose(psum[:, 2, at:at + GH], by_chunk(row, n), identity[0:GH, 0:GH])
                        last.then_inc(turned, 1)
                        for n in range(2 * GH):
                            pe.wait_ge(factors_ready, n // GH + 1)
                            if n >= 4:
                                pe.wait_ge(scaled, n - 3)
                            nc.tensor.matmul(psum[:, 3 + n % 4, :], identity[:, n % GH:n % GH + 1].broadcast_to([P, P]),
                                             rows[:, n // GH, :], start=True, stop=True).then_inc(spread, 1)

                    @block.scalar
                    def _(act):
                        def square(first, end):
                            for n in range(first, end):
                                if n >= 2:
                                    act.wait_ge(summed, n - 1)
                                nc.scalar.activation(squares[:, n % 2, :], qkv[:, n, :], ACT.Square).then_inc(squared, 1)

                        square(0, 4)
                        act.wait_ge(loaded, 32)
                        nc.scalar.activation(head_col[:, 2:3], head_col[:, 0:1], ACT.Exp).then_inc(act_done, 1)
                        nc.scalar.activation(sp, b_raw, ACT.Exp, scale=-1.0).then_inc(act_done, 1)
                        act.wait_ge(dve_done, 2)
                        nc.scalar.activation(e, size, ACT.Exp, scale=-1.0).then_inc(act_done, 1)
                        square(4, 8)
                        act.wait_ge(dve_done, 3)
                        nc.scalar.activation(e, e, ACT.Ln).then_inc(act_done, 1)
                        square(8, 2 * GH)
                        act.wait_ge(dve_done, 7)
                        nc.scalar.activation(decay, decay, ACT.Exp).then_inc(act_done, 1)
                        act.wait_ge(dve_done, 12)
                        for n, mean in enumerate((q_mean, k_mean)):
                            nc.scalar.activation(mean, mean, ACT.Sqrt).then_inc(act_done, 1)

                    @block.vector
                    def _(dve):
                        dve.wait_ge(loaded, 32)
                        nc.vector.memset(one, 1.0)
                        nc.vector.memset(rows[:], 0.0).then_inc(zeroed, 1)
                        dve.wait_ge(zeroed, 1)
                        nc.vector.tensor_scalar(y, a_raw, head_col[:, 1:2], None, ALU.add).then_inc(dve_done, 1)
                        dve.wait_ge(dve_done, 1)
                        nc.vector.scalar_tensor_tensor(out=size, in0=y, scalar=-1.0, in1=y, op0=ALU.mult,
                                                       op1=ALU.max).then_inc(dve_done, 1)
                        dve.wait_ge(act_done, 3)
                        nc.vector.tensor_scalar(e, e, 1.0, None, ALU.add).then_inc(dve_done, 1)
                        dve.wait_ge(act_done, 4)
                        nc.vector.scalar_tensor_tensor(out=size, in0=y, scalar=0.0, in1=e, op0=ALU.max,
                                                       op1=ALU.add).then_inc(dve_done, 1)
                        dve.wait_ge(dve_done, 4)
                        nc.vector.tensor_scalar(size, size, head_col[:, 2:3], -1.0, ALU.mult, ALU.mult).then_inc(dve_done, 1)
                        dve.wait_ge(dve_done, 5)
                        for n in range(TT):
                            last = nc.vector.tensor_tensor_scan(by_chunk(big_g, n), by_chunk(one, n), by_chunk(size, n), 0.0,
                                                                ALU.mult, ALU.add)
                        last.then_inc(dve_done, 1)
                        dve.wait_ge(dve_done, 6)
                        for n in range(TT):
                            last = nc.vector.tensor_scalar(by_chunk(decay, n), by_chunk(big_g, n), -1.0,
                                                           big_g[:, (n + 1) * P - 1:(n + 1) * P], ALU.mult, ALU.add)
                        last.then_inc(dve_done, 1)
                        dve.wait_ge(act_done, 2)
                        nc.vector.tensor_scalar(sp, sp, 1.0, None, ALU.add).then_inc(dve_done, 1)
                        dve.wait_ge(dve_done, 8)
                        nc.vector.reciprocal(rows[0:GH, 2, :], sp).then_inc(dve_done, 1)
                        dve.wait_ge(dve_done, 9)
                        nc.vector.tensor_scalar(y, rows[0:GH, 2, :], 0.5, None, ALU.mult).then_inc(dve_done, 1)
                        dve.wait_ge(summed, 2 * GH)
                        for n, mean in enumerate((q_mean, k_mean)):
                            nc.vector.tensor_scalar(mean, psum[0:GH, n, :], 0.25, EPS, ALU.mult, ALU.add).then_inc(dve_done, 1)
                        dve.wait_ge(act_done, 7)
                        nc.vector.reciprocal(rows[0:GH, 0, :], q_mean).then_inc(dve_done, 1)
                        nc.vector.reciprocal(rows[0:GH, 1, :], k_mean).then_inc(dve_done, 1)
                        dve.wait_ge(dve_done, 13)
                        nc.vector.tensor_scalar(rows[0:GH, 0, :], rows[0:GH, 0, :], 0.5 * P ** -0.5, None,
                                                ALU.mult).then_inc(factors_ready, 1)
                        dve.wait_ge(dve_done, 14)
                        nc.vector.tensor_scalar(rows[0:GH, 1, :], rows[0:GH, 1, :], 0.5, None, ALU.mult).then_inc(factors_ready, 1)
                        dve.wait_ge(squared, 2 * GH)
                        for n in range(2 * GH):
                            dve.wait_ge(spread, n + 1)
                            nc.vector.tensor_tensor(out=qkv[:, n, :], in0=qkv[:, n, :], in1=psum[:, 3 + n % 4, :],
                                                    op=ALU.mult).then_inc(scaled, 1)
                        dve.wait_ge(turned, 1)
                        nc.vector.tensor_copy(columns[:], psum[:, 2, 0:TT * 3 * GH].rearrange("p (n m h) -> p n m h", n=TT, m=3))

        def gdn_chunks(qkv, rows, columns):
            H = GH
            with stage("gdn_chunks") as s:
                def matrix(name):
                    return s.sbuf(name, [P, H, P], f32)

                (kn, kb, kbg, qg, grow, decay, part0, part1, kd, bv, lt, aq, u_, t_, y_, v_, state) = [matrix(n) for n in (
                    "key", "key_beta", "key_beta_grown", "query_grown", "grown", "decay", "part0", "part1",
                    "key_decayed", "value_beta", "lower_t", "query_key", "inverse_t", "inverse", "product", "value", "state")]
                parts = (part0, part1)
                last_growth = s.sbuf("last_growth", [P, H], f32)
                cols = s.sbuf("cols", [P, 3, H], f32)
                mask = s.sbuf("mask", [P, 8, P], f32)
                names = ["masks_in", "cols_in", "key_staged", "b_spread", "g_spread",
                         "kb_ready", "grown_ready", "diff_ready", "diff_exp", "decay_ready", "v_staged", "qg_ready",
                         "kbg_ready", "k_turned", "kd_ready", "v_turned", "bv_ready", "kk_done", "lt_ready", "qk_done",
                         "aq_ready", "u_ready", "t_ready", "part_ready", "part_turned", "y_done", "y_ready", "zt_done",
                         "z_done", "ks_done", "r_ready", "vn_done", "vn_ready", "o_done", "o_read", "ds_done",
                         "state_ready", "last_ready", "part_first"]
                S = {n: s.sem(n) for n in names}

                def pair(n):
                    return psum[:, 2 * n:2 * n + 2, :].rearrange("p b (h c) -> p (b h) c", h=4)

                A, B, C, E = [pair(n) for n in range(4)]
                half = (slice(0, H // 2), slice(H // 2, H))

                def chunk_of(first_tile, i, heads=slice(0, H)):
                    return qkv[:, first_tile + heads.start:first_tile + heads.stop, ds(i * P, P)]

                def over_heads(m):
                    return m.unsqueeze(1).broadcast_to([P, H, P])

                def over_columns(c):
                    return c.unsqueeze(2).broadcast_to([P, H, P])

                with nc.Block() as block:
                    @block.sync
                    def _(sp):
                        at = CONST_AT["earlier"][0]
                        sp.dma_start(mask[:].rearrange("p n c -> p (n c)"), constants[:, at:at + 8 * P]).then_inc(S["masks_in"], 16)

                    @block.tensor
                    def _(pe):
                        for name in ("ds_done", "o_done"):
                            pe.sem_inc(S[name], 1)
                        with pe.Fori(0, TT) as i:
                            def spread(target, row, done):
                                for h in range(H):
                                    last = nc.tensor.matmul(target[:, h, :], identity[:, h:h + 1].broadcast_to([P, P]),
                                                            rows[:, row, ds(i * P, P)], start=True, stop=True)
                                last.then_inc(S[done], 1)

                            def heads(target, left, right, done, which=slice(0, H)):
                                for h in range(which.start, which.stop):
                                    last = nc.tensor.matmul(target[:, h, :], left[:, h, :], right[:, h, :], start=True, stop=True)
                                last.then_inc(S[done], 1)

                            def turn(target, source, done):
                                for h in range(H):
                                    last = nc.tensor.transpose(target[:, h, :], source[:, h, :], identity)
                                last.then_inc(S[done], 1)

                            pe.wait_ge(S["vn_ready"], i * 2 + 1)
                            spread(E, 3, "g_spread")
                            pe.wait_ge(S["state_ready"], i * 2 + 2)
                            spread(C, 2, "b_spread")
                            pe.wait_ge(S["key_staged"], i + 1)
                            turn(A, kn, "k_turned")
                            pe.wait_ge(S["v_staged"], i + 1)
                            pe.wait_ge(S["o_read"], i * 2 + 1)
                            turn(B, v_, "v_turned")
                            pe.wait_ge(S["kb_ready"], i + 1)
                            heads(C, kn, kb, "kk_done")
                            pe.wait_ge(S["diff_ready"], i + 1)
                            pe.wait_ge(S["grown_ready"], i + 1)
                            heads(E, kn, chunk_of(0, i), "qk_done")
                            pe.wait_ge(S["part_first"], i + 1)
                            pe.wait_ge(S["kd_ready"], i + 1)
                            turn(A, part0, "part_turned")
                            for level in range(1, 7):
                                pe.wait_ge(S["part_ready"], i * 6 + level)
                                for g in range(2):
                                    pe.wait_ge(S["t_ready"], i * 12 + (2 * level - 1 + g))
                                    heads(A, parts[level % 2], t_, "y_done", half[g])
                                for g in range(2):
                                    pe.wait_ge(S["y_ready"], i * 12 + (2 * level - 1 + g))
                                    pe.wait_ge(S["u_ready"], i * 14 + (2 * level - 1 + g))
                                    if level == 1 and g == 0:
                                        pe.wait_ge(S["bv_ready"], i + 1)
                                    heads(B, y_, u_, "zt_done", half[g])
                                    if level < 6:
                                        heads(C, u_, y_, "z_done", half[g])
                                if level == 3:
                                    pe.wait_ge(S["aq_ready"], i + 1)
                                    pe.wait_ge(S["kbg_ready"], i + 1)
                                    heads(E, kbg, state, "ks_done")
                            pe.wait_ge(S["r_ready"], i + 1)
                            for g in range(2):
                                pe.wait_ge(S["u_ready"], i * 14 + (13 + g))
                                heads(A, u_, kb, "vn_done", half[g])
                            pe.wait_ge(S["qg_ready"], i + 1)
                            for g in range(2):
                                for h in range(half[g].start, half[g].stop):
                                    nc.tensor.matmul(B[:, h, :], state[:, h, :], qg[:, h, :], start=True, stop=False)
                                    if h == half[g].start:
                                        pe.wait_ge(S["vn_ready"], i * 2 + (2 + g))
                                    last = nc.tensor.matmul(B[:, h, :], grow[:, h, :], aq[:, h, :], start=False, stop=True)
                                last.then_inc(S["o_done"], 1)
                                heads(C, kd, grow, "ds_done", half[g])

                    @block.vector
                    def _(dve):
                        def tt(out_, in0, in1, op, done, count=1):
                            nc.vector.tensor_tensor(out=out_, in0=in0, in1=in1, op=op).then_inc(S[done], count)

                        nc.vector.memset(state[:], 0.0).then_inc(S["state_ready"], 2)
                        dve.wait_ge(S["masks_in"], 16)
                        with dve.Fori(0, TT) as i:
                            nc.vector.tensor_copy(cols[:].unsqueeze(1), columns[:, ds(i, 1), :, :]).then_inc(S["cols_in"], 1)
                            dve.wait_ge(S["g_spread"], i + 1)
                            dve.wait_ge(S["cols_in"], i + 1)
                            for h in range(H):
                                last = nc.vector.tensor_scalar(decay[:, h, :], E[:, h, :], cols[:, 0, h:h + 1], 0.0,
                                                               ALU.subtract, ALU.min)
                            last.then_inc(S["diff_ready"], 1)
                            dve.wait_ge(S["b_spread"], i + 1)
                            dve.wait_ge(S["key_staged"], i + 1)
                            tt(kb[:], kn[:], C, ALU.mult, "kb_ready")
                            dve.wait_ge(S["kk_done"], i + 1)
                            dve.wait_ge(S["diff_exp"], i + 1)
                            tt(lt[:], decay[:], C, ALU.mult, "lt_ready")
                            dve.wait_ge(S["lt_ready"], i + 1)
                            tt(part0[:], lt[:], over_heads(mask[:, 1, :]), ALU.mult, "part_first")
                            dve.wait_ge(S["k_turned"], i + 1)
                            tt(kd[:], A, over_columns(cols[:, 2, :]), ALU.mult, "kd_ready")
                            dve.wait_ge(S["part_first"], i + 1)
                            tt(u_[:], over_heads(identity), part0[:], ALU.subtract, "u_ready", 2)
                            dve.wait_ge(S["part_turned"], i + 1)
                            tt(t_[:], over_heads(identity), A, ALU.subtract, "t_ready", 2)
                            dve.wait_ge(S["v_turned"], i + 1)
                            tt(bv[:], B, over_columns(cols[:, 1, :]), ALU.mult, "bv_ready")
                            dve.wait_ge(S["qk_done"], i + 1)
                            dve.wait_ge(S["decay_ready"], i + 1)
                            for level in range(1, 7):
                                for g in range(2):
                                    at = half[g]
                                    dve.wait_ge(S["zt_done"], i * 12 + (2 * level - 1 + g))
                                    dve.wait_ge(S["u_ready"], i * 14 + (2 * level - 1 + g))
                                    if level < 6:
                                        dve.wait_ge(S["z_done"], i * 10 + (2 * level - 1 + g))
                                        dve.wait_ge(S["t_ready"], i * 12 + (2 * level - 1 + g))
                                        tt(t_[:, at, :], t_[:, at, :], C[:, at, :], ALU.subtract, "t_ready")
                                    tt(u_[:, at, :], u_[:, at, :], B[:, at, :], ALU.subtract, "u_ready")
                                if level == 1:
                                    tt(aq[:], decay[:], E, ALU.mult, "aq_ready")
                                    dve.wait_ge(S["grown_ready"], i + 1)
                                    nc.vector.tensor_copy(last_growth[:].unsqueeze(2), grow[:, :, P - 1:P]
                                                          ).then_inc(S["last_ready"], 1)
                                if level == 4:
                                    dve.wait_ge(S["ks_done"], i + 1)
                                    dve.wait_ge(S["bv_ready"], i + 1)
                                    dve.wait_ge(S["kbg_ready"], i + 1)
                                    tt(kb[:], bv[:], E, ALU.subtract, "r_ready")
                            dve.wait_ge(S["last_ready"], i + 1)
                            for g in range(2):
                                dve.wait_ge(S["ds_done"], i * 2 + (2 + g))
                                for h in range(half[g].start, half[g].stop):
                                    last = nc.vector.scalar_tensor_tensor(out=state[:, h, :], in0=state[:, h, :],
                                                                          scalar=last_growth[:, h:h + 1], in1=C[:, h, :],
                                                                          op0=ALU.mult, op1=ALU.add)
                                last.then_inc(S["state_ready"], 1)

                    @block.scalar
                    def _(act):
                        for name in ("vn_ready", "o_read"):
                            act.sem_inc(S[name], 1)
                        with act.Fori(0, TT) as i:
                            act.wait_ge(S["diff_ready"], i + 1)
                            nc.scalar.activation(decay[:], decay[:], ACT.Exp).then_inc(S["diff_exp"], 1)
                            act.wait_ge(S["ds_done"], i * 2 + 1)
                            nc.scalar.activation(grow[:], E, ACT.Exp).then_inc(S["grown_ready"], 1)
                            for level in range(1, 7):
                                for g in range(2):
                                    act.wait_ge(S["y_done"], i * 12 + (2 * level - 1 + g))
                                    nc.scalar.copy(y_[:, half[g], :], A[:, half[g], :]).then_inc(S["y_ready"], 1)
                            act.wait_ge(S["kbg_ready"], i + 1)
                            act.wait_ge(S["last_ready"], i + 1)
                            for g in range(2):
                                act.wait_ge(S["vn_done"], i * 2 + (1 + g))
                                nc.scalar.copy(grow[:, half[g], :], A[:, half[g], :]).then_inc(S["vn_ready"], 1)
                            for g in range(2):
                                act.wait_ge(S["o_done"], i * 2 + (2 + g))
                                nc.scalar.copy(chunk_of(0, i, half[g]), B[:, half[g], :]).then_inc(S["o_read"], 1)

                    @block.gpsimd
                    def _(pool):
                        pool.wait_ge(S["masks_in"], 16)
                        nc.gpsimd.tensor_copy(kn[:], chunk_of(H, 0)).then_inc(S["key_staged"], 1)
                        nc.gpsimd.tensor_copy(v_[:], chunk_of(2 * H, 0)).then_inc(S["v_staged"], 1)

                        def chunk(i, last):
                            pool.wait_ge(S["lt_ready"], i + 1)
                            for level in range(1, 7):
                                if level == 2:
                                    pool.wait_ge(S["part_turned"], i + 1)
                                    pool.wait_ge(S["u_ready"], i * 14 + 2)
                                if level >= 3:
                                    pool.wait_ge(S["y_done"], i * 12 + 2 * (level - 2))
                                nc.gpsimd.tensor_tensor(out=parts[level % 2][:], in0=lt[:], in1=over_heads(mask[:, 1 + level, :]),
                                                        op=ALU.mult).then_inc(S["part_ready"], 1)
                                if level == 1:
                                    nc.gpsimd.tensor_tensor(out=decay[:], in0=decay[:], in1=over_heads(mask[:, 0, :]),
                                                            op=ALU.mult).then_inc(S["decay_ready"], 1)
                                if level == 2:
                                    pool.wait_ge(S["grown_ready"], i + 1)
                                    pool.wait_ge(S["kb_ready"], i + 1)
                                    nc.gpsimd.tensor_tensor(out=kbg[:], in0=kb[:], in1=grow[:], op=ALU.mult).then_inc(S["kbg_ready"], 1)
                                    nc.gpsimd.tensor_tensor(out=qg[:], in0=chunk_of(0, i), in1=grow[:], op=ALU.mult
                                                            ).then_inc(S["qg_ready"], 1)
                                if level == 5 and not last:
                                    pool.wait_ge(S["qk_done"], i + 1)
                                    nc.gpsimd.tensor_copy(kn[:], chunk_of(H, i + 1)).then_inc(S["key_staged"], 1)
                                    nc.gpsimd.tensor_copy(v_[:], chunk_of(2 * H, i + 1)).then_inc(S["v_staged"], 1)

                        with pool.Fori(0, TT - 1) as i:
                            chunk(i, False)
                        chunk(TT - 1, True)

        def gdn_post(qkv, z2, split):
            with stage("gdn_post") as s:
                squares = s.sbuf("squares", [P, 2, T], f32)
                row = s.sbuf("row", [GH, T], f32)
                factor = s.sbuf("factor", [P, T], f32)
                normed = s.sbuf("normed", [P, 2, T], f32)
                gated = s.sbuf("gated", [P, 2, T], f32)
                squared, summed, mean, root, ready, spread, normed_ready, gated_ready, high_ready, low_done = [s.sem(n) for n in (
                    "squared", "summed", "mean", "root", "ready", "spread", "normed_ready", "gated_ready", "high_ready", "low_done")]
                zeroed = s.sem("zeroed")
                with nc.Block() as block:
                    @block.scalar
                    def _(act):
                        for h in range(GH):
                            if h >= 2:
                                act.wait_ge(summed, h - 1)
                            nc.scalar.activation(squares[:, h % 2, :], qkv[:, h, :], ACT.Square).then_inc(squared, 1)
                        act.wait_ge(mean, 1)
                        nc.scalar.activation(row[:], row[:], ACT.Sqrt).then_inc(root, 1)
                        for h in range(GH):
                            act.wait_ge(gated_ready, h + 1)
                            nc.scalar.copy(split[:, 0, h, :], gated[:, h % 2, :]).then_inc(high_ready, 1)

                    @block.tensor
                    def _(pe):
                        for h in range(GH):
                            pe.wait_ge(squared, h + 1)
                            nc.tensor.matmul(psum[0:GH, 0, :], constant("head_select")[:, h * GH:(h + 1) * GH],
                                             squares[:, h % 2, :], start=(h == 0), stop=(h == GH - 1)).then_inc(summed, 1)
                        pe.wait_ge(ready, 1)
                        for h in range(GH):
                            if h >= 2:
                                pe.wait_ge(normed_ready, h - 1)
                            nc.tensor.matmul(psum[:, 1 + h % 2, :], identity[:, h:h + 1].broadcast_to([P, P]), factor[:],
                                             start=True, stop=True).then_inc(spread, 1)

                    @block.vector
                    def _(dve):
                        nc.vector.memset(factor[:], 0.0).then_inc(zeroed, 1)
                        dve.wait_ge(zeroed, 1)
                        dve.wait_ge(summed, GH)
                        nc.vector.tensor_scalar(row[:], psum[0:GH, 0, :], 1.0 / P, EPS, ALU.mult, ALU.add).then_inc(mean, 1)
                        dve.wait_ge(root, 1)
                        nc.vector.reciprocal(factor[0:GH, :], row[:]).then_inc(ready, 1)
                        for h in range(GH):
                            dve.wait_ge(spread, h + 1)
                            if h >= 2:
                                dve.wait_ge(gated_ready, h - 1)
                            nc.vector.scalar_tensor_tensor(out=normed[:, h % 2, :], in0=qkv[:, h, :], scalar=gain("gdn_out_norm_2"),
                                                           in1=psum[:, 1 + h % 2, :], op0=ALU.mult, op1=ALU.mult
                                                           ).then_inc(normed_ready, 1)
                            dve.wait_ge(normed_ready, h + 1)
                            if h >= 2:
                                dve.wait_ge(low_done, h - 1)
                            nc.vector.scalar_tensor_tensor(out=gated[:, h % 2, :], in0=normed[:, h % 2, :], scalar=0.5,
                                                           in1=z2[:, h, :], op0=ALU.mult, op1=ALU.mult).then_inc(gated_ready, 1)

                    @block.gpsimd
                    def _(pool):
                        for h in range(GH):
                            pool.wait_ge(high_ready, h + 1)
                            nc.gpsimd.tensor_tensor(out=split[:, 1, h, :], in0=gated[:, h % 2, :],
                                                    in1=split[:, 0, h, :].bitcast(f32), op=ALU.subtract).then_inc(low_done, 1)

        def fox_kv(norm, split, keys, values, f_raw):
            start = weights.start["fox_kv"]
            tiles0 = weights.tiles_before[start]
            with stage("fox_kv") as s:
                norm = norm(s)
                key_bank_free, value_bank_free = s.sem("key_bank_free"), s.sem("value_bank_free")
                with nc.Block() as block:
                    @block.sync
                    def _(sp):
                        weights.load_for(sp, "fox_kv")

                    @block.gpsimd
                    def _(pool):
                        norm.gpsimd(pool)
                        weights.split_low_all(pool, "fox_kv")

                    @block.scalar
                    def _(act):
                        norm.scalar(act)
                        for first in (0, 4):
                            with act.Fori(0, 2) as i:
                                for c in range(2):
                                    weights.split_high(act, Chunk(start + first + c + 1, i, 2))
                        weights.split_high(act, Chunk(start + 9))

                    @block.tensor
                    def _(pe):
                        norm.tensor(pe)
                        with pe.Fori(0, 2) as i:
                            for c in range(2):
                                chunk = Chunk(start + c, i, 2)
                                pe.wait_ge(weights.low_ready, chunk.number + 1)
                                high, low = weights.parts(chunk, DT)
                                for j in (2 * c, 2 * c + 1):
                                    pe.wait_ge(key_bank_free, i * 4 + (j + 1))
                                    sl = slice((j % 2) * P, (j % 2 + 1) * P)
                                    for k in range(DT):
                                        if j == 0:
                                            norm.wait_tile(pe, k)
                                        last = product(psum[:, j, :], (high[:, k, sl], low[:, k, sl]),
                                                       (split[:, 0, k, :], split[:, 1, k, :]), k == 0, k == DT - 1)
                                    last.then_inc(weights.products, 1)
                        with pe.Fori(0, 2) as i:
                            for half in range(2):
                                chunk = Chunk(start + 4 + half, i, 2)
                                pe.wait_ge(weights.low_ready, chunk.number + 1)
                                parts = weights.parts(chunk, 4)
                                for j in range(TT):
                                    if half == 0:
                                        pe.wait_ge(value_bank_free, i * 4 + (j + 1))
                                    for k in range(4):
                                        a = 4 * half + k
                                        token = [split[:, n, a, j * P:(j + 1) * P] for n in range(2)]
                                        last = product(psum[:, 4 + j, :], token, [y[:, k, :] for y in parts], a == 0, a == DT - 1)
                                    last.then_inc(weights.products, 1)
                        pe.wait_ge(weights.low_ready, start + 9)
                        parts = weights.parts(Chunk(start + 8), DT)
                        at = 256 - FOX_HEADS - 64
                        for k in range(DT):
                            last = product(psum[0:64 + FOX_HEADS, 0, :], [y[:, k, at:at + 64 + FOX_HEADS] for y in parts],
                                           (split[:, 0, k, :], split[:, 1, k, :]), k == 0, k == DT - 1)
                        last.then_inc(weights.products, 1)

                    @block.vector
                    def _(dve):
                        dve.sem_inc(key_bank_free, 4)
                        dve.sem_inc(value_bank_free, 4)
                        norm.vector(dve)
                        with dve.Fori(0, 2) as i:
                            for j in range(4):
                                dve.wait_ge(weights.products, i * 4 + (tiles0 + j + 1))
                                nc.vector.tensor_copy(keys[:, ds(i * 4 + j, 1), :], psum[:, j:j + 1, :]).then_inc(key_bank_free, 1)
                        with dve.Fori(0, 2) as i:
                            for j in range(TT):
                                dve.wait_ge(weights.products, i * 8 + (tiles0 + 8 + 4 + j + 1))
                                nc.vector.tensor_copy(values[:, j, ds(i * T, T)], psum[:, 4 + j, :]).then_inc(value_bank_free, 1)
                        dve.wait_ge(weights.products, tiles0 + 8 + 16 + 1)
                        nc.vector.tensor_copy(f_raw[:], psum[64:64 + FOX_HEADS, 0, :])

        def fox_rows(f_raw, c_rows, c_cols):
            with stage("fox_rows") as s:
                bias = s.sbuf("bias", [FOX_HEADS, 1], f32)
                work = s.sbuf("work", [FOX_HEADS, 4, T], f32)
                y, size, e, one = [work[:, n, :] for n in range(4)]
                loaded, step, exp_ready, ln_ready, turned = [s.sem(n) for n in ("loaded", "step", "exp_ready", "ln_ready", "turned")]
                with nc.Block() as block:
                    @block.sync
                    def _(sp):
                        sp.dma_start(bias[:], w["b_forget_2"].rearrange("(h a) -> h a", a=1)).then_inc(loaded, 16)

                    @block.scalar
                    def _(act):
                        act.wait_ge(step, 2)
                        nc.scalar.activation(e, size, ACT.Exp, scale=-1.0).then_inc(exp_ready, 1)
                        act.wait_ge(step, 3)
                        nc.scalar.activation(e, e, ACT.Ln).then_inc(ln_ready, 1)

                    @block.tensor
                    def _(pe):
                        pe.wait_ge(step, 5)
                        for n in range(TT):
                            last = nc.tensor.transpose(psum[:, 0, n * FOX_HEADS:(n + 1) * FOX_HEADS], c_rows[:, n * P:(n + 1) * P],
                                                       identity[0:FOX_HEADS, 0:FOX_HEADS])
                        last.then_inc(turned, 1)

                    @block.vector
                    def _(dve):
                        nc.vector.memset(one, 1.0)
                        dve.wait_ge(loaded, 16)
                        nc.vector.tensor_scalar(y, f_raw[:], bias[:], None, ALU.add).then_inc(step, 1)
                        dve.wait_ge(step, 1)
                        nc.vector.scalar_tensor_tensor(out=size, in0=y, scalar=-1.0, in1=y, op0=ALU.mult, op1=ALU.max).then_inc(step, 1)
                        dve.wait_ge(exp_ready, 1)
                        nc.vector.tensor_scalar(e, e, 1.0, None, ALU.add).then_inc(step, 1)
                        dve.wait_ge(ln_ready, 1)
                        nc.vector.scalar_tensor_tensor(out=y, in0=y, scalar=0.0, in1=e, op0=ALU.min, op1=ALU.subtract).then_inc(step, 1)
                        dve.wait_ge(step, 4)
                        nc.vector.tensor_tensor_scan(c_rows[:], one, y, 0.0, ALU.mult, ALU.add).then_inc(step, 1)
                        dve.wait_ge(turned, 1)
                        nc.vector.tensor_copy(c_cols[:], psum[:, 0, 0:TT * FOX_HEADS].rearrange("p (n h) -> p n h", n=TT))


        def block_two():
            with ExitStack() as gdn:
                def keep(name, shape, dtype=f32):
                    return gdn.enter_context(nc.sbuf_tensor(name, shape, dtype))

                qkv = keep("gdn_qkv", [P, 3 * GH, T])
                z2 = keep("gdn_z2", [P, GH, T])
                rows = keep("gdn_rows_kept", [P, 4, T])
                columns = keep("gdn_columns", [P, TT, 3, GH])
                with ExitStack() as early:
                    ba = early.enter_context(nc.sbuf_tensor("gdn_ba", [GH, 2, T], f32))
                    with nc.sbuf_tensor("gdn_split", [P, 2, DT, T], f32r) as split:
                        gdn_in(norm_of(x, DT, lambda t: gain("pre_mix_norm_2", t), split=split, given=True), split, qkv, z2, conv, ba)
                    gdn_rows(qkv, ba, rows, columns)
                gdn_chunks(qkv, rows, columns)
                with nc.sbuf_tensor("gdn_out_split", [P, 2, DT, T], f32r) as split, \
                        nc.sbuf_tensor("gdn_mix", [P, DT, T], f32) as mix:
                    gdn_post(qkv, z2, split)
                    linear("gdn_out", 2, split, copy_to(mix), result=mix)
                    rms_normalize("norm_gdn_out", mix, DT, lambda t: gain("post_mix_norm_2", t), add_to=x, given=True, sum_next=True)

            def feed_forward(layer):
                with nc.sbuf_tensor(f"ffn_split{layer}", [P, 2, DT, T], f32r) as split, \
                        nc.sbuf_tensor(f"ffn_total{layer}", [P, DT, T], f32) as total:
                    swiglu(f"ffn{layer}", norm_of(x, DT, lambda t: gain("pre_ffn_norm_2", layer * DT + t), split=split,
                                                  given=True), split, total)
                    rms_normalize(f"norm_ffn_out{layer}", total, DT, lambda t: gain("post_ffn_norm_2", layer * DT + t), add_to=x, given=True,
                                  sum_next=(layer == 0))

            feed_forward(0)
            with ExitStack() as fox:
                def keep_fox(name, shape, dtype=f32):
                    return fox.enter_context(nc.sbuf_tensor(name, shape, dtype))

                split = keep_fox("fox_split", [P, 2, DT, T], f32r)
                keys = keep_fox("fox_keys", [P, DT, T])
                queries = keep_fox("fox_queries", [P, DT, T])
                values = keep_fox("fox_values", [P, TT, D])
                c_rows = keep_fox("fox_c_rows", [FOX_HEADS, T])
                c_cols = keep_fox("fox_c_cols", [P, TT, FOX_HEADS])
                with nc.sbuf_tensor("fox_f_raw", [FOX_HEADS, T], f32) as f_raw:
                    fox_kv(norm_of(x, DT, lambda t: gain("kv_norm_2", t), split=split, given=True), split, keys, values, f_raw)
                    fox_rows(f_raw, c_rows, c_cols)
                linear("fox_q", 2, split, norm=norm_of(x, DT, lambda t: gain("pre_mix_norm_2", DT + t), split=split, given=True),
                        finish=copy_to(queries, FOX_HD ** -0.5))
                attention("fox", FOX_HEADS // 2, split, 0, queries, keys, values, FOX_HD, FOX_HD, "forget",
                          decay=(c_rows, c_cols))
                linear("fox_out", 2, split, copy_to(queries), result=queries)
                rms_normalize("norm_fox_out", queries, DT, lambda t: gain("post_mix_norm_2", DT + t), add_to=x, given=True, sum_next=True)
            feed_forward(1)

        def write_out():
            with stage("write") as s:
                rows_out = s.sbuf("rows", [P, TT, D], f32)
                turned, copied, stored = s.sem("turned"), s.sem("copied"), s.sem("stored")
                with nc.Block() as block:
                    @block.tensor
                    def _(pe):
                        for n in range(2 * TT):
                            j, half = divmod(n, 2)
                            if n >= 4:
                                pe.wait_ge(copied, n - 3)
                            for t in range(4):
                                last = nc.tensor.transpose(psum[:, n % 4, t * P:(t + 1) * P],
                                                           x[:, half * 4 + t, j * P:(j + 1) * P], identity)
                            last.then_inc(turned, 1)

                    @block.vector
                    def _(dve):
                        for n in range(2 * TT):
                            j, half = divmod(n, 2)
                            dve.wait_ge(turned, n + 1)
                            nc.vector.tensor_copy(rows_out[:, j, half * T:(half + 1) * T], psum[:, n % 4, :]).then_inc(copied, 1)

                    @block.sync
                    def _(sp):
                        for j in range(TT):
                            sp.wait_ge(copied, 2 * j + 2)
                            sp.dma_start(out[0, j * P:(j + 1) * P, :], rows_out[:, j, :]).then_inc(stored, 16)
                        sp.wait_ge(stored, 16 * TT)

        with ExitStack() as first:
            block_one(first)
        block_two()
        write_out()


_OUT_SHAPE = (1, T, D)


def kernel(**inputs):
    import concourse.bacc as bacc
    from concourse import mybir
    from concourse.bass_utils import run_bass_kernel_spmd

    nc = bacc.Bacc("TRN2", target_bir_lowering=False, num_devices=1, dynamic_dma_scratch_size=1024)
    arrays, handles = {}, {}
    for name, value in inputs.items():
        a = np.ascontiguousarray(value)
        arrays[f"in_{name}"] = a
        handles[name] = nc.dram_tensor(f"in_{name}", a.shape, mybir.dt.from_np(a.dtype), kind="ExternalInput").ap()
    arrays["shape_constants"] = shape_constants()
    arrays["rope_tables"] = rope_tables()
    constants = nc.dram_tensor("shape_constants", (P, N_CONST), mybir.dt.float32, kind="ExternalInput").ap()
    tables = nc.dram_tensor("rope_tables", (4, P, T), mybir.dt.float32, kind="ExternalInput").ap()
    out = nc.dram_tensor("out", _OUT_SHAPE, mybir.dt.float32, kind="ExternalOutput").ap()
    build_program(nc, handles, constants, tables, out)
    result = run_bass_kernel_spmd(nc, [arrays], core_ids=[0])
    return result.results[0]["out"]
```
